# Optimizing a Trainium2 kernel written in Bass

```python
import jax, jax.numpy as jnp
from jax import lax
import numpy as np

D_MODEL = 2048
BATCH = 1
SEQ = 256
DEPTH = 2

EPS = 1e-6
MLA_HEADS = 8
MLA_Q_RANK = 512
MLA_KV_RANK = 256
MLA_NOPE = 128
MLA_ROPE = 64
MLA_V = 128
MLA_OUT = MLA_HEADS * MLA_V
ROPE_BASE = 10000.0
Q_BLOCK = 128
SSD_HEADS = 8
SSD_HEAD_DIM = 64
SSD_GROUPS = 2
SSD_STATE = 128
SSD_CONV = 4
SSD_CHUNK = 128
SSD_INNER = SSD_HEADS * SSD_HEAD_DIM
SSD_CONV_DIM = SSD_INNER + 2 * SSD_GROUPS * SSD_STATE
GLA_HEADS = 4
GLA_HEAD_K = 64
GLA_HEAD_V = 128
GLA_GATE_RANK = 16
GLA_GATE_TAU = 16.0
GLA_CHUNK = 64
GLA_KD = GLA_HEADS * GLA_HEAD_K
GLA_VD = GLA_HEADS * GLA_HEAD_V
D_FF = 5632
FFN_CONV = 3
D_MIX = MLA_OUT + SSD_INNER + GLA_VD
IN_SIZES = (MLA_Q_RANK, MLA_KV_RANK, MLA_ROPE,
            SSD_INNER, SSD_CONV_DIM, SSD_HEADS,
            GLA_KD, GLA_KD, GLA_VD, GLA_GATE_RANK, GLA_VD)
D_IN = MLA_Q_RANK + MLA_KV_RANK + MLA_ROPE + SSD_INNER + SSD_CONV_DIM + SSD_HEADS + 2 * GLA_KD + 2 * GLA_VD + GLA_GATE_RANK

kernel_name = "hybrid_mla_ssd_gla_convffn"

def rms_norm(x, g):
    xf = x.astype(jnp.float32)
    var = jnp.mean(xf * xf, axis=-1, keepdims=True)
    return (xf * lax.rsqrt(var + EPS)).astype(x.dtype) * g

def rope_tables(seq, dim, dtype):
    inv_freq = ROPE_BASE ** (-jnp.arange(0, dim, 2, dtype=jnp.float32) / dim)
    ang = jnp.arange(seq, dtype=jnp.float32)[:, None] * inv_freq[None, :]
    return jnp.cos(ang).astype(dtype), jnp.sin(ang).astype(dtype)

def apply_rope(x, cos, sin):
    half = x.shape[-1] // 2
    x1, x2 = x[..., :half], x[..., half:]
    return jnp.concatenate([x1 * cos - x2 * sin, x1 * sin + x2 * cos], axis=-1)

def causal_dwconv(x, w, b):
    k, c = w.shape
    out = lax.conv_general_dilated(
        x, w[:, None, :].astype(x.dtype), window_strides=(1,), padding=[(k - 1, 0)],
        dimension_numbers=("NWC", "WIO", "NWC"), feature_group_count=c)
    return out + b

def mla_mixer(cq_raw, ckv_raw, kpe_raw, q_norm, w_uq, kv_norm, w_ukv, cos, sin):
    b, s, _ = cq_raw.shape
    q = (rms_norm(cq_raw, q_norm) @ w_uq).reshape(b, s, MLA_HEADS, MLA_NOPE + MLA_ROPE)
    q_nope = q[..., :MLA_NOPE]
    q_pe = apply_rope(q[..., MLA_NOPE:], cos[:, None, :], sin[:, None, :])
    kv = (rms_norm(ckv_raw, kv_norm) @ w_ukv).reshape(b, s, MLA_HEADS, MLA_NOPE + MLA_V)
    k_nope, v = kv[..., :MLA_NOPE], kv[..., MLA_NOPE:]
    k_pe = apply_rope(kpe_raw, cos, sin)
    scale = (MLA_NOPE + MLA_ROPE) ** -0.5
    nb = s // Q_BLOCK
    qn_blocks = q_nope.reshape(b, nb, Q_BLOCK, MLA_HEADS, MLA_NOPE).transpose(1, 0, 2, 3, 4)
    qp_blocks = q_pe.reshape(b, nb, Q_BLOCK, MLA_HEADS, MLA_ROPE).transpose(1, 0, 2, 3, 4)
    k_pos = jnp.arange(s)

    def attend(args):
        qn, qp, blk = args
        scores = (jnp.einsum("bqhd,bkhd->bhqk", qn, k_nope)
                  + jnp.einsum("bqhr,bkr->bhqk", qp, k_pe)).astype(jnp.float32) * scale
        q_pos = blk * Q_BLOCK + jnp.arange(Q_BLOCK)
        scores = jnp.where(k_pos[None, :] <= q_pos[:, None], scores, -jnp.inf)
        p = jax.nn.softmax(scores, axis=-1).astype(v.dtype)
        return jnp.einsum("bhqk,bkhd->bqhd", p, v)

    out = lax.map(attend, (qn_blocks, qp_blocks, jnp.arange(nb)))
    return out.transpose(1, 0, 2, 3, 4).reshape(b, s, MLA_OUT)

def ssd_mixer(z, xbc, dt_raw, conv_w, conv_b, dt_bias, a_log, d_skip, norm_g):
    b, s, _ = z.shape
    H, P, N, L = SSD_HEADS, SSD_HEAD_DIM, SSD_STATE, SSD_CHUNK
    xbc = jax.nn.silu(causal_dwconv(xbc, conv_w, conv_b))
    xs, bm, cm = jnp.split(xbc, [SSD_INNER, SSD_INNER + SSD_GROUPS * SSD_STATE], axis=-1)
    xs = xs.reshape(b, s, H, P)
    rep = H // SSD_GROUPS
    bm = jnp.repeat(bm.reshape(b, s, SSD_GROUPS, N), rep, axis=2)
    cm = jnp.repeat(cm.reshape(b, s, SSD_GROUPS, N), rep, axis=2)
    dt = jax.nn.softplus((dt_raw + dt_bias).astype(jnp.float32))
    a_dt = dt * (-jnp.exp(a_log.astype(jnp.float32)))
    x_dt = xs * dt[..., None].astype(xs.dtype)
    nc = s // L
    xc = x_dt.reshape(b, nc, L, H, P)
    bc = bm.reshape(b, nc, L, H, N)
    cc = cm.reshape(b, nc, L, H, N)
    a_cum = jnp.cumsum(a_dt.reshape(b, nc, L, H).transpose(0, 3, 1, 2), axis=-1)
    seg = a_cum[..., :, None] - a_cum[..., None, :]
    causal = jnp.tril(jnp.ones((L, L), dtype=bool))
    decay = jnp.exp(jnp.where(causal, seg, -jnp.inf)).astype(cc.dtype)
    scores = jnp.einsum("bclhn,bcshn->bhcls", cc, bc) * decay
    y_diag = jnp.einsum("bhcls,bcshp->bclhp", scores, xc)
    decay_states = jnp.exp(a_cum[..., -1:] - a_cum).astype(bc.dtype)
    states = jnp.einsum("bclhn,bhcl,bclhp->bchpn", bc, decay_states, xc)
    chunk_decay = jnp.exp(a_cum[..., -1]).astype(states.dtype)

    def step(h, inp):
        st, dec = inp
        return dec[..., None, None] * h + st, h

    h0 = jnp.zeros((b, H, P, N), states.dtype)
    _, prev = lax.scan(step, h0, (states.transpose(1, 0, 2, 3, 4), chunk_decay.transpose(2, 0, 1)))
    prev = prev.transpose(1, 0, 2, 3, 4)
    y_off = jnp.einsum("bclhn,bchpn,bhcl->bclhp", cc, prev, jnp.exp(a_cum).astype(cc.dtype))
    y = (y_diag + y_off).reshape(b, s, H, P) + xs * d_skip[:, None]
    y = y.reshape(b, s, SSD_INNER)
    return rms_norm(y * jax.nn.silu(z), norm_g)

def gla_mixer(q, k, v, gate_low, r, w_gk, b_gk, norm_g):
    b, s, _ = q.shape
    H, K, V, L = GLA_HEADS, GLA_HEAD_K, GLA_HEAD_V, GLA_CHUNK
    nc = s // L
    log_a = jax.nn.log_sigmoid((gate_low @ w_gk + b_gk).astype(jnp.float32)) / GLA_GATE_TAU
    g = jnp.cumsum(log_a.reshape(b, nc, L, H, K), axis=2)
    qc = (q * K ** -0.5).reshape(b, nc, L, H, K).transpose(1, 0, 2, 3, 4)
    kc = k.reshape(b, nc, L, H, K).transpose(1, 0, 2, 3, 4)
    vc = v.reshape(b, nc, L, H, V).transpose(1, 0, 2, 3, 4)
    gc = g.transpose(1, 0, 2, 3, 4)
    causal = jnp.tril(jnp.ones((L, L), dtype=bool))[:, :, None, None]

    def chunk_step(state, inp):
        qb, kb, vb, gb = inp
        rel = gb[:, :, None] - gb[:, None, :]
        rel = jnp.exp(jnp.where(causal, rel, -jnp.inf)).astype(qb.dtype)
        attn = jnp.einsum("blhd,bshd,blshd->bhls", qb, kb, rel)
        o_intra = jnp.einsum("bhls,bshv->blhv", attn, vb)
        o_inter = jnp.einsum("blhd,bhdv->blhv", qb * jnp.exp(gb).astype(qb.dtype), state)
        g_last = gb[:, -1]
        k_dec = kb * jnp.exp(g_last[:, None] - gb).astype(kb.dtype)
        new_state = (jnp.exp(g_last).astype(state.dtype)[..., None] * state
                     + jnp.einsum("bshd,bshv->bhdv", k_dec, vb))
        return new_state, o_intra + o_inter

    s0 = jnp.zeros((b, H, K, V), v.dtype)
    _, o = lax.scan(chunk_step, s0, (qc, kc, vc, gc))
    o = o.transpose(1, 0, 2, 3, 4).reshape(b, s, H, V)
    o = rms_norm(o, norm_g).reshape(b, s, GLA_VD)
    return o * jax.nn.silu(r)

def hybrid_layer(x, cos, sin, attn_norm, w_in, mla_q_norm, mla_w_uq, mla_kv_norm, mla_w_ukv,
                 ssd_conv_w, ssd_conv_b, ssd_dt_bias, ssd_a_log, ssd_d, ssd_norm,
                 gla_w_gk, gla_b_gk, gla_norm, w_out,
                 ffn_norm, ffn_w_gate, ffn_w_up, ffn_dw_w, ffn_dw_b, ffn_w_down):
    h = rms_norm(x, attn_norm)
    proj = h @ w_in
    points = np.cumsum(IN_SIZES)[:-1].tolist()
    cq, ckv, kpe, z, xbc, dt_raw, gq, gk, gv, glow, gr = jnp.split(proj, points, axis=-1)
    y_mla = mla_mixer(cq, ckv, kpe, mla_q_norm, mla_w_uq, mla_kv_norm, mla_w_ukv, cos, sin)
    y_ssd = ssd_mixer(z, xbc, dt_raw, ssd_conv_w, ssd_conv_b, ssd_dt_bias, ssd_a_log, ssd_d, ssd_norm)
    y_gla = gla_mixer(gq, gk, gv, glow, gr, gla_w_gk, gla_b_gk, gla_norm)
    x = x + jnp.concatenate([y_mla, y_ssd, y_gla], axis=-1) @ w_out
    h = rms_norm(x, ffn_norm)
    gate = causal_dwconv(h @ ffn_w_gate, ffn_dw_w, ffn_dw_b)
    return x + (jax.nn.silu(gate) * (h @ ffn_w_up)) @ ffn_w_down

def setup_inputs(seed: int = 0) -> dict:
    key = jax.random.key(seed)
    ks = jax.random.split(key, 24)

    def nrm(k, shape, scale):
        return jax.random.normal(k, shape, jnp.float32) * scale

    def gain(k, shape):
        return 1.0 + 0.02 * jax.random.normal(k, shape, jnp.float32)

    res_scale = (2 * DEPTH) ** -0.5
    dt_init = jnp.exp(jax.random.uniform(ks[9], (DEPTH, SSD_HEADS), jnp.float32,
                                         np.log(1e-3).astype(np.float32), np.log(1e-1).astype(np.float32)))
    return {
        "x": nrm(ks[0], (BATCH, SEQ, D_MODEL), 1.0),
        "attn_norm": gain(ks[1], (DEPTH, D_MODEL)),
        "w_in": nrm(ks[2], (DEPTH, D_MODEL, D_IN), D_MODEL ** -0.5),
        "mla_q_norm": gain(ks[3], (DEPTH, MLA_Q_RANK)),
        "mla_w_uq": nrm(ks[4], (DEPTH, MLA_Q_RANK, MLA_HEADS * (MLA_NOPE + MLA_ROPE)), MLA_Q_RANK ** -0.5),
        "mla_kv_norm": gain(ks[5], (DEPTH, MLA_KV_RANK)),
        "mla_w_ukv": nrm(ks[6], (DEPTH, MLA_KV_RANK, MLA_HEADS * (MLA_NOPE + MLA_V)), MLA_KV_RANK ** -0.5),
        "ssd_conv_w": nrm(ks[7], (DEPTH, SSD_CONV, SSD_CONV_DIM), SSD_CONV ** -0.5),
        "ssd_conv_b": nrm(ks[8], (DEPTH, SSD_CONV_DIM), 0.02),
        "ssd_dt_bias": dt_init + jnp.log(-jnp.expm1(-dt_init)),
        "ssd_a_log": jnp.log(jax.random.uniform(ks[10], (DEPTH, SSD_HEADS), jnp.float32, 1.0, 16.0)),
        "ssd_d": gain(ks[11], (DEPTH, SSD_HEADS)),
        "ssd_norm": gain(ks[12], (DEPTH, SSD_INNER)),
        "gla_w_gk": nrm(ks[13], (DEPTH, GLA_GATE_RANK, GLA_KD), GLA_GATE_RANK ** -0.5),
        "gla_b_gk": nrm(ks[14], (DEPTH, GLA_KD), 0.02),
        "gla_norm": gain(ks[15], (DEPTH, GLA_HEAD_V)),
        "w_out": nrm(ks[16], (DEPTH, D_MIX, D_MODEL), D_MIX ** -0.5 * res_scale),
        "ffn_norm": gain(ks[17], (DEPTH, D_MODEL)),
        "ffn_w_gate": nrm(ks[18], (DEPTH, D_MODEL, D_FF), D_MODEL ** -0.5),
        "ffn_w_up": nrm(ks[19], (DEPTH, D_MODEL, D_FF), D_MODEL ** -0.5),
        "ffn_dw_w": nrm(ks[20], (DEPTH, FFN_CONV, D_FF), FFN_CONV ** -0.5),
        "ffn_dw_b": nrm(ks[21], (DEPTH, D_FF), 0.02),
        "ffn_w_down": nrm(ks[22], (DEPTH, D_FF, D_MODEL), D_FF ** -0.5 * res_scale),
        "final_norm": gain(ks[23], (D_MODEL,)),
    }

def reference(x, attn_norm, w_in, mla_q_norm, mla_w_uq, mla_kv_norm, mla_w_ukv,
              ssd_conv_w, ssd_conv_b, ssd_dt_bias, ssd_a_log, ssd_d, ssd_norm,
              gla_w_gk, gla_b_gk, gla_norm, w_out,
              ffn_norm, ffn_w_gate, ffn_w_up, ffn_dw_w, ffn_dw_b, ffn_w_down, final_norm):
    cos, sin = rope_tables(x.shape[1], MLA_ROPE, x.dtype)
    for i in range(DEPTH):
        x = hybrid_layer(x, cos, sin, attn_norm[i], w_in[i], mla_q_norm[i], mla_w_uq[i],
                         mla_kv_norm[i], mla_w_ukv[i], ssd_conv_w[i], ssd_conv_b[i],
                         ssd_dt_bias[i], ssd_a_log[i], ssd_d[i], ssd_norm[i],
                         gla_w_gk[i], gla_b_gk[i], gla_norm[i], w_out[i],
                         ffn_norm[i], ffn_w_gate[i], ffn_w_up[i], ffn_dw_w[i], ffn_dw_b[i],
                         ffn_w_down[i])
    return rms_norm(x, final_norm)


_drawn_inputs = setup_inputs


def setup_inputs(seed=0):
    import zlib

    import numpy as np

    out = dict(_drawn_inputs(seed))
    spreads = {}
    factors = {'attn_norm': 3.826,
     'mla_q_norm': 8.0,
     'mla_kv_norm': 8.0,
     'ssd_conv_b': 5.705,
     'ssd_d': 8.0,
     'ssd_norm': 8.0,
     'gla_b_gk': 8.0,
     'gla_norm': 8.0,
     'ffn_norm': 4.934,
     'ffn_dw_b': 7.026,
     'final_norm': 2.879}
    for name, (base, spread) in spreads.items():
        noise = np.random.default_rng([zlib.crc32(name.encode()), seed]).standard_normal(out[name].shape)
        drawn = base * np.exp(spread * noise) if base else spread * noise
        out[name] = __import__('jax').numpy.asarray(drawn.astype(out[name].dtype))
    for name, factor in factors.items():
        out[name] = (out[name] * factor).astype(out[name].dtype)
    return out
```

```python
import numpy as np
import concourse.bass as bass
from concourse import mybir
from contextlib import ExitStack

F32 = mybir.dt.float32
F32R = mybir.dt.float32r
U8 = mybir.dt.uint8
ALU = mybir.AluOpType
ACT = mybir.ActivationFunctionType
AX = mybir.AxisListType

P = 128
D = 2048
T = 256
DEPTH = 2
EPS = 1e-6
KT = D // P
TP = T // P
HEADS_MLA, ROPE = 8, 64
SCALE = float((128 + 64) ** -0.5)
SSD_H, SSD_P, SSD_TAPS, XBC = 8, 64, 4, 8
GLA_CH = 64
GLA_TAU = 16.0
LEVELS = 6
FT = 44
HALF = FT // 2
FTAPS = 3

T_XBC, T_Z, T_CQ, T_CKV, T_GQ, T_GK, T_GV, T_GR, T_MIX = 0, 8, 12, 16, 18, 20, 22, 26, 30
IN_TILES = 31
MIX_GLOW, MIX_DT = 64, 96

CHUNK = 16 * P
DOWN_KT = 11
DOWN_CHUNK = DOWN_KT * P
RAW, SPLIT = 2, 2

Q_IN, Q_OUT = 0, 9
Q_GATE = (13, 32)
Q_DOWN = (24, 43)
QUADS = 51
B_IN, B_MLA, B_OUT = 0, 8, 13
B_GATE = (17, 32)
B_DOWN = (28, 43)
TURNS = 47

C_ATTN, C_FFN, C_QG, C_KVG, C_SSDG, C_DSK, C_GLAG, C_BGK = 0, 16, 32, 36, 38, 42, 46, 47
C_DTB, C_ALOG, C_CONV, C_CONVB, C_FW, C_FB, C_WGK = 49, 57, 65, 97, 105, 237, 281
NPAR = C_WGK + 256

K_ID, K_ONES, K_SWAP, K_TRI, K_COS, K_SIN, K_MASK = 0, 128, 256, 384, 512, 768, 1024
NCONST = K_MASK + 384


def turn_of(bank, layer, turn):
    if bank == 3:
        return layer * (TURNS - 1) + (turn - 1 if isinstance(turn, int) and turn >= B_MLA else turn)
    return layer * TURNS + turn


def build(nc, x_in, gains_in, params_in, consts_in, masks_in, front_in, out_in, gate_in, down_in, y_out):
    ctx = ExitStack()
    with ctx:
        def sb(name, shape, dt=F32, where=ctx):
            return where.enter_context(nc.sbuf_tensor(name, shape, dt))

        x = sb("x", [P, KT, T])
        raw = sb("raw", [P, RAW, CHUNK])
        w_hi = sb("w_hi", [P, SPLIT, CHUNK], F32R)
        w_lo = sb("w_lo", [P, SPLIT, CHUNK], F32R)
        par = sb("par", [P, NPAR])
        const = sb("const", [P, NCONST])
        gains = sb("gains", [P, (DEPTH + 1) * KT])
        masks = sb("masks", [P, LEVELS * P + 2 * T], U8)
        ssq = sb("ssq", [P, T])
        sqt = sb("sqt", [P, T])
        rstd = sb("rstd", [P, T])
        eps = sb("eps", [P, 1])
        cat_hi = sb("cat_hi", [P, KT, T], F32R)
        cat_lo = sb("cat_lo", [P, KT, T], F32R)

        with ExitStack() as first:
            h_hi = sb("h_hi", [P, KT, T], F32R, first)
            h_lo = sb("h_lo", [P, KT, T], F32R, first)
            top = nc.sbuf_base
        with ExitStack() as second:
            qn = sb("qn", [P, HEADS_MLA, T], F32, second)
            kn = sb("kn", [P, HEADS_MLA, T], F32, second)
            vv = sb("vv", [P, TP, HEADS_MLA * P], F32, second)
            qp = sb("qp", [P, HEADS_MLA // 2, T], F32, second)
            kp = sb("kp", [P, T], F32, second)
            small = sb("small", [P, 512], F32, second)
        pad = sb("h_region", [P, 2 * KT * T])

        with ExitStack() as first:
            proj = sb("proj", [P, IN_TILES, T], F32, first)
            with ExitStack() as ssd:
                xc = sb("xc", [P, XBC, T], F32, ssd)
                xdt = sb("xdt", [P, TP, SSD_H * SSD_P], F32, ssd)
                btok = sb("btok", [P, 256], F32, ssd)
                dec = sb("dec", [P, TP, SSD_H, P], F32, ssd)
                cea = sb("cea", [P, SSD_H, P], F32, ssd)
                gm = sb("gm", [P, 4, P], F32, ssd)
                dsx = sb("dsx", [P, SSD_H * SSD_P], F32, ssd)
                sst = sb("sst", [P, SSD_H * SSD_P], F32, ssd)
            with ExitStack() as gla:
                ebig = sb("ebig", [P, 8, 2 * T], F32, gla)
                qall = sb("qall", [P, LEVELS, 2 * T], F32, gla)
                attn = sb("attn", [P, 2, 4 * P], F32, gla)
            with ExitStack() as mla:
                prob = sb("prob", [P, HEADS_MLA, 3 * P], F32, mla)
                probt = sb("probt", [P, 2, 3 * P], F32, mla)
                ropet = sb("ropet", [P, 4 * T], F32, mla)
        with ExitStack() as second:
            hid_hi = sb("hid_hi", [P, HALF, T], F32R, second)
            hid_lo = sb("hid_lo", [P, HALF, T], F32R, second)
            gs = sb("gs", [P, 2, T], F32, second)
            cv = sb("cv", [P, 2, T], F32, second)
            sl = sb("sl", [P, 2, T], F32, second)
            us = sb("us", [P, 2, T], F32, second)
            hv = sb("hv", [P, 2, T], F32, second)

        ident = const[:, K_ID:K_ID + P]
        ones = const[:, K_ONES:K_ONES + P]
        swap = const[:, K_SWAP:K_SWAP + P]
        tri = const[:, K_TRI:K_TRI + P]
        cos = const[:, K_COS:K_COS + T]
        sin = const[:, K_SIN:K_SIN + T]
        causal = const[:, K_MASK:K_MASK + 3 * P]
        keep = masks[:, LEVELS * P:LEVELS * P + 2 * T]
        bank = [ctx.enter_context(nc.psum_tensor(f"bank{i}", [P, 512], F32)) for i in range(8)]

        def scol(i, n=1):
            return small[:, i:i + n]

        ta = proj[:, 0:8, :].rearrange("p a t -> p (a t)")
        y_ssd = proj[:, 0:4, :]
        sq_ssd = proj[:, 4:8, :]
        v_gla = proj[:, 0:4, :].rearrange("p a t -> p (a t)").rearrange("p (b n) -> p b n", b=TP)
        kd_t = proj[:, 4:6, :].rearrange("p a t -> p (a t)").rearrange("p (b h n) -> p b h n", b=TP, h=2)
        st_gla = proj[:, 8:12, :].rearrange("p a t -> p (a t)")[:, 0:768].rearrange("p (c h n) -> p c h n", c=3, h=2)
        g_raw = qall[:, 0, :]
        g_neg = qall[:, 1, :]
        g_cum = qall[:, 2, :]
        qs = proj[:, T_GQ:T_GQ + 2, :].rearrange("p a t -> p (a t)")
        ks = proj[:, T_GK:T_GK + 2, :].rearrange("p a t -> p (a t)")
        o_sq = ebig[:, 0:2, :]
        o_rstd = ebig[:, 2:4, :]
        o_y = ebig[:, 4:6, :]

        def sem(name):
            return ctx.enter_context(nc.semaphore(name))

        s_x_loaded = sem("x_loaded")
        s_consts_loaded = sem("consts_loaded")
        s_masks_set = sem("masks_set")
        s_params_loaded = sem("params_loaded")
        s_params_free = sem("params_free")
        s_y_stored = sem("y_stored")
        s_eps_set = sem("eps_set")
        s_hi_ready = sem("hi_ready")
        s_lo_ready = sem("lo_ready")
        s_chunks_used = sem("chunks_used")
        s_x_ready = sem("x_ready")
        s_h_hi_ready = sem("h_hi_ready")
        s_h_ready = sem("h_ready")
        s_sq_ready = sem("sq_ready")
        s_ssq_added = sem("ssq_added")
        s_ssq_zeroed = sem("ssq_zeroed")
        s_sums_ready = sem("sums_ready")
        s_rstd_log = sem("rstd_log")
        s_rstd_ready = sem("rstd_ready")
        s_proj_ready = sem("proj_ready")
        s_conv_step = sem("conv_step")
        s_conv_ready = sem("conv_ready")
        s_silu_ready = sem("silu_ready")
        s_gate_step = sem("gate_step")
        s_gate_ready = sem("gate_ready")
        s_gate_silu = sem("gate_silu")
        s_hid_ready = sem("hid_ready")
        s_hid_hi_ready = sem("hid_hi_ready")
        s_hid_split = sem("hid_split")
        s_mla_sq = sem("mla_sq")
        s_mla_sums = sem("mla_sums")
        s_mla_log = sem("mla_log")
        s_mla_rstd = sem("mla_rstd")
        s_mla_normed = sem("mla_normed")
        s_mla_hi = sem("mla_hi")
        s_mla_split = sem("mla_split")
        s_mla_evac = sem("mla_evac")
        s_mla_evac2 = sem("mla_evac2")
        s_rope_swapped = sem("rope_swapped")
        s_k_rope = sem("k_rope")
        s_k_dup = sem("k_dup")
        s_q_rope = sem("q_rope")
        s_scores_ready = sem("scores_ready")
        s_masked = sem("masked")
        s_prob_ready = sem("prob_ready")
        s_prob_norm = sem("prob_norm")
        s_probt_ready = sem("probt_ready")
        s_probt_copied = sem("probt_copied")
        s_o_ready = sem("o_ready")
        s_o_hi = sem("o_hi")
        s_o_lo = sem("o_lo")
        s_dt_t = sem("dt_t")
        s_xs_t = sem("xs_t")
        s_dt_abs = sem("dt_abs")
        s_dt_exp = sem("dt_exp")
        s_dt_log = sem("dt_log")
        s_neg_a = sem("neg_a")
        s_a_ready = sem("a_ready")
        s_xdt_ready = sem("xdt_ready")
        s_btok_ready = sem("btok_ready")
        s_ta_ready = sem("ta_ready")
        s_acum_ready = sem("acum_ready")
        s_acum_copied = sem("acum_copied")
        s_cumb_ready = sem("cumb_ready")
        s_seg_ready = sem("seg_ready")
        s_seg_exp = sem("seg_exp")
        s_ea_exp = sem("ea_exp")
        s_ds_pre = sem("ds_pre")
        s_ds_exp = sem("ds_exp")
        s_cb_ready = sem("cb_ready")
        s_m_ready = sem("m_ready")
        s_cea_ready = sem("cea_ready")
        s_dsx_ready = sem("dsx_ready")
        s_state_ready = sem("state_ready")
        s_state_copied = sem("state_copied")
        s_y_ready = sem("y_ready")
        s_y_gated = sem("y_gated")
        s_y_sq = sem("y_sq")
        s_y_sums = sem("y_sums")
        s_y_log = sem("y_log")
        s_y_rstd = sem("y_rstd")
        s_y_normed = sem("y_normed")
        s_y_hi = sem("y_hi")
        s_ssd_cat = sem("ssd_cat")
        s_vec_step = sem("vec_step")
        s_gl_pre = sem("gl_pre")
        s_gl_v = sem("gl_v")
        s_gl_neg = sem("gl_neg")
        s_gl_exp = sem("gl_exp")
        s_gl_log = sem("gl_log")
        s_gl_diff = sem("gl_diff")
        s_gl_e = sem("gl_e")
        s_gl_qs = sem("gl_qs")
        s_gl_vcopied = sem("gl_vcopied")
        s_gl_q = sem("gl_q")
        s_gl_k = sem("gl_k")
        s_gl_kt = sem("gl_kt")
        s_gl_ktc = sem("gl_ktc")
        s_gl_zero = sem("gl_zero")
        s_gl_lvl = sem("gl_lvl")
        s_gl_put = sem("gl_put")
        s_gl_u = sem("gl_u")
        s_gl_s = sem("gl_s")
        s_gl_o = sem("gl_o")
        s_gl_osq = sem("gl_osq")
        s_gl_osum = sem("gl_osum")
        s_gl_olog = sem("gl_olog")
        s_gl_orstd = sem("gl_orstd")
        s_gl_y = sem("gl_y")
        s_gl_hi = sem("gl_hi")
        s_gl_cat = sem("gl_cat")
        s_gl_scan = sem("gl_scan")
        s_final_ready = sem("final_ready")
        s_passed_act = sem("passed_act")
        s_passed_dve = sem("passed_dve")
        s_passed_pe = sem("passed_pe")
        raw_landed = [sem(f"raw_landed{i}") for i in range(RAW)]
        bank_free = [sem(f"bank_free{i}") for i in range(4)]

        block = ctx.enter_context(nc.Block())

        @block.sync
        def _(sp):
            sp.dma_start(x[:], x_in).then_inc(s_x_loaded, 16)
            sp.dma_start(gains[:], gains_in).then_inc(s_x_loaded, 16)

            def load(source, row, quad, j, width=CHUNK):
                sp.wait_ge(s_lo_ready, quad * 4 + j + 1)
                sp.dma_start(raw[:, j % RAW, 0:width],
                             source[bass.ds(row, 1), :, :].rearrange("a p n -> p (a n)")).then_inc(raw_landed[j % RAW], 16)

            with sp.Fori(0, DEPTH) as L:
                with sp.Fori(0, 9) as i:
                    for j in range(4):
                        load(front_in, L * 36 + i * 4 + j, L * QUADS + i, j)
                with sp.Fori(0, 4) as i:
                    for j in range(4):
                        load(out_in, L * 16 + i * 4 + j, L * QUADS + Q_OUT + i, j)
                for half in range(2):
                    with sp.Fori(0, 11) as i:
                        for j in range(4):
                            load(gate_in, L * 88 + half * 44 + i * 4 + j, L * QUADS + Q_GATE[half] + i, j)
                    with sp.Fori(0, 8) as i:
                        for j in range(4):
                            load(down_in, L * 64 + half * 32 + i * 4 + j, L * QUADS + Q_DOWN[half] + i, j, DOWN_CHUNK)
            sp.wait_ge(s_final_ready, KT)
            sp.dma_start(y_out, x[:]).then_inc(s_y_stored, 16)
            sp.wait_ge(s_y_stored, 16)

        @block.gpsimd
        def _(pool):
            pool.dma_start(const[:], consts_in).then_inc(s_consts_loaded, 16)
            pool.dma_start(proj[:, 0:5, :].rearrange("p a t -> p (a t)"), masks_in).then_inc(s_consts_loaded, 16)
            with pool.Fori(0, DEPTH) as L:
                pool.wait_ge(s_params_free, L + 1)
                pool.dma_start(par[:], params_in[bass.ds(L, 1), :, :].rearrange("a p n -> p (a n)")).then_inc(s_params_loaded, 16)

        @block.scalar
        def _(act):
            def split_hi(quad, j, width=CHUNK):
                j, quad = j % 4, quad + j // 4
                act.wait_ge(raw_landed[j % RAW], quad * 32 + 16 * (j // RAW + 1))
                act.wait_ge(s_chunks_used, quad * 4 + j + 1)
                nc.scalar.copy(w_hi[:, j % SPLIT, 0:width], raw[:, j % RAW, 0:width]).then_inc(s_hi_ready, 1)

            def refresh(tile, nth, gain):
                act.sem_inc(s_passed_act, 1)
                nc.scalar.activation(h_hi[:, bass.ds(tile, 1), :], x[:, bass.ds(tile, 1), :], ACT.Copy,
                                     scale=gain).then_inc(s_h_hi_ready, 1)
                act.wait_ge(s_ssq_added, nth + 1)
                act.sem_inc(s_passed_act, 1)
                nc.scalar.activation(sqt[:], x[:, bass.ds(tile, 1), :].rearrange("p a t -> p (a t)"),
                                     ACT.Square).then_inc(s_sq_ready, 1)

            def token_rstd(nth):
                act.wait_ge(s_sums_ready, nth + 1)
                nc.scalar.activation(rstd[:], bank[4][:, 0:T], ACT.Ln, bias=eps[:], scale=1.0 / D).then_inc(s_rstd_log, 1)
                act.wait_ge(s_rstd_log, nth + 1)
                nc.scalar.activation(rstd[:], rstd[:], ACT.Exp, scale=-0.5).then_inc(s_rstd_ready, 1)

            act.wait_ge(s_x_loaded, 32)
            act.sem_inc(s_passed_act, 1)
            with act.Fori(0, KT) as m:
                refresh(m, m, gains[:, bass.ds(m, 1)])

            with act.Fori(0, DEPTH) as L:
                q0 = L * QUADS
                split_hi(q0, 0)
                split_hi(q0, 1)
                token_rstd(L * 2)
                act.sem_inc(s_passed_act, 1)
                with act.Fori(0, 7) as i:
                    for j in range(4):
                        split_hi(q0 + i, j + 2)
                for j in range(3):
                    split_hi(q0 + 7, j + 2)
                act.wait_ge(s_conv_ready, 8 * (L + 1))
                nc.scalar.activation(xc[:], xc[:], ACT.Silu).then_inc(s_silu_ready, 1)
                act.wait_ge(s_proj_ready, IN_TILES * (L + 1))
                nc.scalar.activation(proj[:, T_Z:T_Z + 4, :], proj[:, T_Z:T_Z + 4, :], ACT.Silu).then_inc(s_silu_ready, 1)
                nc.scalar.activation(proj[:, T_GR:T_GR + 4, :], proj[:, T_GR:T_GR + 4, :], ACT.Silu).then_inc(s_silu_ready, 1)

                nc.scalar.activation(qn[:, 0:6, :], proj[:, T_CQ:T_CQ + 6, :], ACT.Square).then_inc(s_mla_sq, 1)
                act.wait_ge(s_mla_sums, L + 1)
                nc.scalar.activation(kn[:, 0, :], bank[5][:, 0:T], ACT.Ln, bias=eps[:], scale=1.0 / 512).then_inc(s_mla_log, 1)
                nc.scalar.activation(kn[:, 1, :], bank[5][:, T:2 * T], ACT.Ln, bias=eps[:], scale=1.0 / 256).then_inc(s_mla_log, 1)
                act.wait_ge(s_mla_log, 2 * (L + 1))
                nc.scalar.activation(kn[:, 2:4, :], kn[:, 0:2, :], ACT.Exp, scale=-0.5).then_inc(s_mla_rstd, 1)
                act.wait_ge(s_params_loaded, 16 * (L + 1))
                for k in range(6):
                    act.wait_ge(s_mla_normed, 2 * L + (1 if k < 4 else 2))
                    nc.scalar.activation(cat_hi[:, k, :], proj[:, T_CQ + k, :], ACT.Copy,
                                         scale=par[:, C_QG + k:C_QG + k + 1]).then_inc(s_mla_hi, 1)
                for c in range(5):
                    if c + 2 < 5:
                        split_hi(q0 + 7, 3 + c + 2)
                    act.wait_ge(s_chunks_used, q0 * 4 + 31 + c + 1 + SPLIT)
                    for b in range(4):
                        if c < 2:
                            nc.scalar.copy(qn[:, 4 * c + b, :], bank[b][:, 0:T]).then_inc(bank_free[b], 1)
                        if c == 3:
                            nc.scalar.copy(kn[:, 2 * b:2 * b + 2, :], bank[b][:, :].rearrange("p (a t) -> p a t", a=2)).then_inc(bank_free[b], 1)
                    if c == 1 or c == 3:
                        for b in range(4):
                            act.wait_ge(bank_free[b], turn_of(b, L, B_MLA + c) + 2)
                        act.sem_inc(s_mla_evac, 1)

                act.wait_ge(s_dt_abs, L + 1)
                nc.scalar.activation(scol(32, 16), scol(16, 16), ACT.Exp).then_inc(s_dt_exp, 1)
                nc.scalar.activation(scol(64, 8), par[:, C_ALOG:C_ALOG + 8], ACT.Exp).then_inc(s_neg_a, 1)
                act.wait_ge(s_dt_exp, L + 1)
                nc.scalar.activation(scol(48, 16), scol(32, 16), ACT.Ln, bias=1.0).then_inc(s_dt_log, 1)
                act.wait_ge(s_xs_t, 3 * (L + 1))
                nc.scalar.copy(btok[:], bank[7][:, 0:256]).then_inc(s_btok_ready, 1)
                act.wait_ge(s_ds_pre, L + 1)
                nc.scalar.activation(scol(128, 8), scol(120, 8), ACT.Exp).then_inc(s_ds_exp, 1)
                act.wait_ge(s_seg_ready, 4 * (L + 1))
                nc.scalar.activation(dec[:], dec[:], ACT.Exp).then_inc(s_seg_exp, 1)
                for g in range(2):
                    nc.scalar.activation(cea[:, 4 * g:4 * g + 4, :], bank[6 + g][:, :].rearrange("p (h t) -> p h t", h=4),
                                         ACT.Exp).then_inc(s_ea_exp, 1)
                act.wait_ge(s_state_ready, L + 1)
                nc.scalar.copy(sst[:], bank[5][:, :]).then_inc(s_state_copied, 1)
                act.wait_ge(s_y_gated, L + 1)
                nc.scalar.activation(sq_ssd, y_ssd, ACT.Square).then_inc(s_y_sq, 1)
                act.wait_ge(s_y_sums, L + 1)
                nc.scalar.activation(gm[:, 0:2, :].rearrange("p a t -> p (a t)"), bank[4][:, 0:T], ACT.Ln, bias=eps[:],
                                     scale=1.0 / 512).then_inc(s_y_log, 1)
                act.wait_ge(s_y_log, L + 1)
                nc.scalar.activation(gm[:, 2:4, :], gm[:, 0:2, :], ACT.Exp, scale=-0.5).then_inc(s_y_rstd, 1)
                act.wait_ge(s_y_normed, L + 1)
                for k in range(4):
                    nc.scalar.activation(cat_hi[:, 8 + k, :], y_ssd[:, k, :], ACT.Copy,
                                         scale=par[:, C_SSDG + k:C_SSDG + k + 1]).then_inc(s_y_hi, 1)

                nc.scalar.activation(qs, qs, ACT.Copy, scale=GLA_CH ** -0.5).then_inc(s_gl_qs, 1)
                act.wait_ge(s_gl_neg, L + 1)
                nc.scalar.activation(g_neg, g_neg, ACT.Exp).then_inc(s_gl_exp, 1)
                act.wait_ge(s_gl_exp, L + 1)
                nc.scalar.activation(g_neg, g_neg, ACT.Ln, bias=1.0).then_inc(s_gl_log, 1)
                act.wait_ge(s_gl_v, L + 1)
                act.wait_ge(s_ssd_cat, 4 * (L + 1))
                nc.scalar.copy(v_gla[:, 0, :], bank[5][:, :]).then_inc(s_gl_vcopied, 1)
                nc.scalar.copy(v_gla[:, 1, :], bank[6][:, :]).then_inc(s_gl_vcopied, 1)
                act.wait_ge(s_gl_diff, L + 1)
                nc.scalar.activation(ebig[:], ebig[:], ACT.Exp, scale=1.0 / GLA_TAU).then_inc(s_gl_e, 1)
                act.wait_ge(s_gl_kt, L + 1)
                nc.scalar.copy(kd_t, bank[4][:, :].rearrange("p (b h n) -> p b h n", b=TP, h=2)).then_inc(s_gl_ktc, 1)
                act.wait_ge(s_gl_o, L + 1)
                for par_ in range(2):
                    nc.scalar.activation(o_sq[:, par_, :], bank[4 + par_][:, :], ACT.Square).then_inc(s_gl_osq, 1)
                act.wait_ge(s_gl_osum, L + 1)
                for par_ in range(2):
                    nc.scalar.activation(o_rstd[:, par_, :], bank[6 + par_][:, :], ACT.Ln, bias=eps[:],
                                         scale=1.0 / P).then_inc(s_gl_olog, 1)
                act.wait_ge(s_gl_olog, 2 * (L + 1))
                nc.scalar.activation(o_rstd, o_rstd, ACT.Exp, scale=-0.5).then_inc(s_gl_orstd, 1)
                act.wait_ge(s_gl_y, L + 1)
                nc.scalar.copy(cat_hi[:, 12:16, :].rearrange("p (h q) t -> p q h t", q=2),
                               o_y.rearrange("p q (h t) -> p q h t", h=2)).then_inc(s_gl_hi, 1)

                act.wait_ge(s_k_rope, L + 1)
                nc.scalar.copy(kp[64:128, :], kp[0:64, :]).then_inc(s_k_dup, 1)

                def weights_of(h):
                    act.wait_ge(s_masked, 8 * L + h + 1)
                    for qb, lo_, hi_ in ((0, 0, P), (1, P, 3 * P)):
                        nc.scalar.activation(prob[:, h, lo_:hi_], prob[:, h, lo_:hi_], ACT.Exp, scale=SCALE,
                                             bias=scol(192 + 2 * h + qb), accum_out=scol(224 + 2 * h + qb)).then_inc(s_prob_ready, 1)

                def copy_transposed(h):
                    act.wait_ge(s_probt_ready, 8 * L + h + 1)
                    if h >= 2:
                        act.wait_ge(s_o_ready, 8 * L + h - 1)
                    nc.scalar.copy(probt[:, h % 2, :], bank[6][:, 0:3 * P]).then_inc(s_probt_copied, 1)

                def split_out(h):
                    act.wait_ge(s_o_ready, 8 * L + h + 1)
                    nc.scalar.copy(cat_hi[:, h, :], bank[7][:, 0:T]).then_inc(s_o_hi, 1)

                for h in range(HEADS_MLA + 2):
                    if h < HEADS_MLA:
                        weights_of(h)
                    if 1 <= h <= HEADS_MLA:
                        copy_transposed(h - 1)
                    if h >= 2:
                        split_out(h - 2)

                split_hi(q0 + Q_OUT, 0)
                split_hi(q0 + Q_OUT, 1)
                act.sem_inc(s_passed_act, 1)
                with act.Fori(0, 4) as i:
                    for j in range(4):
                        split_hi(q0 + Q_OUT + i, j + 2)
                        m = i * 4 + j
                        act.wait_ge(s_x_ready, L * 2 * KT + m + 1)
                        refresh(m, KT + L * 2 * KT + m, par[:, bass.ds(m + C_FFN, 1)])
                token_rstd(L * 2 + 1)

                for half in range(2):
                    def hidden(i, j, ahead):
                        f = j // 2
                        nth = L * FT + half * HALF + i * 2 + f
                        if ahead:
                            split_hi(q0 + Q_GATE[half] + i, j + 2, *ahead)
                        if j % 2 == 1:
                            act.wait_ge(s_gate_ready, nth + 1)
                            nc.scalar.activation(sl[:, f, :], cv[:, f, :], ACT.Silu).then_inc(s_gate_silu, 1)
                        if j >= 2:
                            g = j - 2
                            act.wait_ge(s_hid_ready, L * FT + half * HALF + i * 2 + g + 1)
                            nc.scalar.copy(hid_hi[:, bass.ds(i * 2 + g, 1), :], hv[:, g:g + 1, :]).then_inc(s_hid_hi_ready, 1)

                    act.sem_inc(s_passed_act, 1)
                    with act.Fori(0, 10) as i:
                        for j in range(4):
                            hidden(i, j, (CHUNK,))
                    for j in range(4):
                        hidden(10, j, (CHUNK,) if j < 2 else (DOWN_CHUNK,))
                    def down(i, jj, ahead):
                        if ahead:
                            split_hi(q0 + Q_DOWN[half] + i * 2, jj + 2, ahead)
                        if half == 1 and jj % 2 == 1:
                            m = i * 4 + jj // 2
                            act.wait_ge(s_x_ready, L * 2 * KT + KT + m + 1)
                            refresh(m, KT + L * 2 * KT + KT + m, gains[:, bass.ds((L + 1) * KT + m, 1)])

                    act.sem_inc(s_passed_act, 1)
                    with act.Fori(0, 3) as i:
                        for jj in range(8):
                            down(i, jj, DOWN_CHUNK)
                    for jj in range(8):
                        down(3, jj, DOWN_CHUNK if jj < 6 else (CHUNK if half == 0 else None))

            token_rstd(2 * DEPTH)

        @block.vector
        def _(dve):
            def split_lo(quad, j, width=CHUNK):
                j, quad = j % 4, quad + j // 4
                dve.wait_ge(s_hi_ready, quad * 4 + j + 1)
                nc.vector.tensor_tensor(w_lo[:, j % SPLIT, 0:width], raw[:, j % RAW, 0:width],
                                        w_hi[:, j % SPLIT, 0:width].bitcast(F32), ALU.subtract).then_inc(s_lo_ready, 1)

            def refresh(tile, nth, gain):
                at = bass.ds(tile, 1)
                dve.wait_ge(s_h_hi_ready, nth + 1)
                nc.vector.scalar_tensor_tensor(out=h_lo[:, at, :], in0=x[:, at, :], scalar=gain,
                                               in1=h_hi[:, at, :].bitcast(F32), op0=ALU.mult,
                                               op1=ALU.subtract).then_inc(s_h_ready, 1)
                dve.wait_ge(s_sq_ready, nth + 1)
                dve.wait_ge(s_ssq_added, nth + 1)
                nc.vector.tensor_tensor(ssq[:], ssq[:], sqt[:], ALU.add).then_inc(s_ssq_added, 1)

            nc.vector.memset(eps[:], EPS).then_inc(s_eps_set, 1)
            nc.vector.memset(ssq[:], 0.0).then_inc(s_ssq_zeroed, 1)
            dve.wait_ge(s_consts_loaded, 32)
            nc.vector.tensor_copy(masks[:], proj[:, 0:5, :].rearrange("p a t -> p (a t)")).then_inc(s_masks_set, 1)
            dve.wait_ge(s_masks_set, 1)
            dve.sem_inc(s_lo_ready, RAW)
            dve.sem_inc(s_ssq_added, 1)
            dve.sem_inc(s_params_free, 1)
            for b in range(4):
                dve.sem_inc(bank_free[b], 1)
            dve.wait_ge(s_ssq_zeroed, 1)
            dve.sem_inc(s_passed_dve, 1)
            with dve.Fori(0, KT) as m:
                refresh(m, m, gains[:, bass.ds(m, 1)])

            class Steps:
                def __init__(self, counted, before):
                    self.counted, self.before, self.n = counted, before, 0

                def step(self, ins):
                    ins.then_inc(self.counted, 1)
                    self.n += 1

                def settle(self):
                    dve.wait_ge(self.counted, self.before + self.n)

            with dve.Fori(0, DEPTH) as L:
                q0 = L * QUADS
                n0 = q0 * 4
                split_lo(q0, 0)
                split_lo(q0, 1)
                dve.wait_ge(s_params_loaded, 16 * (L + 1))

                def take(b, turn, chunk, tile):
                    dve.wait_ge(s_chunks_used, n0 + chunk + 1 + SPLIT)
                    nc.vector.tensor_tensor(proj[:, bass.ds(tile, 1), :].rearrange("p a t -> p (a t)"),
                                            bank[b][:, 0:T], rstd[:], ALU.mult).then_inc(bank_free[b], 1)

                dve.wait_ge(s_rstd_ready, 2 * L + 1)
                dve.sem_inc(s_passed_dve, 1)
                with dve.Fori(0, 2) as i:
                    for j in range(4):
                        t = i * 4 + j
                        split_lo(q0 + i, j + 2)
                        take(j, i, i * 4 + j, t)
                        dve.wait_ge(bank_free[j], turn_of(j, L, i) + 2)
                        tile, out = proj[:, bass.ds(t, 1), :], xc[:, bass.ds(t, 1), :]
                        for k in range(SSD_TAPS):
                            tap = par[:, bass.ds(t * SSD_TAPS + (C_CONV + SSD_TAPS - 1 - k), 1)]
                            if k == 0:
                                nc.vector.tensor_scalar(out, tile, tap, par[:, bass.ds(t + C_CONVB, 1)],
                                                        ALU.mult, ALU.add).then_inc(s_conv_step, 1)
                            else:
                                dve.wait_ge(s_conv_step, (L * 8 + t) * 3 + k)
                                nc.vector.scalar_tensor_tensor(
                                    out=out[:, :, k:T], in0=tile[:, :, 0:T - k], scalar=tap, in1=out[:, :, k:T],
                                    op0=ALU.mult, op1=ALU.add).then_inc(s_conv_step if k < 3 else s_conv_ready, 1)
                with dve.Fori(2, 7) as i:
                    for j in range(4):
                        split_lo(q0 + i, j + 2)
                        take(j, i, i * 4 + j, i * 4 + j)
                for j in range(3):
                    split_lo(q0 + 7, j + 2)
                    take(j, 7, 28 + j, 28 + j)
                for b in range(4):
                    dve.wait_ge(bank_free[b], turn_of(b, L, 8 if b < 3 else 7) + 1)
                dve.sem_inc(s_proj_ready, IN_TILES)

                dve.wait_ge(s_mla_rstd, L + 1)
                cq, ckv = proj[:, T_CQ:T_CQ + 4, :], proj[:, T_CKV:T_CKV + 2, :]
                nc.vector.tensor_tensor(cq, cq, kn[:, 2:3, :].to_broadcast([P, 4, T]), ALU.mult).then_inc(s_mla_normed, 1)
                nc.vector.tensor_tensor(ckv, ckv, kn[:, 3:4, :].to_broadcast([P, 2, T]), ALU.mult).then_inc(s_mla_normed, 1)
                dve.wait_ge(s_mla_normed, 2 * (L + 1))
                for k in range(6):
                    dve.wait_ge(s_mla_hi, 6 * L + k + 1)
                    nc.vector.scalar_tensor_tensor(out=cat_lo[:, k, :], in0=proj[:, T_CQ + k, :],
                                                   scalar=par[:, C_QG + k:C_QG + k + 1],
                                                   in1=cat_hi[:, k, :].bitcast(F32), op0=ALU.mult,
                                                   op1=ALU.subtract).then_inc(s_mla_split, 1)
                for c in range(5):
                    if c + 2 < 5:
                        split_lo(q0 + 7, 3 + c + 2)
                    dve.wait_ge(s_chunks_used, n0 + 31 + c + 1 + SPLIT)
                    for b in range(4):
                        if c == 2:
                            nc.vector.tensor_copy(qp[:, b, :], bank[b][:, 0:T]).then_inc(bank_free[b], 1)
                        if c == 4:
                            nc.vector.tensor_copy(vv[:, b // 2, (b % 2) * 512:(b % 2) * 512 + 512], bank[b][:, :]).then_inc(bank_free[b], 1)
                for b in range(4):
                    dve.wait_ge(bank_free[b], L * (TURNS - (b == 3)) + 13 - (b == 3) + 1)
                dve.sem_inc(s_mla_evac2, 1)

                vec = Steps(s_vec_step, L * VEC_STEPS)
                step, settle = vec.step, vec.settle

                dve.wait_ge(s_dt_t, L + 1)
                two8 = lambda ap: ap.rearrange("p (c h) -> p c h", c=TP)
                step(nc.vector.tensor_tensor(two8(scol(0, 16)), two8(bank[4][:, 0:16]),
                                             par[:, C_DTB:C_DTB + 8].unsqueeze(1).to_broadcast([P, TP, 8]), ALU.add))
                settle()
                nc.vector.scalar_tensor_tensor(out=scol(16, 16), in0=scol(0, 16), scalar=-1.0, in1=scol(0, 16),
                                               op0=ALU.mult, op1=ALU.min).then_inc(s_dt_abs, 1)
                dve.wait_ge(s_dt_log, L + 1)
                step(nc.vector.scalar_tensor_tensor(out=scol(80, 16), in0=scol(0, 16), scalar=0.0, in1=scol(48, 16),
                                                    op0=ALU.max, op1=ALU.add))
                settle()
                dve.wait_ge(s_neg_a, L + 1)
                nc.vector.scalar_tensor_tensor(out=two8(scol(96, 16)), in0=two8(scol(80, 16)), scalar=-1.0,
                                               in1=scol(64, 8).unsqueeze(1).to_broadcast([P, TP, 8]),
                                               op0=ALU.mult, op1=ALU.mult).then_inc(s_a_ready, 1)
                dve.wait_ge(s_a_ready, L + 1)
                nc.vector.tensor_tensor(ta.rearrange("p (a t) -> p a t", t=P),
                                        scol(96, 16).unsqueeze(2).to_broadcast([P, 16, P]),
                                        tri.unsqueeze(1).to_broadcast([P, 16, P]), ALU.mult).then_inc(s_ta_ready, 1)
                dve.wait_ge(s_xs_t, 3 * (L + 1))
                for c in range(TP):
                    nc.vector.tensor_tensor(xdt[:, c, :].rearrange("p (h q) -> p h q", h=8),
                                            bank[5 + c][:, :].rearrange("p (h q) -> p h q", h=8),
                                            scol(80 + 8 * c, 8).unsqueeze(2).to_broadcast([P, 8, SSD_P]),
                                            ALU.mult).then_inc(s_xdt_ready, 1)
                dve.wait_ge(s_acum_ready, L + 1)
                nc.vector.tensor_copy(scol(144, 16), bank[7][:, 256:272]).then_inc(s_acum_copied, 1)
                dve.wait_ge(s_acum_copied, L + 1)
                for c in range(TP):
                    for g in range(2):
                        dve.wait_ge(s_cumb_ready, 4 * L + 2 * c + g + 1)
                        b = bank[4 + 2 * c + g]
                        for h in range(4):
                            ins = nc.vector.tensor_scalar(dec[:, c, 4 * g + h, :], b[:, h * P:(h + 1) * P],
                                                          scol(144 + 8 * c + 4 * g + h), 0.0, ALU.subtract, ALU.min)
                            if h < 3:
                                step(ins)
                        if c == 0:
                            step(ins)
                            ins = nc.vector.tensor_tensor(scol(120 + 4 * g, 4),
                                                          b[:, :].rearrange("p (h t) -> p h t", h=4)[:, :, P - 1],
                                                          scol(144 + 4 * g, 4), ALU.subtract)
                            step(ins)
                            settle()
                            dve.sem_inc(s_seg_ready, 1)
                        else:
                            step(ins)
                            settle()
                            dve.sem_inc(s_seg_ready, 1)
                    if c == 0:
                        dve.sem_inc(s_ds_pre, 1)
                dve.wait_ge(s_ds_exp, L + 1)
                nc.vector.tensor_tensor(dsx[:].rearrange("p (h q) -> p h q", h=8), xdt[:, 0, :].rearrange("p (h q) -> p h q", h=8),
                                        scol(128, 8).unsqueeze(2).to_broadcast([P, 8, SSD_P]), ALU.mult).then_inc(s_dsx_ready, 1)
                dve.wait_ge(s_cb_ready, L + 1)
                step(nc.vector.tensor_tensor(gm[:], bank[4][:, :].rearrange("p (a t) -> p a t", a=4),
                                             tri.unsqueeze(1).to_broadcast([P, 4, P]), ALU.mult))
                settle()
                dve.wait_ge(s_seg_exp, L + 1)
                for c in range(TP):
                    for g in range(2):
                        nc.vector.tensor_tensor(dec[:, c, 4 * g:4 * g + 4, :], dec[:, c, 4 * g:4 * g + 4, :],
                                                gm[:, 2 * c + g:2 * c + g + 1, :].to_broadcast([P, 4, P]),
                                                ALU.mult).then_inc(s_m_ready, 1)
                dve.wait_ge(s_ea_exp, 2 * (L + 1))
                for g in range(2):
                    nc.vector.tensor_tensor(cea[:, 4 * g:4 * g + 4, :], cea[:, 4 * g:4 * g + 4, :],
                                            xc[:, 6 + g:7 + g, P:T].to_broadcast([P, 4, P]), ALU.mult).then_inc(s_cea_ready, 1)
                dve.wait_ge(s_y_ready, L + 1)
                for k in range(4):
                    step(nc.vector.scalar_tensor_tensor(out=y_ssd[:, k, :], in0=xc[:, k, :],
                                                        scalar=par[:, C_DSK + k:C_DSK + k + 1],
                                                        in1=bank[6 + k // 2][:, (k % 2) * T:(k % 2) * T + T],
                                                        op0=ALU.mult, op1=ALU.add))
                settle()
                nc.vector.tensor_tensor(y_ssd, y_ssd, proj[:, T_Z:T_Z + 4, :], ALU.mult).then_inc(s_y_gated, 1)
                dve.wait_ge(s_y_gated, L + 1)
                dve.wait_ge(s_y_rstd, L + 1)
                nc.vector.tensor_tensor(y_ssd, y_ssd,
                                        gm[:, 2:4, :].rearrange("p a t -> p (a t)").unsqueeze(1).to_broadcast([P, 4, T]),
                                        ALU.mult).then_inc(s_y_normed, 1)
                dve.wait_ge(s_y_normed, L + 1)
                for k in range(4):
                    dve.wait_ge(s_y_hi, 4 * L + k + 1)
                    nc.vector.scalar_tensor_tensor(out=cat_lo[:, 8 + k, :], in0=y_ssd[:, k, :],
                                                   scalar=par[:, C_SSDG + k:C_SSDG + k + 1],
                                                   in1=cat_hi[:, 8 + k, :].bitcast(F32), op0=ALU.mult,
                                                   op1=ALU.subtract).then_inc(s_ssd_cat, 1)
                dve.wait_ge(s_ssd_cat, 4 * (L + 1))

                nc.vector.memset(attn[:], 0.0).then_inc(s_gl_zero, 1)
                dve.wait_ge(s_gl_pre, L + 1)
                for k in range(2):
                    step(nc.vector.tensor_scalar(g_raw[:, k * T:(k + 1) * T], bank[4][:, k * T:(k + 1) * T],
                                                 par[:, C_BGK + k:C_BGK + k + 1], None, ALU.add))
                settle()
                nc.vector.scalar_tensor_tensor(out=g_neg, in0=g_raw, scalar=-1.0, in1=g_raw,
                                               op0=ALU.mult, op1=ALU.min).then_inc(s_gl_neg, 1)
                dve.wait_ge(s_gl_log, L + 1)
                step(nc.vector.scalar_tensor_tensor(out=g_raw, in0=g_raw, scalar=0.0, in1=g_neg,
                                                    op0=ALU.min, op1=ALU.subtract))
                settle()
                nc.vector.tensor_tensor_scan(g_cum, keep, g_raw, 0.0, ALU.mult, ALU.add).then_inc(s_gl_scan, 1)
                dve.wait_ge(s_gl_scan, L + 1)
                for e in range(LEVELS):
                    half_ = GLA_CH >> (e + 1)
                    g_v = g_cum.rearrange("p (n b) -> p n b", b=2 * half_)
                    e_v = ebig[:, e, :].rearrange("p (n b) -> p n b", b=2 * half_)
                    n_ = 2 * T // (2 * half_)
                    ref = g_v[:, :, half_ - 1:half_].to_broadcast([P, n_, half_])
                    step(nc.vector.tensor_tensor(e_v[:, :, half_:], g_v[:, :, half_:], ref, ALU.subtract))
                    step(nc.vector.tensor_tensor(e_v[:, :, :half_], ref, g_v[:, :, :half_], ALU.subtract))
                g_v = g_cum.rearrange("p (n b) -> p n b", b=GLA_CH)
                step(nc.vector.tensor_tensor(ebig[:, 6, :].rearrange("p (n b) -> p n b", b=GLA_CH),
                                             g_v[:, :, GLA_CH - 1:GLA_CH].to_broadcast([P, 8, GLA_CH]), g_v, ALU.subtract))
                step(nc.vector.tensor_copy(ebig[:, 7, :], g_cum))
                settle()
                dve.sem_inc(s_gl_diff, 1)
                dve.wait_ge(s_gl_e, L + 1)
                dve.wait_ge(s_gl_qs, L + 1)
                step(nc.vector.tensor_copy(scol(176, 8).unsqueeze(2),
                                           ebig[:, 7, :].rearrange("p (n b) -> p n b", b=GLA_CH)[:, :, GLA_CH - 1:GLA_CH]))
                nc.vector.tensor_tensor(qall[:], ebig[:, 0:LEVELS, :], qs.unsqueeze(1).to_broadcast([P, LEVELS, 2 * T]),
                                        ALU.mult).then_inc(s_gl_q, 1)
                settle()
                dve.wait_ge(s_gl_q, 2 * L + 1)
                nc.vector.tensor_tensor(ebig[:, 7, :], ebig[:, 7, :], qs, ALU.mult).then_inc(s_gl_q, 1)
                nc.vector.tensor_tensor(ebig[:, 0:7, :], ebig[:, 0:7, :], ks.unsqueeze(1).to_broadcast([P, 7, 2 * T]),
                                        ALU.mult).then_inc(s_gl_k, 1)
                dve.wait_ge(s_gl_zero, L + 1)
                for e in range(LEVELS + 1):
                    which = ident.bitcast(mybir.dt.int32) if e == 0 else masks[:, (e - 1) * P:e * P]
                    for q in range(2):
                        dve.wait_ge(s_gl_lvl, 14 * L + 2 * e + q + 1)
                        if e:
                            dve.wait_ge(s_gl_put, 14 * L + 2 * e - 1 + q)
                        dve.sem_inc(s_passed_dve, 1)
                        nc.vector.copy_predicated(attn[:, q, :].rearrange("p (n t) -> p n t", n=4),
                                                  which.unsqueeze(1).to_broadcast([P, 4, P]),
                                                  bank[4 + 2 * (e % 2) + q][:, :].rearrange("p (n t) -> p n t", n=4)).then_inc(s_gl_put, 1)
                for c in range(3):
                    b = bank[6 + c % 2]
                    dve.wait_ge(s_gl_u, 3 * L + c + 1)
                    if c:
                        settle()
                    for hp in range(2):
                        for q in range(2):
                            rows = slice(64 * q, 64 * q + 64)
                            new = b[rows, hp * 256 + q * P:hp * 256 + q * P + P]
                            if c == 0:
                                step(nc.vector.tensor_copy(st_gla[rows, 0, hp, :], new))
                            else:
                                step(nc.vector.scalar_tensor_tensor(
                                    out=st_gla[rows, c, hp, :], in0=st_gla[rows, c - 1, hp, :],
                                    scalar=small[rows, 176 + 4 * hp + c:177 + 4 * hp + c], in1=new,
                                    op0=ALU.mult, op1=ALU.add))
                    if c == 0:
                        settle()
                        dve.sem_inc(s_gl_s, 1)
                settle()
                dve.sem_inc(s_gl_s, 1)
                dve.wait_ge(s_gl_orstd, L + 1)
                for q in range(2):
                    step(nc.vector.scalar_tensor_tensor(out=o_y[:, q, :], in0=bank[4 + q][:, :],
                                                        scalar=par[:, C_GLAG:C_GLAG + 1], in1=o_rstd[:, q, :],
                                                        op0=ALU.mult, op1=ALU.mult))
                settle()
                for q in range(2):
                    ins = nc.vector.tensor_tensor(
                        o_y[:, q, :].rearrange("p (h t) -> p h t", h=2), o_y[:, q, :].rearrange("p (h t) -> p h t", h=2),
                        proj[:, T_GR:T_GR + 4, :].rearrange("p (h q) t -> p q h t", q=2)[:, q], ALU.mult)
                    if q == 0:
                        step(ins)
                        settle()
                    else:
                        ins.then_inc(s_gl_y, 1)
                dve.wait_ge(s_gl_y, L + 1)
                dve.wait_ge(s_gl_hi, L + 1)
                nc.vector.tensor_tensor(cat_lo[:, 12:16, :].rearrange("p (h q) t -> p q h t", q=2),
                                        o_y.rearrange("p q (h t) -> p q h t", h=2),
                                        cat_hi[:, 12:16, :].rearrange("p (h q) t -> p q h t", q=2).bitcast(F32),
                                        ALU.subtract).then_inc(s_gl_cat, 1)

                dve.wait_ge(s_gl_cat, L + 1)
                dve.wait_ge(s_rope_swapped, 3 * L + 1)
                r2 = ropet[:].rearrange("p (a t) -> p a t", t=T)
                step(nc.vector.tensor_tensor(ropet[0:64, 0:T], bank[4][0:64, 0:T], sin[0:64, :], ALU.mult))
                step(nc.vector.tensor_tensor(kp[0:64, :], proj[0:64, T_MIX, :], cos[0:64, :], ALU.mult))
                settle()
                nc.vector.tensor_tensor(kp[0:64, :], kp[0:64, :], ropet[0:64, 0:T], ALU.add).then_inc(s_k_rope, 1)
                dve.wait_ge(s_rope_swapped, 3 * L + 3)
                dve.wait_ge(s_k_rope, L + 1)
                for b in range(2):
                    step(nc.vector.tensor_tensor(r2[:, 2 * b:2 * b + 2, :], bank[6 + b][:, :].rearrange("p (a t) -> p a t", a=2),
                                                 sin.unsqueeze(1).to_broadcast([P, 2, T]), ALU.mult))
                step(nc.vector.tensor_tensor(qp[:], qp[:], cos.unsqueeze(1).to_broadcast([P, 4, T]), ALU.mult))
                settle()
                nc.vector.tensor_tensor(qp[:], qp[:], r2, ALU.add).then_inc(s_q_rope, 1)

                def mask_and_max(h):
                    b = bank[4 + h % 2]
                    dve.wait_ge(s_scores_ready, 8 * L + h + 1)
                    step(nc.vector.tensor_tensor(prob[:, h, :], b[:, 0:3 * P], causal, ALU.add))
                    settle()
                    step(nc.vector.reduce_max(scol(208 + 2 * h), prob[:, h, 0:P], AX.X))
                    step(nc.vector.reduce_max(scol(209 + 2 * h), prob[:, h, P:3 * P], AX.X))
                    settle()
                    nc.vector.tensor_scalar(scol(192 + 2 * h, 2), scol(208 + 2 * h, 2), -SCALE, None, ALU.mult).then_inc(s_masked, 1)

                def normalise(h):
                    dve.wait_ge(s_prob_ready, 16 * L + 2 * h + 2)
                    step(nc.vector.reciprocal(scol(240 + 2 * h, 2), scol(224 + 2 * h, 2)))
                    settle()
                    step(nc.vector.tensor_scalar(prob[:, h, 0:P], prob[:, h, 0:P], scol(240 + 2 * h), None, ALU.mult))
                    settle()
                    nc.vector.tensor_scalar(prob[:, h, P:3 * P], prob[:, h, P:3 * P], scol(241 + 2 * h), None, ALU.mult).then_inc(s_prob_norm, 1)

                def split_out(h):
                    dve.wait_ge(s_o_hi, 8 * L + h + 1)
                    nc.vector.tensor_tensor(cat_lo[:, h, :], bank[7][:, 0:T], cat_hi[:, h, :].bitcast(F32),
                                            ALU.subtract).then_inc(s_o_lo, 1)

                for h in range(HEADS_MLA + 2):
                    if h < HEADS_MLA:
                        mask_and_max(h)
                    if 1 <= h <= HEADS_MLA:
                        normalise(h - 1)
                    if h >= 2:
                        split_out(h - 2)

                assert vec.n == VEC_STEPS, vec.n

                def residual(b, chunk, m, nth):
                    dve.wait_ge(s_chunks_used, n0 + chunk + 1 + SPLIT)
                    xt = x[:, bass.ds(m, 1), :].rearrange("p a t -> p (a t)")
                    return nc.vector.tensor_tensor(xt, xt, bank[b][:, 0:T], ALU.add)

                split_lo(q0 + Q_OUT, 0)
                split_lo(q0 + Q_OUT, 1)
                nc.vector.memset(ssq[:], 0.0).then_inc(s_ssq_zeroed, 1)
                dve.wait_ge(s_ssq_zeroed, 2 * L + 2)
                dve.sem_inc(s_passed_dve, 1)
                with dve.Fori(0, 4) as i:
                    for j in range(4):
                        m = i * 4 + j
                        split_lo(q0 + Q_OUT + i, j + 2)
                        residual(j, Q_OUT * 4 + i * 4 + j, m, 0).then_inc(bank_free[j], 1)
                        dve.wait_ge(bank_free[j], turn_of_expr(j, L, i + B_OUT) + 2)
                        dve.sem_inc(s_x_ready, 1)
                        refresh(m, KT + L * 2 * KT + m, par[:, bass.ds(m + C_FFN, 1)])

                dve.wait_ge(s_rstd_ready, 2 * L + 2)
                nc.vector.memset(ssq[:], 0.0).then_inc(s_ssq_zeroed, 1)
                for half in range(2):
                    def hidden(i, j, ahead):
                        f = j // 2
                        nth = L * FT + half * HALF + i * 2 + f
                        ft = half * HALF + i * 2 + f
                        split_lo(q0 + Q_GATE[half] + i, j + 2, ahead)
                        dve.wait_ge(s_chunks_used, n0 + Q_GATE[half] * 4 + i * 4 + j + 1 + SPLIT)
                        if j % 2 == 0:
                            nc.vector.tensor_tensor(gs[:, f, :], bank[j][:, 0:T], rstd[:], ALU.mult).then_inc(bank_free[j], 1)
                            dve.wait_ge(bank_free[j], turn_of_expr(j, L, i + B_GATE[half]) + 2)
                            for k in range(FTAPS):
                                tap = par[:, bass.ds(ft * FTAPS + (C_FW + FTAPS - 1 - k), 1)]
                                if k == 0:
                                    nc.vector.tensor_scalar(cv[:, f, :], gs[:, f, :], tap, par[:, bass.ds(ft + C_FB, 1)],
                                                            ALU.mult, ALU.add).then_inc(s_gate_step, 1)
                                else:
                                    dve.wait_ge(s_gate_step, nth * 2 + k)
                                    nc.vector.scalar_tensor_tensor(
                                        out=cv[:, f, k:T], in0=gs[:, f, 0:T - k], scalar=tap, in1=cv[:, f, k:T],
                                        op0=ALU.mult, op1=ALU.add).then_inc(s_gate_step if k < 2 else s_gate_ready, 1)
                        else:
                            nc.vector.tensor_tensor(us[:, f, :], bank[j][:, 0:T], rstd[:], ALU.mult).then_inc(bank_free[j], 1)
                            dve.wait_ge(bank_free[j], turn_of_expr(j, L, i + B_GATE[half]) + 2)
                            dve.wait_ge(s_gate_silu, nth + 1)
                            nc.vector.tensor_tensor(hv[:, f, :], us[:, f, :], sl[:, f, :], ALU.mult).then_inc(s_hid_ready, 1)
                        if j >= 2:
                            g = j - 2
                            dve.wait_ge(s_hid_hi_ready, L * FT + half * HALF + i * 2 + g + 1)
                            nc.vector.tensor_tensor(hid_lo[:, bass.ds(i * 2 + g, 1), :], hv[:, g:g + 1, :],
                                                    hid_hi[:, bass.ds(i * 2 + g, 1), :].bitcast(F32), ALU.subtract).then_inc(s_hid_split, 1)

                    dve.sem_inc(s_passed_dve, 1)
                    with dve.Fori(0, 10) as i:
                        for j in range(4):
                            hidden(i, j, CHUNK)
                    for j in range(4):
                        hidden(10, j, CHUNK if j < 2 else DOWN_CHUNK)
                    if half == 1:
                        dve.wait_ge(s_gate_ready, (L + 1) * FT)
                        dve.sem_inc(s_params_free, 1)
                        dve.wait_ge(s_ssq_zeroed, 2 * L + 3)

                    def down(i, jj, ahead):
                        if ahead:
                            split_lo(q0 + Q_DOWN[half] + i * 2, jj + 2, ahead)
                        if jj % 2 == 1:
                            b = jj // 2
                            m = i * 4 + b
                            residual(b, Q_DOWN[half] * 4 + i * 8 + jj, m, 0).then_inc(bank_free[b], 1)
                            if half == 1:
                                dve.wait_ge(bank_free[b], turn_of_expr(b, L, i + B_DOWN[half]) + 2)
                                dve.sem_inc(s_x_ready, 1)
                                refresh(m, KT + L * 2 * KT + KT + m, gains[:, bass.ds((L + 1) * KT + m, 1)])

                    dve.sem_inc(s_passed_dve, 1)
                    with dve.Fori(0, 3) as i:
                        for jj in range(8):
                            down(i, jj, DOWN_CHUNK)
                    for jj in range(8):
                        down(3, jj, DOWN_CHUNK if jj < 6 else (CHUNK if half == 0 else None))
                    if half == 0:
                        for b in range(4):
                            dve.wait_ge(bank_free[b], turn_of_expr(b, L, B_DOWN[0] + 4) + 1)

            dve.wait_ge(s_rstd_ready, 2 * DEPTH + 1)
            dve.sem_inc(s_passed_dve, 1)
            with dve.Fori(0, KT) as m:
                xt = x[:, bass.ds(m, 1), :].rearrange("p a t -> p (a t)")
                nc.vector.scalar_tensor_tensor(out=xt, in0=xt, scalar=gains[:, bass.ds(DEPTH * KT + m, 1)],
                                               in1=rstd[:], op0=ALU.mult, op1=ALU.mult).then_inc(s_final_ready, 1)

        @block.tensor
        def _(pe):
            pe.sem_inc(s_chunks_used, SPLIT)
            pe.wait_ge(s_consts_loaded, 32)

            def three(out, w, rhs_hi, rhs_lo, first, last, quiet=False):
                hi, lo = w
                nc.tensor.matmul(out, hi, rhs_hi, start=first, stop=False)
                nc.tensor.matmul(out, hi, rhs_lo, start=False, stop=False)
                return nc.tensor.matmul(out, lo, rhs_hi, start=False, stop=last)

            def chunk_ready(quad, j):
                pe.wait_ge(s_lo_ready, quad * 4 + (j + 1 + RAW))

            def unit(j, u, n=P):
                return w_hi[:, j % SPLIT, u * n:(u + 1) * n], w_lo[:, j % SPLIT, u * n:(u + 1) * n]

            def norm_sums(nth):
                pe.wait_ge(s_ssq_added, nth + 1)
                nc.tensor.matmul(bank[4][:, 0:T], ones, ssq[:], start=True, stop=True).then_inc(s_sums_ready, 1)

            with pe.Fori(0, DEPTH) as L:
                q0 = L * QUADS
                norm_sums(KT + L * 2 * KT)
                pe.wait_ge(s_h_ready, KT + L * 2 * KT)

                def wide_tile(quad, j, rhs_hi, rhs_lo, uses):
                    chunk_ready(quad, j)
                    pe.wait_ge(bank_free[j], uses + 1)
                    for k in range(KT):
                        last = three(bank[j][:, 0:T], unit(j, k), rhs_hi[:, k, :], rhs_lo[:, k, :], k == 0, k == KT - 1)
                    last.then_inc(s_chunks_used, 1)

                pe.sem_inc(s_passed_pe, 1)
                with pe.Fori(0, 7) as i:
                    for j in range(4):
                        wide_tile(q0 + i, j, h_hi, h_lo, turn_of_expr(j, L, i, 0))
                for j in range(3):
                    wide_tile(q0 + 7, j, h_hi, h_lo, turn_of(j, L, 7))

                pe.wait_ge(s_mla_sq, L + 1)
                for k in range(4):
                    nc.tensor.matmul(bank[5][:, 0:T], ones, qn[:, k, :], start=k == 0, stop=k == 3)
                for k in range(2):
                    last = nc.tensor.matmul(bank[5][:, T:2 * T], ones, qn[:, 4 + k, :], start=k == 0, stop=k == 1)
                last.then_inc(s_mla_sums, 1)
                pe.wait_ge(s_mla_split, 6 * (L + 1))
                for c in range(5):
                    j = (3 + c) % 4
                    chunk_ready(q0 + 7 + (3 + c) // 4, j)
                    for b in range(4):
                        pe.wait_ge(bank_free[b], turn_of(b, L, B_MLA + c) + 1)
                        if c < 3:
                            for k in range(4):
                                last = three(bank[b][:, 0:T], unit(j, 4 * b + k), cat_hi[:, k, :], cat_lo[:, k, :], k == 0, k == 3)
                        elif c == 3:
                            for a in range(2):
                                for k in range(2):
                                    last = three(bank[b][:, a * T:(a + 1) * T], unit(j, (2 * b + a) * 2 + k),
                                                 cat_hi[:, 4 + k, :], cat_lo[:, 4 + k, :], k == 0, k == 1)
                        else:
                            tp, part = b // 2, b % 2
                            at = slice(tp * P, tp * P + P)
                            for k in range(2):
                                w = unit(j, 2 * k + part, 512)
                                nc.tensor.matmul(bank[b][:, :], cat_hi[:, 4 + k, at], w[0], start=k == 0, stop=False)
                                nc.tensor.matmul(bank[b][:, :], cat_lo[:, 4 + k, at], w[0], start=False, stop=False)
                                last = nc.tensor.matmul(bank[b][:, :], cat_hi[:, 4 + k, at], w[1], start=False, stop=k == 1)
                    last.then_inc(s_chunks_used, 1)

                mix = proj[:, T_MIX, :]
                for c in range(TP):
                    last = nc.tensor.transpose(bank[4][:, 8 * c:8 * c + 8], mix[MIX_DT:MIX_DT + 8, c * P:(c + 1) * P],
                                               ident[MIX_DT:MIX_DT + 8, MIX_DT:MIX_DT + 8])
                last.then_inc(s_dt_t, 1)
                pe.wait_ge(s_silu_ready, 3 * L + 1)
                for c in range(TP):
                    for k in range(4):
                        last = nc.tensor.transpose(bank[5 + c][:, k * P:(k + 1) * P], xc[:, k, c * P:(c + 1) * P], ident)
                    last.then_inc(s_xs_t, 1)
                for g in range(2):
                    last = nc.tensor.transpose(bank[7][:, g * P:(g + 1) * P], xc[:, 4 + g, 0:P], ident)
                last.then_inc(s_xs_t, 1)
                pe.wait_ge(s_a_ready, L + 1)
                pe.wait_ge(s_btok_ready, L + 1)
                nc.tensor.matmul(bank[7][:, 256:272], tri, scol(96, 16), start=True, stop=True).then_inc(s_acum_ready, 1)
                pe.wait_ge(s_ta_ready, L + 1)
                pe.wait_ge(s_xdt_ready, 2 * (L + 1))
                pe.wait_ge(s_acum_copied, L + 1)
                for b in range(4):
                    nc.tensor.matmul(bank[4 + b][:, :], ones, ta[:, b * 512:(b + 1) * 512], start=True, stop=True).then_inc(s_cumb_ready, 1)
                pe.wait_ge(s_ds_pre, L + 1)
                for c in range(TP):
                    for g in range(2):
                        last = nc.tensor.matmul(bank[4][:, (2 * c + g) * P:(2 * c + g + 1) * P], xc[:, 4 + g, c * P:(c + 1) * P],
                                                xc[:, 6 + g, c * P:(c + 1) * P], start=True, stop=True)
                last.then_inc(s_cb_ready, 1)
                pe.wait_ge(s_dsx_ready, L + 1)
                for g in range(2):
                    last = nc.tensor.matmul(bank[5][:, g * 256:(g + 1) * 256], btok[:, g * P:(g + 1) * P],
                                            dsx[:, g * 256:(g + 1) * 256], start=True, stop=True)
                last.then_inc(s_state_ready, 1)
                pe.wait_ge(s_state_copied, L + 1)
                pe.wait_ge(s_m_ready, 4 * (L + 1))
                pe.wait_ge(s_cea_ready, 2 * (L + 1))
                for h in range(SSD_H):
                    rows = slice(64 * (h % 2), 64 * (h % 2) + 64)
                    for c in range(TP):
                        col = ((h // 2) % 2) * T + c * P
                        out = bank[6 + h // 4][rows, col:col + P]
                        last = nc.tensor.matmul(out, xdt[:, c, h * 64:(h + 1) * 64], dec[:, c, h, :], start=True, stop=c == 0)
                        if c == 1:
                            last = nc.tensor.matmul(out, sst[:, h * 64:(h + 1) * 64], cea[:, h, :], start=False, stop=True)
                last.then_inc(s_y_ready, 1)
                pe.wait_ge(s_y_sq, L + 1)
                for k in range(4):
                    last = nc.tensor.matmul(bank[4][:, 0:T], ones, sq_ssd[:, k, :], start=k == 0, stop=k == 3)
                last.then_inc(s_y_sums, 1)

                pe.wait_ge(s_y_rstd, L + 1)
                for k in range(2):
                    last = nc.tensor.matmul(bank[4][:, k * T:(k + 1) * T], par[MIX_GLOW:MIX_GLOW + 16, C_WGK + k * P:C_WGK + (k + 1) * P],
                                            mix[MIX_GLOW:MIX_GLOW + 16, :], start=True, stop=True)
                last.then_inc(s_gl_pre, 1)
                pe.wait_ge(s_ssd_cat, 4 * (L + 1))
                for c in range(TP):
                    for k in range(4):
                        last = nc.tensor.transpose(bank[5 + c][:, k * P:(k + 1) * P], proj[:, T_GV + k, c * P:(c + 1) * P], ident)
                last.then_inc(s_gl_v, 1)
                pe.wait_ge(s_gl_k, L + 1)
                for c in range(TP):
                    for hp in range(2):
                        last = nc.tensor.transpose(bank[4][:, (2 * c + hp) * P:(2 * c + hp + 1) * P],
                                                   ebig[:, 6, hp * T + c * P:hp * T + (c + 1) * P], ident)
                last.then_inc(s_gl_kt, 1)
                pe.wait_ge(s_gl_ktc, L + 1)
                pe.wait_ge(s_gl_vcopied, 2 * (L + 1))
                for e in range(LEVELS + 1):
                    for q in range(2):
                        if e >= 2:
                            pe.wait_ge(s_gl_put, 14 * L + 2 * (e - 2) + q + 1)
                        for hp in range(2):
                            for c in range(TP):
                                at = slice(hp * T + c * P, hp * T + (c + 1) * P)
                                rows = slice(64 * q, 64 * q + 64)
                                k_, q_ = (ks, qs) if e == 0 else (ebig[:, e - 1, :], qall[:, e - 1, :])
                                last = nc.tensor.matmul(bank[4 + 2 * (e % 2) + q][:, (2 * hp + c) * P:(2 * hp + c + 1) * P],
                                                        k_[rows, at], q_[rows, at], start=True, stop=True)
                        last.then_inc(s_gl_lvl, 1)
                for c in range(3):
                    pe.wait_ge(s_gl_put, 14 * (L + 1))
                    if c == 2:
                        pe.wait_ge(s_gl_s, 2 * L + 1)
                    rows = slice((c % 2) * 64, (c % 2) * 64 + 64)
                    for hp in range(2):
                        last = nc.tensor.matmul(bank[6 + c % 2][:, hp * 256:(hp + 1) * 256], kd_t[rows, c // 2, hp, :],
                                                v_gla[rows, c // 2, hp * 256:(hp + 1) * 256], start=True, stop=True)
                    last.then_inc(s_gl_u, 1)
                pe.wait_ge(s_gl_s, 2 * (L + 1))
                for q in range(2):
                    for hp in range(2):
                        head = 2 * hp + q
                        for c in range(TP):
                            out = bank[4 + q][:, hp * T + c * P:hp * T + (c + 1) * P]
                            nc.tensor.matmul(out, v_gla[:, c, head * P:(head + 1) * P],
                                             attn[:, q, (2 * hp + c) * P:(2 * hp + c + 1) * P], start=True, stop=False)
                            rows = slice(64 * q, 64 * q + 64)
                            for s in range(2):
                                n = 2 * c + s
                                if n == 0:
                                    continue
                                at = slice(hp * T + n * 64, hp * T + (n + 1) * 64)
                                last = nc.tensor.matmul(bank[4 + q][:, at], st_gla[rows, n - 1, hp, :], ebig[rows, 7, at],
                                                        start=False, stop=s == 1)
                last.then_inc(s_gl_o, 1)
                pe.wait_ge(s_gl_osq, 2 * (L + 1))
                for q in range(2):
                    last = nc.tensor.matmul(bank[6 + q][:, :], ones, o_sq[:, q, :], start=True, stop=True)
                last.then_inc(s_gl_osum, 1)

                pe.wait_ge(s_mla_evac, 2 * (L + 1))
                pe.wait_ge(s_mla_evac2, L + 1)
                pe.wait_ge(s_gl_y, L + 1)
                nc.tensor.matmul(bank[4][:, 0:T], swap[0:64, :], mix[0:64, :], start=True, stop=True).then_inc(s_rope_swapped, 1)
                for b in range(2):
                    for k in range(2):
                        last = nc.tensor.matmul(bank[6 + b][:, k * T:(k + 1) * T], swap, qp[:, 2 * b + k, :], start=True, stop=True)
                    last.then_inc(s_rope_swapped, 1)
                pe.wait_ge(s_k_dup, L + 1)
                pe.wait_ge(s_q_rope, L + 1)

                def scores(h):
                    b = bank[4 + h % 2]
                    if h >= 2:
                        pe.wait_ge(s_masked, 8 * L + h - 1)
                    rows = slice(64 * (h % 2), 64 * (h % 2) + 64)
                    nc.tensor.matmul(b[:, 0:P], qn[:, h, 0:P], kn[:, h, 0:P], start=True, stop=False)
                    nc.tensor.matmul(b[:, 0:P], qp[rows, h // 2, 0:P], kp[rows, 0:P], start=False, stop=True)
                    nc.tensor.matmul(b[:, P:3 * P], qn[:, h, P:T], kn[:, h, :], start=True, stop=False)
                    nc.tensor.matmul(b[:, P:3 * P], qp[rows, h // 2, P:T], kp[rows, :], start=False, stop=True).then_inc(s_scores_ready, 1)

                def transpose_weights(h):
                    pe.wait_ge(s_prob_norm, 8 * L + h + 1)
                    if h >= 1:
                        pe.wait_ge(s_probt_copied, 8 * L + h)
                    for k in range(3):
                        last = nc.tensor.transpose(bank[6][:, k * P:(k + 1) * P], prob[:, h, k * P:(k + 1) * P], ident)
                    last.then_inc(s_probt_ready, 1)

                def weighted(h):
                    pe.wait_ge(s_probt_copied, 8 * L + h + 1)
                    if h >= 1:
                        pe.wait_ge(s_o_lo, 8 * L + h)
                    pt, v = probt[:, h % 2, :], vv[:, :, h * P:(h + 1) * P]
                    nc.tensor.matmul(bank[7][:, 0:P], v[:, 0, :], pt[:, 0:P], start=True, stop=True)
                    nc.tensor.matmul(bank[7][:, P:T], v[:, 0, :], pt[:, P:2 * P], start=True, stop=False)
                    nc.tensor.matmul(bank[7][:, P:T], v[:, 1, :], pt[:, 2 * P:3 * P], start=False, stop=True).then_inc(s_o_ready, 1)

                scores(0)
                for h in range(HEADS_MLA + 1):
                    if h + 1 < HEADS_MLA:
                        scores(h + 1)
                    if h < HEADS_MLA:
                        transpose_weights(h)
                    if h >= 1:
                        weighted(h - 1)

                pe.wait_ge(s_o_lo, 8 * (L + 1))
                pe.wait_ge(s_gl_cat, L + 1)
                pe.sem_inc(s_passed_pe, 1)
                with pe.Fori(0, 4) as i:
                    for j in range(4):
                        wide_tile(q0 + Q_OUT + i, j, cat_hi, cat_lo, turn_of_expr(j, L, i + B_OUT))
                norm_sums(KT + L * 2 * KT + KT)
                pe.wait_ge(s_h_ready, KT + L * 2 * KT + KT)

                for half in range(2):
                    pe.sem_inc(s_passed_pe, 1)
                    with pe.Fori(0, 11) as i:
                        for j in range(4):
                            wide_tile(q0 + Q_GATE[half] + i, j, h_hi, h_lo, turn_of_expr(j, L, i + B_GATE[half]))
                    pe.wait_ge(s_hid_split, L * FT + (half + 1) * HALF)
                    pe.sem_inc(s_passed_pe, 1)
                    with pe.Fori(0, 4) as i:
                        for jj in range(8):
                            b, part, j = jj // 2, jj % 2, jj % 4
                            chunk_ready(q0 + Q_DOWN[half] + i * 2, jj)
                            if part == 0:
                                pe.wait_ge(bank_free[b], turn_of_expr(b, L, i + B_DOWN[half]) + 1)
                            for k in range(DOWN_KT):
                                kt = part * DOWN_KT + k
                                last = three(bank[b][:, 0:T], unit(j, k), hid_hi[:, kt, :], hid_lo[:, kt, :],
                                             kt == 0, kt == HALF - 1)
                            last.then_inc(s_chunks_used, 1)
            norm_sums(KT + DEPTH * 2 * KT)


VEC_STEPS = 103


def turn_of_expr(b, layer, turn, after=1):
    if b == 3:
        return layer * (TURNS - 1) + turn - after
    return layer * TURNS + turn


def _tiles(w, kt):
    k, m = w.shape
    return w.reshape(kt, P, m // P, P).transpose(2, 1, 0, 3).reshape(m // P, P, kt * P)


def _cols(v):
    return v.reshape(-1, P).T


def kernel(**inputs):
    import concourse.bacc as _bacc
    from concourse.bass_utils import run_bass_kernel_spmd as _run

    a = {k: np.asarray(v) for k, v in inputs.items()}
    f = np.float32
    order = []
    at = lambda s, n: order.extend(range(s, s + n))
    at(1344, 1024); at(832, 512); at(0, 512); at(512, 256); at(2376, 256); at(2632, 256); at(2888, 512); at(3416, 512)
    front, outw, gate, down, params = [], [], [], [], []
    for l in range(DEPTH):
        w = a["w_in"][l]
        mix = np.zeros((D, P), f)
        mix[:, 0:64] = w[:, 768:832]
        mix[:, MIX_GLOW:MIX_GLOW + 16] = w[:, 3400:3416]
        mix[:, MIX_DT:MIX_DT + 8] = w[:, 2368:2376]
        front.append(_tiles(np.concatenate([w[:, order], mix], 1), KT))
        uq = a["mla_w_uq"][l].reshape(512, 8, 192)
        uq = np.concatenate([uq[:, :, :128].reshape(512, 1024), uq[:, :, 128:].reshape(512, 512)], 1)
        front.append(_tiles(uq, 4).reshape(3, 4, P, 512).transpose(0, 2, 1, 3).reshape(3, P, CHUNK))
        ukv = a["mla_w_ukv"][l].reshape(256, 8, 256)
        front.append(_tiles(np.ascontiguousarray(ukv[:, :, :128]).reshape(256, 1024), 2).transpose(1, 0, 2).reshape(1, P, CHUNK))
        front.append(np.ascontiguousarray(ukv[:, :, 128:]).reshape(2, P, 1024).transpose(1, 0, 2).reshape(1, P, CHUNK))
        outw.append(_tiles(a["w_out"][l], KT))
        g, u = _tiles(a["ffn_w_gate"][l], KT), _tiles(a["ffn_w_up"][l], KT)
        gate.append(np.stack([g, u], 1).reshape(2 * FT, P, CHUNK))
        dn = a["ffn_w_down"][l].reshape(2, 2, DOWN_KT, P, KT, P)
        down.append(dn.transpose(0, 4, 1, 3, 2, 5).reshape(64, P, DOWN_CHUNK))
        p = np.zeros((P, NPAR), f)
        p[:, C_ATTN:C_ATTN + 16] = _cols(a["attn_norm"][l])
        p[:, C_FFN:C_FFN + 16] = _cols(a["ffn_norm"][l])
        p[:, C_QG:C_QG + 4] = _cols(a["mla_q_norm"][l])
        p[:, C_KVG:C_KVG + 2] = _cols(a["mla_kv_norm"][l])
        p[:, C_SSDG:C_SSDG + 4] = _cols(a["ssd_norm"][l])
        p[:, C_DSK:C_DSK + 4] = _cols(np.repeat(a["ssd_d"][l], SSD_P))
        p[:, C_GLAG] = a["gla_norm"][l]
        p[:, C_BGK:C_BGK + 2] = _cols(a["gla_b_gk"][l])
        p[:, C_DTB:C_DTB + 8] = a["ssd_dt_bias"][l][None]
        p[:, C_ALOG:C_ALOG + 8] = a["ssd_a_log"][l][None]
        p[:, C_CONV:C_CONV + 32] = a["ssd_conv_w"][l].reshape(4, 8, P).transpose(2, 1, 0).reshape(P, 32)
        p[:, C_CONVB:C_CONVB + 8] = _cols(a["ssd_conv_b"][l])
        p[:, C_FW:C_FW + 132] = a["ffn_dw_w"][l].reshape(3, FT, P).transpose(2, 1, 0).reshape(P, 132)
        p[:, C_FB:C_FB + 44] = _cols(a["ffn_dw_b"][l])
        p[MIX_GLOW:MIX_GLOW + 16, C_WGK:C_WGK + 256] = a["gla_w_gk"][l]
        params.append(p)

    consts = np.zeros((P, NCONST), f)
    i = np.arange(P)
    consts[:, K_ID:K_ID + P] = np.eye(P)
    consts[:, K_ONES:K_ONES + P] = 1
    consts[i, K_SWAP + (i ^ 32)] = 1
    consts[:, K_TRI:K_TRI + P] = i[:, None] <= i[None]
    freq = f(10000.0) ** (-np.arange(0, ROPE, 2, dtype=f) / f(ROPE))
    ang = np.arange(T, dtype=f)[:, None] * freq[None]
    consts[:, K_COS:K_COS + T] = np.cos(ang).T[i % 32]
    consts[:, K_SIN:K_SIN + T] = np.sin(ang).T[i % 32] * np.where(i % 64 < 32, -1, 1)[:, None]
    hide = np.where(i[None] <= i[:, None], 0, -1e30)
    consts[:, K_MASK:K_MASK + P] = hide
    consts[:, K_MASK + 2 * P:K_MASK + 3 * P] = hide
    masks = np.zeros((P, LEVELS * P + 2 * T), f)
    for e in range(LEVELS):
        b = GLA_CH >> (e + 1)
        masks[:, e * P:(e + 1) * P] = ((i[:, None] // (2 * b) == i[None] // (2 * b))
                                       & (i[:, None] % (2 * b) < b) & (i[None] % (2 * b) >= b))
    masks[:, LEVELS * P:] = np.arange(2 * T) % GLA_CH != 0

    gains = np.concatenate([_cols(a["attn_norm"][l]) for l in range(DEPTH)] + [_cols(a["final_norm"])], 1)
    arrays = {
        "x_in": a["x"][0].T.reshape(KT, P, T).transpose(1, 0, 2),
        "gains_in": gains,
        "params_in": np.stack(params),
        "consts_in": consts,
        "masks_in": masks,
        "front_in": np.concatenate(front),
        "out_in": np.concatenate(outw),
        "gate_in": np.concatenate(gate),
        "down_in": np.concatenate(down),
    }
    arrays = {k: np.ascontiguousarray(v) for k, v in arrays.items()}
    nc = _bacc.Bacc("TRN2", target_bir_lowering=False, num_devices=1)
    args = [nc.dram_tensor(k, v.shape, mybir.dt.from_np(v.dtype), kind="ExternalInput").ap() for k, v in arrays.items()]
    args.append(nc.dram_tensor("y_out", (P, KT, T), F32, kind="ExternalOutput").ap())
    build(nc, *args)
    r = _run(nc, [arrays], core_ids=[0])
    y = r.results[0]["y_out"]
    return y.transpose(1, 0, 2).reshape(D, T).T.reshape(1, T, D)
```

```python
import numpy as np
import concourse.bass as bass
from concourse import mybir
from contextlib import ExitStack

F32 = mybir.dt.float32
F32R = mybir.dt.float32r
U8 = mybir.dt.uint8
ALU = mybir.AluOpType
ACT = mybir.ActivationFunctionType
AX = mybir.AxisListType

P = 128
D = 2048
T = 256
DEPTH = 2
EPS = 1e-6
KT = D // P
TP = T // P
HEADS_MLA, ROPE = 8, 64
SCALE = float((128 + 64) ** -0.5)
SSD_H, SSD_P, SSD_TAPS, XBC = 8, 64, 4, 8
GLA_CH = 64
GLA_TAU = 16.0
LEVELS = 6
FT = 44
HALF = FT // 2
FTAPS = 3

T_XBC, T_Z, T_CQ, T_CKV, T_GQ, T_GK, T_GV, T_GR, T_MIX = 0, 8, 12, 16, 18, 20, 22, 26, 30
IN_ORDER = [T_MIX, *range(T_XBC, T_XBC + 8), *range(T_GV, T_GV + 4), *range(T_GQ, T_GQ + 2), *range(T_GK, T_GK + 2),
            *range(T_CQ, T_CQ + 4), *range(T_CKV, T_CKV + 2), *range(T_Z, T_Z + 4), *range(T_GR, T_GR + 4)]
IN_TILES = 31
MIX_GLOW, MIX_DT = 64, 96

CHUNK = 16 * P
DOWN_KT = 11
DOWN_CHUNK = DOWN_KT * P
RAW, SPLIT = 2, 2

PIECES = 2
OFFSET = CHUNK // PIECES
WIDE = (CHUNK // 2, CHUNK // 2)
DOWN_KTS = (6, 5)
NARROW = (DOWN_KTS[0] * P, DOWN_KTS[1] * P)

N_MLA, N_OUT, N_OUT_MLA, CHUNKS = 31, 36, 44, 204
QUADS = CHUNKS // 4
Q_GATE = (13, 32)
Q_DOWN = (24, 43)


def _turns():
    n, use = [0, 0, 0, 0], {}

    def turn(b, *key):
        use[key] = n[b]
        n[b] += 1

    for c in range(N_MLA):
        turn(c % 2, "in", c)
    for c in range(5):
        for r in range(1 if c < 3 else 2):
            for b in range(2):
                turn(b, "mla", c, r, b)
    for k in range(2 * KT):
        turn(k % 2, "out", k)
    for half in range(2):
        for b in range(4):
            use["gate", half, b] = n[b]
            n[b] += HALF // 2
            use["down", half, b] = n[b]
            n[b] += KT // 4
    return use, n


TURN, TURNS = _turns()

C_UNUSED, C_FFN, C_QG, C_KVG, C_SSDG, C_DSK, C_GLAG, C_BGK = 0, 16, 32, 36, 38, 42, 46, 47
C_DTB, C_ALOG, C_CONV, C_CONVB, C_FW, C_FB, C_WGK = 49, 57, 65, 97, 105, 237, 281
NPAR = C_WGK + 256

K_ID, K_ONES, K_SWAP, K_TRI, K_COS, K_SIN, K_MASK = 0, 128, 256, 384, 512, 768, 1024
NCONST = K_MASK + 384


def build(nc, x_in, gains_in, params_in, consts_in, masks_in, front_in, out_in, gate_in, down_in, y_out):
    ctx = ExitStack()
    with ctx:
        def sb(name, shape, dt=F32, where=ctx):
            return where.enter_context(nc.sbuf_tensor(name, shape, dt))

        x = sb("x", [P, KT, T])
        raw = sb("raw", [P, RAW, CHUNK])
        w_hi = sb("w_hi", [P, SPLIT, CHUNK], F32R)
        w_lo = sb("w_lo", [P, SPLIT, CHUNK], F32R)
        par = sb("par", [P, NPAR])
        const = sb("const", [P, NCONST])
        gains = sb("gains", [P, (DEPTH + 1) * KT])
        masks = sb("masks", [P, LEVELS * P + 2 * T], U8)
        ssq = sb("ssq", [P, T])
        sqt = sb("sqt", [P, T])
        rstd = sb("rstd", [P, T])
        eps = sb("eps", [P, 1])
        small = sb("small", [P, 256])
        catb_hi = sb("catb_hi", [P, 8, T], F32R)
        catb_lo = sb("catb_lo", [P, 8, T], F32R)

        with ExitStack() as first:
            cata_hi = sb("cata_hi", [P, 8, T], F32R, first)
            cata_lo = sb("cata_lo", [P, 8, T], F32R, first)
        with ExitStack() as second:
            dec = sb("dec", [P, TP, SSD_H, P], F32, second)
            xdt = sb("xdt", [P, TP, SSD_H * SSD_P], F32, second)
            cea = sb("cea", [P, SSD_H, P], F32, second)
        sb("cata_region", [P, 16 * T])

        with ExitStack() as first:
            h_hi = sb("h_hi", [P, KT, T], F32R, first)
            h_lo = sb("h_lo", [P, KT, T], F32R, first)
        with ExitStack() as second:
            qn = sb("qn", [P, HEADS_MLA, T], F32, second)
            kn = sb("kn", [P, HEADS_MLA, T], F32, second)
            vv = sb("vv", [P, TP, HEADS_MLA * P], F32, second)
            qp = sb("qp", [P, HEADS_MLA // 2, T], F32, second)
            probt = sb("probt", [P, 2, 3 * P], F32, second)
        sb("h_region", [P, 2 * KT * T])

        with ExitStack() as first:
            proj = sb("proj", [P, IN_TILES, T], F32, first)
            with ExitStack() as mixers:
                xc = sb("xc", [P, XBC, T], F32, mixers)
                e3 = sb("e3", [P, 3, 2 * T], F32, mixers)
                q3 = sb("q3", [P, 3, 2 * T], F32, mixers)
                kq = sb("kq", [P, 2, 2 * T], F32, mixers)
                attn = sb("attn", [P, 2, 4 * P], F32, mixers)
                gm = sb("gm", [P, 4, P], F32, mixers)
                dsx = sb("dsx", [P, SSD_H * SSD_P], F32, mixers)
            with ExitStack() as start:
                x_g = sb("x_g", [P, KT, T], F32, start)
                x_sq = sb("x_sq", [P, KT, T], F32, start)
        with ExitStack() as second:
            hid_hi = sb("hid_hi", [P, HALF, T], F32R, second)
            hid_lo = sb("hid_lo", [P, HALF, T], F32R, second)
            gs = sb("gs", [P, 2, T], F32, second)
            cv = sb("cv", [P, 2, T], F32, second)
            sl = sb("sl", [P, 2, T], F32, second)
            us = sb("us", [P, 2, T], F32, second)
            hv = sb("hv", [P, 2, T], F32, second)

        ident = const[:, K_ID:K_ID + P]
        ones = const[:, K_ONES:K_ONES + P]
        swap = const[:, K_SWAP:K_SWAP + P]
        tri = const[:, K_TRI:K_TRI + P]
        cos = const[:, K_COS:K_COS + T]
        sin = const[:, K_SIN:K_SIN + T]
        causal = const[:, K_MASK:K_MASK + 3 * P]
        keep = masks[:, LEVELS * P:LEVELS * P + 2 * T]
        bank = [ctx.enter_context(nc.psum_tensor(f"bank{i}", [P, 512], F32)) for i in range(8)]

        def scol(i, n=1):
            return small[:, i:i + n]

        def flat(ap):
            return ap.rearrange("p a t -> p (a t)")

        ta = flat(proj[:, T_XBC:T_XBC + 8, :])
        y_ssd = proj[:, T_XBC:T_XBC + 4, :]
        st_gla = flat(proj[:, T_XBC + 4:T_XBC + 7, :]).rearrange("p (c h n) -> p c h n", c=3, h=2)
        prob = flat(proj[:, T_XBC:T_XBC + 6, :]).rearrange("p (a n) -> p a n", n=3 * P)
        sst = flat(proj[:, T_Z:T_Z + 2, :])
        btok = proj[:, T_Z + 2, :]
        z = proj[:, T_Z:T_Z + 4, :]
        g_cum = flat(proj[:, T_GR:T_GR + 2, :])
        v_gla = flat(proj[:, T_GV:T_GV + 4, :]).rearrange("p (b n) -> p b n", b=TP)
        qs = flat(proj[:, T_GQ:T_GQ + 2, :])
        ks = flat(proj[:, T_GK:T_GK + 2, :])
        kp = proj[:, T_CQ, :]
        ropet = proj[:, T_CQ + 1:T_CQ + 5, :]
        lat_sq = xc[:, 0:6, :]
        lat_rstd = xc[:, 6:8, :]
        kd_t = gm[:].rearrange("p (b h) n -> p b h n", b=TP)
        g_raw, g_neg = e3[:, 0, :], e3[:, 1, :]
        sum_rstd = dsx[:, 0:T]
        o_sq = e3[:].rearrange("p a t -> p (a t)")[:, 0:1024].rearrange("p (a t) -> p a t", a=2)
        o_rstd = q3[:].rearrange("p a t -> p (a t)")[:, 0:1024].rearrange("p (a t) -> p a t", a=2)
        o_y = attn

        def sem(name):
            return ctx.enter_context(nc.semaphore(name))

        s_x_loaded = [sem("x_loaded0"), sem("x_loaded1")]
        s_consts_loaded = sem("consts_loaded")
        s_masks_set = sem("masks_set")
        s_params_loaded = sem("params_loaded")
        s_params_free = sem("params_free")
        s_y_stored = sem("y_stored")
        s_eps_set = sem("eps_set")
        s_hi_ready = sem("hi_ready")
        s_lo_ready = sem("lo_ready")
        s_pieces_used = sem("pieces_used")
        s_x_ready = sem("x_ready")
        s_h_hi_ready = sem("h_hi_ready")
        s_h_ready = sem("h_ready")
        s_sq_ready = sem("sq_ready")
        s_ssq_added = sem("ssq_added")
        s_sums_ready = sem("sums_ready")
        s_rstd_log = sem("rstd_log")
        s_rstd_ready = sem("rstd_ready")
        s_conv_step = sem("conv_step")
        s_conv_ready = sem("conv_ready")
        s_silu_ready = sem("silu_ready")
        s_gate_step = sem("gate_step")
        s_gate_ready = sem("gate_ready")
        s_gate_silu = sem("gate_silu")
        s_hid_ready = sem("hid_ready")
        s_hid_hi_ready = sem("hid_hi_ready")
        s_hid_split = sem("hid_split")
        s_mla_sq = sem("mla_sq")
        s_mla_sums = sem("mla_sums")
        s_mla_log = sem("mla_log")
        s_mla_rstd = sem("mla_rstd")
        s_mla_normed = sem("mla_normed")
        s_mla_hi = sem("mla_hi")
        s_mla_split = sem("mla_split")
        s_rope_swapped = sem("rope_swapped")
        s_k_rope = sem("k_rope")
        s_k_dup = sem("k_dup")
        s_q_rope = sem("q_rope")
        s_scores_ready = sem("scores_ready")
        s_masked = sem("masked")
        s_prob_ready = sem("prob_ready")
        s_prob_norm = sem("prob_norm")
        s_probt_ready = sem("probt_ready")
        s_probt_copied = sem("probt_copied")
        s_o_ready = sem("o_ready")
        s_o_hi = sem("o_hi")
        s_o_lo = sem("o_lo")
        s_dt_t = sem("dt_t")
        s_xs_t = sem("xs_t")
        s_dt_abs = sem("dt_abs")
        s_dt_exp = sem("dt_exp")
        s_dt_log = sem("dt_log")
        s_neg_a = sem("neg_a")
        s_a_ready = sem("a_ready")
        s_xdt_ready = sem("xdt_ready")
        s_btok_ready = sem("btok_ready")
        s_ta_ready = sem("ta_ready")
        s_acum_ready = sem("acum_ready")
        s_acum_copied = sem("acum_copied")
        s_cumb_ready = sem("cumb_ready")
        s_seg_ready = sem("seg_ready")
        s_seg_exp = sem("seg_exp")
        s_ea_exp = sem("ea_exp")
        s_ds_exp = sem("ds_exp")
        s_cb_ready = sem("cb_ready")
        s_m_ready = sem("m_ready")
        s_cea_ready = sem("cea_ready")
        s_dsx_ready = sem("dsx_ready")
        s_state_ready = sem("state_ready")
        s_state_copied = sem("state_copied")
        s_y_ready = sem("y_ready")
        s_y_gated = sem("y_gated")
        s_y_sq = sem("y_sq")
        s_y_sums = sem("y_sums")
        s_y_log = sem("y_log")
        s_y_rstd = sem("y_rstd")
        s_y_normed = sem("y_normed")
        s_y_hi = sem("y_hi")
        s_ssd_cat = sem("ssd_cat")
        s_vec_step = sem("vec_step")
        s_gl_pre = sem("gl_pre")
        s_gl_v = sem("gl_v")
        s_gl_neg = sem("gl_neg")
        s_gl_exp = sem("gl_exp")
        s_gl_log = sem("gl_log")
        s_gl_diff = sem("gl_diff")
        s_gl_e = sem("gl_e")
        s_gl_qs = sem("gl_qs")
        s_gl_vcopied = sem("gl_vcopied")
        s_gl_q = sem("gl_q")
        s_gl_k = sem("gl_k")
        s_gl_kt = sem("gl_kt")
        s_gl_ktc = sem("gl_ktc")
        s_gl_zero = sem("gl_zero")
        s_gl_lvl = sem("gl_lvl")
        s_gl_put = sem("gl_put")
        s_gl_u = sem("gl_u")
        s_gl_s = sem("gl_s")
        s_gl_o = sem("gl_o")
        s_gl_osq = sem("gl_osq")
        s_gl_osum = sem("gl_osum")
        s_gl_olog = sem("gl_olog")
        s_gl_orstd = sem("gl_orstd")
        s_gl_y = sem("gl_y")
        s_gl_hi = sem("gl_hi")
        s_gl_cat = sem("gl_cat")
        s_gl_scan = sem("gl_scan")
        s_final_ready = sem("final_ready")
        s_passed_act = sem("passed_act")
        s_passed_dve = sem("passed_dve")
        s_passed_pe = sem("passed_pe")
        s_gains_loaded = sem("gains_loaded")
        s_start_sq = sem("start_sq")
        s_start_xg = sem("start_xg")
        s_start_hi = sem("start_hi")
        s_start_lo = sem("start_lo")
        s_in_taken = sem("in_taken")
        s_y_skip = sem("y_skip")
        s_gl_kq = sem("gl_kq")
        s_gl_kqd = sem("gl_kqd")
        s_gl_kd = sem("gl_kd")
        s_gl_qe = sem("gl_qe")
        s_ssq_zeroed = sem("ssq_zeroed")
        raw_landed = [sem(f"raw_landed{i}") for i in range(RAW)]
        bank_free = [sem(f"bank_free{i}") for i in range(4)]

        def mla_evac(engine, on_act, L, c0, c, piece):
            by_act = {0: False, 1: True, 2: True, 3: piece == 0, 4: piece == 1}[c]
            if on_act != by_act:
                return
            copy = nc.scalar.copy if on_act else nc.vector.tensor_copy
            engine.wait_ge(s_pieces_used, (c0 + N_MLA + c) * PIECES + (piece + 1 + SPLIT * PIECES))
            for b in (range(2) if c >= 3 else [piece]):
                source, two = bank[b][:, :], bank[b][:, :].rearrange("p (a t) -> p a t", a=2)
                if c == 0:
                    copy(qp[:, 2 * b:2 * b + 2, :], two).then_inc(bank_free[b], 1)
                elif c < 3:
                    copy(qn[:, 4 * (c - 1) + 2 * b:4 * (c - 1) + 2 * b + 2, :], two).then_inc(bank_free[b], 1)
                elif c == 3:
                    copy(kn[:, 4 * piece + 2 * b:4 * piece + 2 * b + 2, :], two).then_inc(bank_free[b], 1)
                else:
                    copy(vv[:, b, piece * 512:piece * 512 + 512], source).then_inc(bank_free[b], 1)

        block = ctx.enter_context(nc.Block())

        @block.sync
        def _(sp):
            sp.dma_start(gains[:], gains_in).then_inc(s_gains_loaded, 16)
            for k in range(2):
                sp.dma_start(x[:, 8 * k:8 * k + 8, :], x_in[:, 8 * k:8 * k + 8, :]).then_inc(s_x_loaded[k], 16)

            def load(source, row, chunk, j, width=CHUNK):
                sp.wait_ge(s_lo_ready, chunk * PIECES + PIECES)
                sp.dma_start(raw[:, j % RAW, 0:width],
                             source[bass.ds(row, 1), :, :].rearrange("a p n -> p (a n)")).then_inc(raw_landed[j % RAW], 16)

            with sp.Fori(0, DEPTH) as L:
                c0 = L * CHUNKS
                with sp.Fori(0, 9) as i:
                    for j in range(4):
                        load(front_in, L * 36 + i * 4 + j, c0 + i * 4 + j, j)
                with sp.Fori(0, 4) as i:
                    for j in range(4):
                        load(out_in, L * 16 + i * 4 + j, c0 + N_OUT + i * 4 + j, j)
                for half in range(2):
                    with sp.Fori(0, 11) as i:
                        for j in range(4):
                            load(gate_in, L * 88 + half * 44 + i * 4 + j, c0 + Q_GATE[half] * 4 + i * 4 + j, j)
                    with sp.Fori(0, 8) as i:
                        for j in range(4):
                            load(down_in, L * 64 + half * 32 + i * 4 + j, c0 + Q_DOWN[half] * 4 + i * 4 + j, j, DOWN_CHUNK)
            for k in range(4):
                sp.wait_ge(s_final_ready, 4 * k + 4)
                sp.dma_start(y_out[:, 4 * k:4 * k + 4, :], x[:, 4 * k:4 * k + 4, :]).then_inc(s_y_stored, 16)
            sp.wait_ge(s_y_stored, 64)

        @block.gpsimd
        def _(pool):
            pool.dma_start(const[:], consts_in).then_inc(s_consts_loaded, 16)
            pool.dma_start(proj[:, 0:5, :].rearrange("p a t -> p (a t)"), masks_in).then_inc(s_consts_loaded, 16)
            with pool.Fori(0, DEPTH) as L:
                pool.wait_ge(s_params_free, L + 1)
                pool.dma_start(par[:], params_in[bass.ds(L, 1), :, :].rearrange("a p n -> p (a n)")).then_inc(s_params_loaded, 16)

        @block.scalar
        def _(act):
            def hi(chunk, quad, j, piece, widths=WIDE):
                if piece == 0:
                    act.wait_ge(raw_landed[j % RAW], quad * 32 + 16 * (j // RAW + 1))
                act.wait_ge(s_pieces_used, chunk * PIECES + (piece + 1))
                n, at = widths[piece], widths[0] * piece
                nc.scalar.copy(w_hi[:, j % SPLIT, OFFSET * piece:OFFSET * piece + n],
                               raw[:, j % RAW, at:at + n]).then_inc(s_hi_ready, 1)

            def refresh(tile, nth, gain):
                act.wait_ge(s_x_ready, nth + 1)
                act.sem_inc(s_passed_act, 1)
                nc.scalar.activation(h_hi[:, bass.ds(tile, 1), :], x[:, bass.ds(tile, 1), :], ACT.Copy,
                                     scale=gain).then_inc(s_h_hi_ready, 1)
                act.wait_ge(s_ssq_added, nth + 1)
                act.sem_inc(s_passed_act, 1)
                nc.scalar.activation(sqt[:], x[:, bass.ds(tile, 1), :].rearrange("p a t -> p (a t)"),
                                     ACT.Square).then_inc(s_sq_ready, 1)

            def token_rstd(nth):
                act.wait_ge(s_sums_ready, nth + 1)
                nc.scalar.activation(rstd[:], bank[4][:, 0:T], ACT.Ln, bias=eps[:], scale=1.0 / D).then_inc(s_rstd_log, 1)
                act.wait_ge(s_rstd_log, nth + 1)
                nc.scalar.activation(rstd[:], rstd[:], ACT.Exp, scale=-0.5).then_inc(s_rstd_ready, 1)

            for k in range(2):
                at = slice(8 * k, 8 * k + 8)
                act.wait_ge(s_x_loaded[k], 16)
                nc.scalar.activation(x_sq[:, at, :], x[:, at, :], ACT.Square).then_inc(s_start_sq, 1)
                act.wait_ge(s_start_xg, k + 1)
                nc.scalar.copy(h_hi[:, at, :], x_g[:, at, :]).then_inc(s_start_hi, 1)
            act.wait_ge(s_eps_set, 1)
            act.sem_inc(s_passed_act, 1)

            with act.Fori(0, DEPTH) as L:
                c0, q0 = L * CHUNKS, L * QUADS
                for s in range(2):
                    for piece in range(PIECES):
                        hi(c0 + s, q0, s, piece)
                token_rstd(L * 2)

                def ahead(s, piece):
                    s += 2
                    hi(c0 + s, q0 + s // 4, s % 4, piece)

                def head_weights(h):
                    act.wait_ge(s_masked, 8 * L + h + 1)
                    for qb, first, end in ((0, 0, P), (1, P, 3 * P)):
                        nc.scalar.activation(prob[:, h % 4, first:end], prob[:, h % 4, first:end], ACT.Exp, scale=SCALE,
                                             bias=scol(192 + 2 * h + qb), accum_out=scol(224 + 2 * h + qb)).then_inc(s_prob_ready, 1)

                def head_transposed(h):
                    act.wait_ge(s_probt_ready, 8 * L + h + 1)
                    if h >= 2:
                        act.wait_ge(s_o_ready, 8 * L + h - 1)
                    nc.scalar.copy(probt[:, h % 2, :], bank[6][:, 0:3 * P]).then_inc(s_probt_copied, 1)

                def head_out(h):
                    act.wait_ge(s_o_ready, 8 * L + h + 1)
                    nc.scalar.copy(cata_hi[:, h, :], bank[7][:, 0:T]).then_inc(s_o_hi, 1)

                for s in range(N_OUT):
                    ahead(s, 0)
                    if s >= N_MLA:
                        mla_evac(act, True, L, c0, s - N_MLA, 0)
                    ahead(s, 1)
                    if s >= N_MLA:
                        mla_evac(act, True, L, c0, s - N_MLA, 1)
                    if s == 2:
                        act.wait_ge(s_params_loaded, 16 * (L + 1))
                        nc.scalar.activation(scol(64, 8), par[:, C_ALOG:C_ALOG + 8], ACT.Exp).then_inc(s_neg_a, 1)
                        act.wait_ge(s_dt_abs, L + 1)
                        nc.scalar.activation(scol(32, 16), scol(16, 16), ACT.Exp).then_inc(s_dt_exp, 1)
                        act.wait_ge(s_dt_exp, L + 1)
                        nc.scalar.activation(scol(48, 16), scol(32, 16), ACT.Ln, bias=1.0).then_inc(s_dt_log, 1)
                    if s == 7:
                        act.wait_ge(s_seg_ready, 4 * L + 2)
                        nc.scalar.activation(scol(128, 8), scol(120, 8), ACT.Exp).then_inc(s_ds_exp, 1)
                        nc.scalar.activation(dec[:, 0], dec[:, 0], ACT.Exp).then_inc(s_seg_exp, 1)
                    if s == 8:
                        act.wait_ge(s_seg_ready, 4 * L + 4)
                        nc.scalar.activation(dec[:, 1], dec[:, 1], ACT.Exp).then_inc(s_seg_exp, 1)
                        for g, b in ((0, 7), (1, 4)):
                            nc.scalar.activation(cea[:, 4 * g:4 * g + 4, :], bank[b][:, :].rearrange("p (h t) -> p h t", h=4),
                                                 ACT.Exp).then_inc(s_ea_exp, 1)
                    if s == 9:
                        act.wait_ge(s_conv_ready, 8 * (L + 1))
                        nc.scalar.activation(xc[:], xc[:], ACT.Silu).then_inc(s_silu_ready, 1)
                    if s == 10:
                        act.wait_ge(s_gl_neg, L + 1)
                        nc.scalar.activation(g_neg, g_neg, ACT.Exp).then_inc(s_gl_exp, 1)
                        act.wait_ge(s_gl_exp, L + 1)
                        nc.scalar.activation(g_neg, g_neg, ACT.Ln, bias=1.0).then_inc(s_gl_log, 1)
                    if s == 11:
                        act.wait_ge(s_xs_t, 3 * (L + 1))
                        nc.scalar.copy(btok, bank[7][:, 0:256]).then_inc(s_btok_ready, 1)
                    if s == 14:
                        act.wait_ge(s_state_ready, L + 1)
                        nc.scalar.copy(sst, bank[5][:, :]).then_inc(s_state_copied, 1)
                        act.wait_ge(s_gl_v, L + 1)
                        for c in range(TP):
                            nc.scalar.copy(v_gla[:, c, :], bank[2 + c][:, :]).then_inc(s_gl_vcopied, 1)
                        act.wait_ge(s_gl_diff, 2 * L + 1)
                        nc.scalar.activation(e3[:], e3[:], ACT.Exp, scale=1.0 / GLA_TAU).then_inc(s_gl_e, 1)
                    if s == 15:
                        act.wait_ge(s_gl_kqd, L + 1)
                        nc.scalar.activation(kq[:], kq[:], ACT.Exp, scale=1.0 / GLA_TAU).then_inc(s_gl_kq, 1)
                        act.wait_ge(s_in_taken, IN_TILES * L + 15)
                        nc.scalar.activation(qs, qs, ACT.Copy, scale=GLA_CH ** -0.5).then_inc(s_gl_qs, 1)
                    if s == 19:
                        act.wait_ge(s_gl_kt, L + 1)
                        nc.scalar.copy(kd_t, bank[2][:, :].rearrange("p (b h n) -> p b h n", b=TP, h=2)).then_inc(s_gl_ktc, 1)
                    if s == 23:
                        act.wait_ge(s_in_taken, IN_TILES * L + 23)
                        act.wait_ge(s_y_skip, L + 1)
                        nc.scalar.activation(lat_sq, proj[:, T_CQ:T_CQ + 6, :], ACT.Square).then_inc(s_mla_sq, 1)
                        act.wait_ge(s_gl_diff, 2 * L + 2)
                        nc.scalar.activation(e3[:], e3[:], ACT.Exp, scale=1.0 / GLA_TAU).then_inc(s_gl_e, 1)
                    if s == 25:
                        act.wait_ge(s_mla_sums, L + 1)
                        nc.scalar.activation(lat_rstd[:, 0, :], bank[3][:, 0:T], ACT.Ln, bias=eps[:], scale=1.0 / 512).then_inc(s_mla_log, 1)
                        nc.scalar.activation(lat_rstd[:, 1, :], bank[3][:, T:2 * T], ACT.Ln, bias=eps[:], scale=1.0 / 256).then_inc(s_mla_log, 1)
                        act.wait_ge(s_mla_log, 2 * (L + 1))
                        nc.scalar.activation(lat_rstd, lat_rstd, ACT.Exp, scale=-0.5).then_inc(s_mla_rstd, 1)
                    if s == 27:
                        for k in range(6):
                            act.wait_ge(s_mla_normed, 2 * L + (1 if k < 4 else 2))
                            nc.scalar.activation(cata_hi[:, k, :], proj[:, T_CQ + k, :], ACT.Copy,
                                                 scale=par[:, C_QG + k:C_QG + k + 1]).then_inc(s_mla_hi, 1)
                        act.wait_ge(s_in_taken, IN_TILES * L + 27)
                        nc.scalar.activation(z, z, ACT.Silu).then_inc(s_silu_ready, 1)
                    if s == 28:
                        act.wait_ge(s_y_gated, L + 1)
                        nc.scalar.activation(z, y_ssd, ACT.Square).then_inc(s_y_sq, 1)
                    if s == 30:
                        act.wait_ge(s_gl_o, L + 1)
                        for q in range(2):
                            nc.scalar.activation(o_sq[:, q, :], bank[4 + q][:, :], ACT.Square).then_inc(s_gl_osq, 1)
                        act.wait_ge(s_in_taken, IN_TILES * (L + 1))
                        nc.scalar.activation(proj[:, T_GR:T_GR + 4, :], proj[:, T_GR:T_GR + 4, :], ACT.Silu).then_inc(s_silu_ready, 1)
                        act.wait_ge(s_y_sums, L + 1)
                        nc.scalar.activation(sum_rstd, bank[2][:, 0:T], ACT.Ln, bias=eps[:], scale=1.0 / 512).then_inc(s_y_log, 1)
                        act.wait_ge(s_y_log, L + 1)
                        nc.scalar.activation(sum_rstd, sum_rstd, ACT.Exp, scale=-0.5).then_inc(s_y_rstd, 1)
                    if s == 31:
                        act.wait_ge(s_k_rope, L + 1)
                        nc.scalar.copy(kp[64:128, :], kp[0:64, :]).then_inc(s_k_dup, 1)
                        act.wait_ge(s_y_normed, L + 1)
                        for k in range(4):
                            nc.scalar.activation(catb_hi[:, k, :], y_ssd[:, k, :], ACT.Copy,
                                                 scale=par[:, C_SSDG + k:C_SSDG + k + 1]).then_inc(s_y_hi, 1)
                    if s == 32:
                        act.wait_ge(s_gl_osum, L + 1)
                        for q in range(2):
                            nc.scalar.activation(o_rstd[:, q, :], bank[6 + q][:, :], ACT.Ln, bias=eps[:],
                                                 scale=1.0 / P).then_inc(s_gl_olog, 1)
                        act.wait_ge(s_gl_olog, 2 * (L + 1))
                        nc.scalar.activation(o_rstd, o_rstd, ACT.Exp, scale=-0.5).then_inc(s_gl_orstd, 1)
                    if s == 34:
                        act.wait_ge(s_gl_y, L + 1)
                        nc.scalar.copy(catb_hi[:, 4:8, :].rearrange("p (h q) t -> p q h t", q=2),
                                       o_y.rearrange("p q (h t) -> p q h t", h=2)).then_inc(s_gl_hi, 1)
                for k in range(2 * KT):
                    if k < HEADS_MLA:
                        head_weights(k)
                    if 2 <= k < HEADS_MLA + 2:
                        head_transposed(k - 2)
                    if 3 <= k < HEADS_MLA + 3:
                        head_out(k - 3)
                    ahead(N_OUT + k // 2, k % 2)
                    if k >= KT:
                        refresh(k - KT, L * 2 * KT + k - KT, par[:, C_FFN + k - KT:C_FFN + k - KT + 1])
                token_rstd(L * 2 + 1)

                for half in range(2):
                    def gate_chunk(i, j, widths):
                        quad = q0 + Q_GATE[half] + i
                        f, nth = j // 2, L * FT + (half * HALF + j // 2) + i * 2
                        for piece in range(PIECES):
                            hi(quad * 4 + j + 2, quad + (j + 2) // 4, (j + 2) % 4, piece, widths)
                        if j % 2 == 0:
                            act.wait_ge(s_gate_ready, nth + 1)
                            nc.scalar.activation(sl[:, f, :], cv[:, f, :], ACT.Silu).then_inc(s_gate_silu, 1)
                        else:
                            act.wait_ge(s_hid_ready, nth + 1)
                            nc.scalar.copy(hid_hi[:, bass.ds(i * 2 + f, 1), :], hv[:, f:f + 1, :]).then_inc(s_hid_hi_ready, 1)

                    act.sem_inc(s_passed_act, 1)
                    with act.Fori(0, 10) as i:
                        for j in range(4):
                            gate_chunk(i, j, WIDE)
                    for j in range(4):
                        gate_chunk(10, j, WIDE if j < 2 else NARROW)

                    def down_chunk(i, jj, widths):
                        quad = q0 + Q_DOWN[half] + i * 2
                        if widths:
                            for piece in range(PIECES):
                                hi(quad * 4 + jj + 2, quad + (jj + 2) // 4, (jj + 2) % 4, piece, widths)
                        if half == 1 and jj % 2 == 1:
                            m = i * 4 + jj // 2
                            refresh(m, L * 2 * KT + KT + m, gains[:, bass.ds((L + 1) * KT + m, 1)])

                    act.sem_inc(s_passed_act, 1)
                    with act.Fori(0, 3) as i:
                        for jj in range(8):
                            down_chunk(i, jj, NARROW)
                    for jj in range(8):
                        down_chunk(3, jj, NARROW if jj < 6 else (WIDE if half == 0 else None))

            token_rstd(2 * DEPTH)

        @block.vector
        def _(dve):
            def lo(chunk, j, piece, widths=WIDE):
                dve.wait_ge(s_hi_ready, chunk * PIECES + (piece + 1))
                n, at = widths[piece], widths[0] * piece
                slot = slice(OFFSET * piece, OFFSET * piece + n)
                nc.vector.tensor_tensor(w_lo[:, j % SPLIT, slot], raw[:, j % RAW, at:at + n],
                                        w_hi[:, j % SPLIT, slot].bitcast(F32), ALU.subtract).then_inc(s_lo_ready, 1)

            def refresh(tile, nth, gain):
                at = bass.ds(tile, 1)
                dve.wait_ge(s_h_hi_ready, nth + 1)
                nc.vector.scalar_tensor_tensor(out=h_lo[:, at, :], in0=x[:, at, :], scalar=gain,
                                               in1=h_hi[:, at, :].bitcast(F32), op0=ALU.mult,
                                               op1=ALU.subtract).then_inc(s_h_ready, 1)
                dve.wait_ge(s_sq_ready, nth + 1)
                dve.wait_ge(s_ssq_added, nth + 1)
                nc.vector.tensor_tensor(ssq[:], ssq[:], sqt[:], ALU.add).then_inc(s_ssq_added, 1)

            nc.vector.memset(eps[:], EPS).then_inc(s_eps_set, 1)
            dve.sem_inc(s_lo_ready, RAW * PIECES)
            dve.sem_inc(s_params_free, 1)
            for b in range(4):
                dve.sem_inc(bank_free[b], 1)
            dve.wait_ge(s_gains_loaded, 16)
            for k in range(2):
                at = slice(8 * k, 8 * k + 8)
                dve.wait_ge(s_x_loaded[k], 16)
                nc.vector.tensor_tensor(x_g[:, at, :], x[:, at, :], gains[:, at].unsqueeze(2).to_broadcast([P, 8, T]),
                                        ALU.mult).then_inc(s_start_xg, 1)
            for k in range(2):
                at = slice(8 * k, 8 * k + 8)
                dve.wait_ge(s_start_hi, k + 1)
                nc.vector.tensor_tensor(h_lo[:, at, :], x_g[:, at, :], h_hi[:, at, :].bitcast(F32),
                                        ALU.subtract).then_inc(s_start_lo, 1)
            dve.wait_ge(s_start_lo, 2)
            dve.sem_inc(s_h_ready, 1)
            dve.wait_ge(s_start_sq, 2)
            nc.vector.tensor_reduce(ssq[:], x_sq[:].rearrange("p k t -> p t k"), AX.X, ALU.add).then_inc(s_ssq_added, 1)
            dve.wait_ge(s_consts_loaded, 32)
            nc.vector.tensor_copy(masks[:], flat(proj[:, 0:5, :])).then_inc(s_masks_set, 1)
            dve.wait_ge(s_masks_set, 1)

            class Steps:
                def __init__(self, counted, before):
                    self.counted, self.before, self.n = counted, before, 0

                def step(self, ins):
                    ins.then_inc(self.counted, 1)
                    self.n += 1

                def settle(self):
                    dve.wait_ge(self.counted, self.before + self.n)

            with dve.Fori(0, DEPTH) as L:
                c0 = L * CHUNKS
                for s in range(2):
                    for piece in range(PIECES):
                        lo(c0 + s, s, piece)
                vec = Steps(s_vec_step, L * VEC_STEPS)
                step, settle = vec.step, vec.settle

                def ahead(s, piece):
                    lo(c0 + s + 2, s + 2, piece)

                def after_piece(chunk, piece):
                    dve.wait_ge(s_pieces_used, (c0 + chunk) * PIECES + (piece + 1 + SPLIT * PIECES))

                def take(s):
                    after_piece(s, 1)
                    nc.vector.tensor_tensor(proj[:, IN_ORDER[s], :], bank[s % 2][:, 0:T], rstd[:],
                                            ALU.mult).then_inc(bank_free[s % 2], 1)
                    dve.wait_ge(bank_free[s % 2], L * TURNS[s % 2] + (TURN["in", s] + 2))
                    dve.sem_inc(s_in_taken, 1)

                def convolve(t):
                    for k in range(SSD_TAPS):
                        at = C_CONV + SSD_TAPS * t + SSD_TAPS - 1 - k
                        tap = par[:, at:at + 1]
                        if k == 0:
                            nc.vector.tensor_scalar(xc[:, t, :], proj[:, t, :], tap, par[:, C_CONVB + t:C_CONVB + t + 1],
                                                    ALU.mult, ALU.add).then_inc(s_conv_step, 1)
                        else:
                            dve.wait_ge(s_conv_step, (L * 8 + t) * 3 + k)
                            nc.vector.scalar_tensor_tensor(
                                out=xc[:, t, k:T], in0=proj[:, t, 0:T - k], scalar=tap, in1=xc[:, t, k:T],
                                op0=ALU.mult, op1=ALU.add).then_inc(s_conv_step if k < 3 else s_conv_ready, 1)

                two8 = lambda ap: ap.rearrange("p (c h) -> p c h", c=TP)
                heads = lambda ap: ap.rearrange("p (h q) -> p h q", h=8)

                def segments(c):
                    for g in range(2):
                        b = bank[(5, 6, 7, 4)[2 * c + g]]
                        dve.wait_ge(s_cumb_ready, 4 * L + 2 * c + g + 1)
                        for h in range(4):
                            step(nc.vector.tensor_scalar(dec[:, c, 4 * g + h, :], b[:, h * P:(h + 1) * P],
                                                         scol(144 + 8 * c + 4 * g + h), 0.0, ALU.subtract, ALU.min))
                        if c == 0:
                            step(nc.vector.tensor_tensor(scol(120 + 4 * g, 4),
                                                         b[:, :].rearrange("p (h t) -> p h t", h=4)[:, :, P - 1],
                                                         scol(144 + 4 * g, 4), ALU.subtract))
                        settle()
                        dve.sem_inc(s_seg_ready, 1)

                def level_distances(batch):
                    for e in range(3):
                        size = GLA_CH >> (3 * batch + e + 1)
                        g_v = g_cum.rearrange("p (n b) -> p n b", b=2 * size)
                        e_v = e3[:, e, :].rearrange("p (n b) -> p n b", b=2 * size)
                        ref = g_v[:, :, size - 1:size].to_broadcast([P, 2 * T // (2 * size), size])
                        step(nc.vector.tensor_tensor(e_v[:, :, size:], g_v[:, :, size:], ref, ALU.subtract))
                        step(nc.vector.tensor_tensor(e_v[:, :, :size], ref, g_v[:, :, :size], ALU.subtract))
                    settle()
                    dve.sem_inc(s_gl_diff, 1)

                def level_queries(batch):
                    dve.wait_ge(s_gl_e, 2 * L + batch + 1)
                    dve.wait_ge(s_gl_qs, L + 1)
                    nc.vector.tensor_tensor(q3[:], e3[:], qs.unsqueeze(1).to_broadcast([P, 3, 2 * T]),
                                            ALU.mult).then_inc(s_gl_q, 1)

                def level_keys(batch):
                    dve.wait_ge(s_gl_q, 2 * L + batch + 1)
                    nc.vector.tensor_tensor(e3[:], e3[:], ks.unsqueeze(1).to_broadcast([P, 3, 2 * T]),
                                            ALU.mult).then_inc(s_gl_k, 1)

                def place_level(e):
                    which = ident.bitcast(mybir.dt.int32) if e == 0 else masks[:, (e - 1) * P:e * P]
                    for q in range(2):
                        dve.wait_ge(s_gl_lvl, 14 * L + 2 * e + q + 1)
                        if e:
                            dve.wait_ge(s_gl_put, 14 * L + 2 * e - 1 + q)
                        else:
                            dve.wait_ge(s_gl_zero, L + 1)
                        dve.sem_inc(s_passed_dve, 1)
                        nc.vector.copy_predicated(attn[:, q, :].rearrange("p (n t) -> p n t", n=4),
                                                  which.unsqueeze(1).to_broadcast([P, 4, P]),
                                                  bank[4 + 2 * (e % 2) + q][:, :].rearrange("p (n t) -> p n t", n=4)).then_inc(s_gl_put, 1)

                def gla_state(c):
                    b = bank[2 + c % 2]
                    dve.wait_ge(s_gl_u, 3 * L + c + 1)
                    for hp in range(2):
                        for q in range(2):
                            rows = slice(64 * q, 64 * q + 64)
                            new = b[rows, hp * 256 + q * P:hp * 256 + q * P + P]
                            if c == 0:
                                step(nc.vector.tensor_copy(st_gla[rows, 0, hp, :], new))
                            else:
                                step(nc.vector.scalar_tensor_tensor(
                                    out=st_gla[rows, c, hp, :], in0=st_gla[rows, c - 1, hp, :],
                                    scalar=small[rows, 176 + 4 * hp + c:177 + 4 * hp + c], in1=new,
                                    op0=ALU.mult, op1=ALU.add))
                    settle()
                    dve.sem_inc(s_gl_s, 1)

                def head_scores(h):
                    dve.wait_ge(s_scores_ready, 8 * L + h + 1)
                    if h >= 4:
                        dve.wait_ge(s_probt_ready, 8 * L + h - 3)
                    row = prob[:, h % 4, :]
                    step(nc.vector.tensor_tensor(row, bank[4 + h % 2][:, 0:3 * P], causal, ALU.add))
                    settle()
                    step(nc.vector.reduce_max(scol(208 + 2 * h), row[:, 0:P], AX.X))
                    step(nc.vector.reduce_max(scol(209 + 2 * h), row[:, P:3 * P], AX.X))
                    settle()
                    nc.vector.tensor_scalar(scol(192 + 2 * h, 2), scol(208 + 2 * h, 2), -SCALE, None, ALU.mult).then_inc(s_masked, 1)

                def head_normalise(h):
                    dve.wait_ge(s_prob_ready, 16 * L + 2 * h + 2)
                    row = prob[:, h % 4, :]
                    step(nc.vector.reciprocal(scol(240 + 2 * (h % 4), 2), scol(224 + 2 * h, 2)))
                    settle()
                    step(nc.vector.tensor_scalar(row[:, 0:P], row[:, 0:P], scol(240 + 2 * (h % 4)), None, ALU.mult))
                    settle()
                    nc.vector.tensor_scalar(row[:, P:3 * P], row[:, P:3 * P], scol(241 + 2 * (h % 4)), None, ALU.mult).then_inc(s_prob_norm, 1)

                def head_out(h):
                    dve.wait_ge(s_o_hi, 8 * L + h + 1)
                    nc.vector.tensor_tensor(cata_lo[:, h, :], bank[7][:, 0:T], cata_hi[:, h, :].bitcast(F32),
                                            ALU.subtract).then_inc(s_o_lo, 1)

                dve.wait_ge(s_rstd_ready, 2 * L + 1)
                dve.wait_ge(s_params_loaded, 16 * (L + 1))

                for s in range(N_OUT):
                    ahead(s, 0)
                    if s < N_MLA:
                        take(s)
                    else:
                        mla_evac(dve, False, L, c0, s - N_MLA, 0)
                    ahead(s, 1)
                    if s >= N_MLA:
                        mla_evac(dve, False, L, c0, s - N_MLA, 1)
                    if 1 <= s <= 8:
                        convolve(s - 1)
                    if s == 2:
                        dve.wait_ge(s_dt_t, L + 1)
                        step(nc.vector.tensor_tensor(two8(scol(0, 16)), two8(bank[4][:, 0:16]),
                                                     par[:, C_DTB:C_DTB + 8].unsqueeze(1).to_broadcast([P, TP, 8]), ALU.add))
                        settle()
                        nc.vector.scalar_tensor_tensor(out=scol(16, 16), in0=scol(0, 16), scalar=-1.0, in1=scol(0, 16),
                                                       op0=ALU.mult, op1=ALU.min).then_inc(s_dt_abs, 1)
                    if s == 3:
                        dve.wait_ge(s_dt_log, L + 1)
                        step(nc.vector.scalar_tensor_tensor(out=scol(80, 16), in0=scol(0, 16), scalar=0.0, in1=scol(48, 16),
                                                            op0=ALU.max, op1=ALU.add))
                        settle()
                        dve.wait_ge(s_neg_a, L + 1)
                        nc.vector.scalar_tensor_tensor(out=two8(scol(96, 16)), in0=two8(scol(80, 16)), scalar=-1.0,
                                                       in1=scol(64, 8).unsqueeze(1).to_broadcast([P, TP, 8]),
                                                       op0=ALU.mult, op1=ALU.mult).then_inc(s_a_ready, 1)
                        dve.wait_ge(s_a_ready, L + 1)
                        nc.vector.tensor_tensor(dec[:].rearrange("p c h t -> p (c h) t"),
                                                scol(96, 16).unsqueeze(2).to_broadcast([P, 16, P]),
                                                tri.unsqueeze(1).to_broadcast([P, 16, P]), ALU.mult).then_inc(s_ta_ready, 1)
                    if s == 5:
                        dve.wait_ge(s_acum_ready, L + 1)
                        nc.vector.tensor_copy(scol(144, 16), bank[4][:, 0:16]).then_inc(s_acum_copied, 1)
                        dve.wait_ge(s_acum_copied, L + 1)
                    if s == 6:
                        dve.wait_ge(s_cumb_ready, 4 * L + 4)
                        segments(0)
                    if s == 7:
                        segments(1)
                    if s == 9:
                        dve.wait_ge(s_gl_pre, L + 1)
                        for k in range(2):
                            step(nc.vector.tensor_scalar(g_raw[:, k * T:(k + 1) * T], bank[2][:, k * T:(k + 1) * T],
                                                         par[:, C_BGK + k:C_BGK + k + 1], None, ALU.add))
                        settle()
                        nc.vector.scalar_tensor_tensor(out=g_neg, in0=g_raw, scalar=-1.0, in1=g_raw,
                                                       op0=ALU.mult, op1=ALU.min).then_inc(s_gl_neg, 1)
                    if s == 10:
                        dve.wait_ge(s_gl_log, L + 1)
                        step(nc.vector.scalar_tensor_tensor(out=g_raw, in0=g_raw, scalar=0.0, in1=g_neg,
                                                            op0=ALU.min, op1=ALU.subtract))
                        settle()
                        nc.vector.tensor_tensor_scan(g_cum, keep, g_raw, 0.0, ALU.mult, ALU.add).then_inc(s_gl_scan, 1)
                        dve.wait_ge(s_gl_scan, L + 1)
                    if s == 11:
                        dve.wait_ge(s_xs_t, 3 * (L + 1))
                        for c in range(TP):
                            nc.vector.tensor_tensor(heads(xdt[:, c, :]), heads(bank[5 + c][:, :]),
                                                    scol(80 + 8 * c, 8).unsqueeze(2).to_broadcast([P, 8, SSD_P]),
                                                    ALU.mult).then_inc(s_xdt_ready, 1)
                        dve.wait_ge(s_cb_ready, L + 1)
                        step(nc.vector.tensor_tensor(gm[:], bank[4][:, :].rearrange("p (a t) -> p a t", a=4),
                                                     tri.unsqueeze(1).to_broadcast([P, 4, P]), ALU.mult))
                        settle()
                    if s == 12:
                        dve.wait_ge(s_ds_exp, L + 1)
                        dve.wait_ge(s_xdt_ready, 2 * (L + 1))
                        nc.vector.tensor_tensor(heads(dsx[:]), heads(xdt[:, 0, :]),
                                                scol(128, 8).unsqueeze(2).to_broadcast([P, 8, SSD_P]), ALU.mult).then_inc(s_dsx_ready, 1)
                        dve.wait_ge(s_seg_exp, 2 * (L + 1))
                        for c in range(TP):
                            for g in range(2):
                                nc.vector.tensor_tensor(dec[:, c, 4 * g:4 * g + 4, :], dec[:, c, 4 * g:4 * g + 4, :],
                                                        gm[:, 2 * c + g:2 * c + g + 1, :].to_broadcast([P, 4, P]),
                                                        ALU.mult).then_inc(s_m_ready, 1)
                    if s == 13:
                        dve.wait_ge(s_ea_exp, 2 * (L + 1))
                        for g in range(2):
                            nc.vector.tensor_tensor(cea[:, 4 * g:4 * g + 4, :], cea[:, 4 * g:4 * g + 4, :],
                                                    xc[:, 6 + g:7 + g, P:T].to_broadcast([P, 4, P]), ALU.mult).then_inc(s_cea_ready, 1)
                        level_distances(0)
                    if s == 14:
                        g_v = g_cum.rearrange("p (n b) -> p n b", b=GLA_CH)
                        step(nc.vector.tensor_tensor(kq[:, 0, :].rearrange("p (n b) -> p n b", b=GLA_CH),
                                                     g_v[:, :, GLA_CH - 1:GLA_CH].to_broadcast([P, 8, GLA_CH]), g_v, ALU.subtract))
                        step(nc.vector.tensor_copy(kq[:, 1, :], g_cum))
                        settle()
                        dve.sem_inc(s_gl_kqd, 1)
                        nc.vector.memset(attn[:], 0.0).then_inc(s_gl_zero, 1)
                    if s == 16:
                        dve.wait_ge(s_y_ready, L + 1)
                        for k in range(4):
                            step(nc.vector.scalar_tensor_tensor(out=y_ssd[:, k, :], in0=xc[:, k, :],
                                                                scalar=par[:, C_DSK + k:C_DSK + k + 1],
                                                                in1=bank[6 + k // 2][:, (k % 2) * T:(k % 2) * T + T],
                                                                op0=ALU.mult, op1=ALU.add))
                        settle()
                        dve.sem_inc(s_y_skip, 1)
                    if s == 17:
                        dve.wait_ge(s_gl_kq, L + 1)
                        step(nc.vector.tensor_copy(scol(176, 8).unsqueeze(2),
                                                   kq[:, 1, :].rearrange("p (n b) -> p n b", b=GLA_CH)[:, :, GLA_CH - 1:GLA_CH]))
                        nc.vector.tensor_tensor(kq[:, 0, :], kq[:, 0, :], ks, ALU.mult).then_inc(s_gl_kd, 1)
                        settle()
                        dve.wait_ge(s_gl_qs, L + 1)
                        nc.vector.tensor_tensor(kq[:, 1, :], kq[:, 1, :], qs, ALU.mult).then_inc(s_gl_qe, 1)
                        level_queries(0)
                    if s == 18:
                        level_keys(0)
                    if s == 19:
                        place_level(0)
                    if s == 20:
                        place_level(1)
                    if s == 21:
                        place_level(2)
                        place_level(3)
                    if s == 22:
                        level_distances(1)
                    if s == 23:
                        gla_state(0)
                        gla_state(1)
                    if s == 24:
                        level_queries(1)
                    if s == 25:
                        level_keys(1)
                        gla_state(2)
                    if s == 26:
                        dve.wait_ge(s_mla_rstd, L + 1)
                        for first, n, which in ((T_CQ, 4, 0), (T_CKV, 2, 1)):
                            nc.vector.tensor_tensor(proj[:, first:first + n, :], proj[:, first:first + n, :],
                                                    lat_rstd[:, which:which + 1, :].to_broadcast([P, n, T]),
                                                    ALU.mult).then_inc(s_mla_normed, 1)
                        dve.wait_ge(s_mla_normed, 2 * (L + 1))
                    if s == 27:
                        place_level(4)
                        place_level(5)
                    if s == 28:
                        dve.wait_ge(s_silu_ready, 3 * L + 2)
                        nc.vector.tensor_tensor(y_ssd, y_ssd, z, ALU.mult).then_inc(s_y_gated, 1)
                        for k in range(6):
                            dve.wait_ge(s_mla_hi, 6 * L + k + 1)
                            nc.vector.scalar_tensor_tensor(out=cata_lo[:, k, :], in0=proj[:, T_CQ + k, :],
                                                           scalar=par[:, C_QG + k:C_QG + k + 1],
                                                           in1=cata_hi[:, k, :].bitcast(F32), op0=ALU.mult,
                                                           op1=ALU.subtract).then_inc(s_mla_split, 1)
                    if s == 29:
                        place_level(6)
                    if s == 30:
                        dve.wait_ge(s_mla_split, 6 * (L + 1))
                        dve.wait_ge(s_rope_swapped, 3 * L + 1)
                        step(nc.vector.tensor_tensor(ropet[0:64, 0, :], bank[3][0:64, 0:T], sin[0:64, :], ALU.mult))
                        step(nc.vector.tensor_tensor(kp[0:64, :], proj[0:64, T_MIX, :], cos[0:64, :], ALU.mult))
                        settle()
                        nc.vector.tensor_tensor(kp[0:64, :], kp[0:64, :], ropet[0:64, 0, :], ALU.add).then_inc(s_k_rope, 1)
                        dve.wait_ge(s_k_rope, L + 1)
                        dve.wait_ge(s_y_rstd, L + 1)
                        nc.vector.tensor_tensor(y_ssd, y_ssd, sum_rstd.unsqueeze(1).to_broadcast([P, 4, T]),
                                                ALU.mult).then_inc(s_y_normed, 1)
                    if s == 32:
                        dve.wait_ge(s_y_normed, L + 1)
                        for k in range(4):
                            dve.wait_ge(s_y_hi, 4 * L + k + 1)
                            nc.vector.scalar_tensor_tensor(out=catb_lo[:, k, :], in0=y_ssd[:, k, :],
                                                           scalar=par[:, C_SSDG + k:C_SSDG + k + 1],
                                                           in1=catb_hi[:, k, :].bitcast(F32), op0=ALU.mult,
                                                           op1=ALU.subtract).then_inc(s_ssd_cat, 1)
                    if s == 33:
                        dve.wait_ge(s_silu_ready, 3 * (L + 1))
                        dve.wait_ge(s_gl_orstd, L + 1)
                        for q in range(2):
                            step(nc.vector.scalar_tensor_tensor(out=o_y[:, q, :], in0=bank[4 + q][:, :],
                                                                scalar=par[:, C_GLAG:C_GLAG + 1], in1=o_rstd[:, q, :],
                                                                op0=ALU.mult, op1=ALU.mult))
                        settle()
                        for q in range(2):
                            pair = o_y[:, q, :].rearrange("p (h t) -> p h t", h=2)
                            step(nc.vector.tensor_tensor(
                                pair, pair, proj[:, T_GR:T_GR + 4, :].rearrange("p (h q) t -> p q h t", q=2)[:, q], ALU.mult))
                        settle()
                        dve.sem_inc(s_gl_y, 1)
                    if s == 34:
                        dve.wait_ge(s_rope_swapped, 3 * L + 3)
                        for b in range(2):
                            step(nc.vector.tensor_tensor(ropet[:, 2 * b:2 * b + 2, :], bank[2 + b][:, :].rearrange("p (a t) -> p a t", a=2),
                                                         sin.unsqueeze(1).to_broadcast([P, 2, T]), ALU.mult))
                        step(nc.vector.tensor_tensor(qp[:], qp[:], cos.unsqueeze(1).to_broadcast([P, 4, T]), ALU.mult))
                        settle()
                        nc.vector.tensor_tensor(qp[:], qp[:], ropet, ALU.add).then_inc(s_q_rope, 1)
                        dve.wait_ge(s_gl_hi, L + 1)
                        nc.vector.tensor_tensor(catb_lo[:, 4:8, :].rearrange("p (h q) t -> p q h t", q=2),
                                                o_y.rearrange("p q (h t) -> p q h t", h=2),
                                                catb_hi[:, 4:8, :].rearrange("p (h q) t -> p q h t", q=2).bitcast(F32),
                                                ALU.subtract).then_inc(s_gl_cat, 1)

                for k in range(2 * KT):
                    if k == 0:
                        nc.vector.memset(ssq[:], 0.0).then_inc(s_ssq_zeroed, 1)
                    if k < HEADS_MLA:
                        head_scores(k)
                    if 1 <= k < HEADS_MLA + 1:
                        head_normalise(k - 1)
                    if 3 <= k < HEADS_MLA + 3:
                        head_out(k - 3)
                    ahead(N_OUT + k // 2, k % 2)
                    after_piece(N_OUT + k // 2, k % 2)
                    b, m = k % 2, k % KT
                    nc.vector.tensor_tensor(x[:, m, :], x[:, m, :], bank[b][:, 0:T], ALU.add).then_inc(bank_free[b], 1)
                    if k >= KT - 1:
                        dve.wait_ge(bank_free[b], L * TURNS[b] + (TURN["out", k] + 2))
                    if k == KT:
                        dve.wait_ge(s_ssq_zeroed, 2 * L + 1)
                    if k >= KT:
                        dve.sem_inc(s_x_ready, 1)
                        refresh(m, L * 2 * KT + m, par[:, C_FFN + m:C_FFN + m + 1])
                assert vec.n == VEC_STEPS, vec.n

                dve.wait_ge(s_rstd_ready, 2 * L + 2)
                nc.vector.memset(ssq[:], 0.0).then_inc(s_ssq_zeroed, 1)
                for half in range(2):
                    def gate_chunk(i, j, widths):
                        chunk = c0 + Q_GATE[half] * 4 + i * 4 + j
                        f, ft, nth = j // 2, i * 2 + (half * HALF + j // 2), L * FT + (half * HALF + j // 2) + i * 2
                        lo(chunk + 2, j + 2, 0, widths)
                        dve.wait_ge(s_pieces_used, chunk * PIECES + (PIECES + SPLIT * PIECES))
                        to = gs if j % 2 == 0 else us
                        nc.vector.tensor_tensor(to[:, f, :], bank[j][:, 0:T], rstd[:], ALU.mult).then_inc(bank_free[j], 1)
                        lo(chunk + 2, j + 2, 1, widths)
                        dve.wait_ge(bank_free[j], L * TURNS[j] + i + (TURN["gate", half, j] + 2))
                        if j % 2 == 0:
                            for k in range(FTAPS):
                                tap = par[:, bass.ds(ft * FTAPS + (C_FW + FTAPS - 1 - k), 1)]
                                if k == 0:
                                    nc.vector.tensor_scalar(cv[:, f, :], gs[:, f, :], tap, par[:, bass.ds(ft + C_FB, 1)],
                                                            ALU.mult, ALU.add).then_inc(s_gate_step, 1)
                                else:
                                    dve.wait_ge(s_gate_step, nth * 2 + k)
                                    nc.vector.scalar_tensor_tensor(
                                        out=cv[:, f, k:T], in0=gs[:, f, 0:T - k], scalar=tap, in1=cv[:, f, k:T],
                                        op0=ALU.mult, op1=ALU.add).then_inc(s_gate_step if k < 2 else s_gate_ready, 1)
                        else:
                            dve.wait_ge(s_gate_silu, nth + 1)
                            nc.vector.tensor_tensor(hv[:, f, :], us[:, f, :], sl[:, f, :], ALU.mult).then_inc(s_hid_ready, 1)
                            dve.wait_ge(s_hid_hi_ready, nth + 1)
                            at = bass.ds(i * 2 + f, 1)
                            nc.vector.tensor_tensor(hid_lo[:, at, :], hv[:, f:f + 1, :], hid_hi[:, at, :].bitcast(F32),
                                                    ALU.subtract).then_inc(s_hid_split, 1)

                    dve.sem_inc(s_passed_dve, 1)
                    with dve.Fori(0, 10) as i:
                        for j in range(4):
                            gate_chunk(i, j, WIDE)
                    for j in range(4):
                        gate_chunk(10, j, WIDE if j < 2 else NARROW)
                    if half == 1:
                        dve.wait_ge(s_gate_ready, (L + 1) * FT)
                        dve.sem_inc(s_params_free, 1)
                        dve.wait_ge(s_ssq_zeroed, 2 * L + 2)

                    def down_chunk(i, jj, widths):
                        chunk = c0 + Q_DOWN[half] * 4 + i * 8 + jj
                        if widths:
                            lo(chunk + 2, jj + 2, 0, widths)
                        if jj % 2 == 1:
                            b, m = jj // 2, i * 4 + jj // 2
                            dve.wait_ge(s_pieces_used, chunk * PIECES + (PIECES + SPLIT * PIECES))
                            xt = x[:, bass.ds(m, 1), :].rearrange("p a t -> p (a t)")
                            nc.vector.tensor_tensor(xt, xt, bank[b][:, 0:T], ALU.add).then_inc(bank_free[b], 1)
                        if widths:
                            lo(chunk + 2, jj + 2, 1, widths)
                        if jj % 2 == 1 and half == 1:
                            dve.wait_ge(bank_free[b], L * TURNS[b] + i + (TURN["down", half, b] + 2))
                            dve.sem_inc(s_x_ready, 1)
                            refresh(m, L * 2 * KT + KT + m, gains[:, bass.ds((L + 1) * KT + m, 1)])

                    dve.sem_inc(s_passed_dve, 1)
                    with dve.Fori(0, 3) as i:
                        for jj in range(8):
                            down_chunk(i, jj, NARROW)
                    for jj in range(8):
                        down_chunk(3, jj, NARROW if jj < 6 else (WIDE if half == 0 else None))
                    if half == 0:
                        for b in range(4):
                            dve.wait_ge(bank_free[b], L * TURNS[b] + (TURN["down", 0, b] + 5))

            dve.wait_ge(s_rstd_ready, 2 * DEPTH + 1)
            dve.sem_inc(s_passed_dve, 1)
            with dve.Fori(0, KT) as m:
                xt = x[:, bass.ds(m, 1), :].rearrange("p a t -> p (a t)")
                nc.vector.scalar_tensor_tensor(out=xt, in0=xt, scalar=gains[:, bass.ds(DEPTH * KT + m, 1)],
                                               in1=rstd[:], op0=ALU.mult, op1=ALU.mult).then_inc(s_final_ready, 1)

        @block.tensor
        def _(pe):
            pe.sem_inc(s_pieces_used, SPLIT * PIECES)
            pe.wait_ge(s_consts_loaded, 32)

            def three(out, w, rhs_hi, rhs_lo, first, last):
                w_high, w_low = w
                nc.tensor.matmul(out, w_high, rhs_hi, start=first, stop=False)
                nc.tensor.matmul(out, w_high, rhs_lo, start=False, stop=False)
                return nc.tensor.matmul(out, w_low, rhs_hi, start=False, stop=last)

            def piece_ready(chunk, piece):
                pe.wait_ge(s_lo_ready, chunk * PIECES + (piece + 1 + RAW * PIECES))

            def unit(j, piece, u, n=P):
                at = slice(OFFSET * piece + u * n, OFFSET * piece + (u + 1) * n)
                return w_hi[:, j % SPLIT, at], w_lo[:, j % SPLIT, at]

            def norm_sums(nth):
                pe.wait_ge(s_ssq_added, nth + 1)
                nc.tensor.matmul(bank[4][:, 0:T], ones, ssq[:], start=True, stop=True).then_inc(s_sums_ready, 1)

            def wide_tile(chunk, j, b, rhs_hi, rhs_lo, uses):
                for piece in range(PIECES):
                    piece_ready(chunk, piece)
                    if piece == 0:
                        pe.wait_ge(bank_free[b], uses)
                    for u in range(8):
                        k = 8 * piece + u
                        last = three(bank[b][:, 0:T], unit(j, piece, u), rhs_hi[:, k, :], rhs_lo[:, k, :], k == 0, k == KT - 1)
                    last.then_inc(s_pieces_used, 1)

            with pe.Fori(0, DEPTH) as L:
                c0 = L * CHUNKS
                norm_sums(L * 2 * KT)
                pe.wait_ge(s_h_ready, L * 2 * KT + 1)
                mix = proj[:, T_MIX, :]

                def mla_chunk(c):
                    j = (N_MLA + c) % 4
                    for piece in range(PIECES):
                        piece_ready(c0 + N_MLA + c, piece)
                        for b in (range(2) if c >= 3 else [piece]):
                            pe.wait_ge(bank_free[b], L * TURNS[b] + (TURN["mla", c, piece if c >= 3 else 0, b] + 1))
                            if c < 3:
                                for a in range(2):
                                    for k in range(4):
                                        last = three(bank[b][:, a * T:(a + 1) * T], unit(j, piece, 4 * a + k),
                                                     cata_hi[:, k, :], cata_lo[:, k, :], k == 0, k == 3)
                            elif c == 3:
                                for a in range(2):
                                    for k in range(2):
                                        last = three(bank[b][:, a * T:(a + 1) * T], unit(j, piece, 2 * (2 * b + a) + k),
                                                     cata_hi[:, 4 + k, :], cata_lo[:, 4 + k, :], k == 0, k == 1)
                            else:
                                at = slice(b * P, b * P + P)
                                for k in range(2):
                                    w_high, w_low = unit(j, piece, k, 512)
                                    nc.tensor.matmul(bank[b][:, :], cata_hi[:, 4 + k, at], w_high, start=k == 0, stop=False)
                                    nc.tensor.matmul(bank[b][:, :], cata_lo[:, 4 + k, at], w_high, start=False, stop=False)
                                    last = nc.tensor.matmul(bank[b][:, :], cata_hi[:, 4 + k, at], w_low, start=False, stop=k == 1)
                        last.then_inc(s_pieces_used, 1)

                def gla_level(e):
                    for q in range(2):
                        if e >= 2:
                            pe.wait_ge(s_gl_put, 14 * L + 2 * (e - 2) + q + 1)
                        rows = slice(64 * q, 64 * q + 64)
                        k_, q_ = (ks, qs) if e == 0 else (e3[:, (e - 1) % 3, :], q3[:, (e - 1) % 3, :])
                        for n in range(4):
                            at = slice(n * P, (n + 1) * P)
                            last = nc.tensor.matmul(bank[4 + 2 * (e % 2) + q][:, at], k_[rows, at], q_[rows, at],
                                                    start=True, stop=True)
                        last.then_inc(s_gl_lvl, 1)

                def gla_update(c):
                    rows = slice((c % 2) * 64, (c % 2) * 64 + 64)
                    for hp in range(2):
                        last = nc.tensor.matmul(bank[2 + c % 2][:, hp * 256:(hp + 1) * 256], kd_t[rows, c // 2, hp, :],
                                                v_gla[rows, c // 2, hp * 256:(hp + 1) * 256], start=True, stop=True)
                    last.then_inc(s_gl_u, 1)

                def head_scores(h):
                    b = bank[4 + h % 2]
                    if h >= 2:
                        pe.wait_ge(s_masked, 8 * L + h - 1)
                    rows = slice(64 * (h % 2), 64 * (h % 2) + 64)
                    nc.tensor.matmul(b[:, 0:P], qn[:, h, 0:P], kn[:, h, 0:P], start=True, stop=False)
                    nc.tensor.matmul(b[:, 0:P], qp[rows, h // 2, 0:P], kp[rows, 0:P], start=False, stop=True)
                    nc.tensor.matmul(b[:, P:3 * P], qn[:, h, P:T], kn[:, h, :], start=True, stop=False)
                    nc.tensor.matmul(b[:, P:3 * P], qp[rows, h // 2, P:T], kp[rows, :], start=False, stop=True).then_inc(s_scores_ready, 1)

                def head_transpose(h):
                    pe.wait_ge(s_prob_norm, 8 * L + h + 1)
                    if h >= 1:
                        pe.wait_ge(s_probt_copied, 8 * L + h)
                    for k in range(3):
                        last = nc.tensor.transpose(bank[6][:, k * P:(k + 1) * P], prob[:, h % 4, k * P:(k + 1) * P], ident)
                    last.then_inc(s_probt_ready, 1)

                def head_values(h):
                    pe.wait_ge(s_probt_copied, 8 * L + h + 1)
                    if h >= 1:
                        pe.wait_ge(s_o_lo, 8 * L + h)
                    pt, v = probt[:, h % 2, :], vv[:, :, h * P:(h + 1) * P]
                    nc.tensor.matmul(bank[7][:, 0:P], v[:, 0, :], pt[:, 0:P], start=True, stop=True)
                    nc.tensor.matmul(bank[7][:, P:T], v[:, 0, :], pt[:, P:2 * P], start=True, stop=False)
                    nc.tensor.matmul(bank[7][:, P:T], v[:, 1, :], pt[:, 2 * P:3 * P], start=False, stop=True).then_inc(s_o_ready, 1)

                for s in range(N_OUT):
                    if s == 2:
                        pe.wait_ge(s_in_taken, IN_TILES * L + 1)
                        pe.wait_ge(s_rstd_ready, 2 * L + 1)
                        pe.sem_inc(s_passed_pe, 1)
                        for c in range(TP):
                            last = nc.tensor.transpose(bank[4][:, 8 * c:8 * c + 8], mix[MIX_DT:MIX_DT + 8, c * P:(c + 1) * P],
                                                       ident[MIX_DT:MIX_DT + 8, MIX_DT:MIX_DT + 8])
                        last.then_inc(s_dt_t, 1)
                    if s == 5:
                        pe.wait_ge(s_a_ready, L + 1)
                        nc.tensor.matmul(bank[4][:, 0:16], tri, scol(96, 16), start=True, stop=True).then_inc(s_acum_ready, 1)
                    if s == 6:
                        pe.wait_ge(s_ta_ready, L + 1)
                        pe.wait_ge(s_acum_copied, L + 1)
                        ta = dec[:].rearrange("p c h t -> p (c h t)")
                        for n, b in enumerate((5, 6, 7, 4)):
                            nc.tensor.matmul(bank[b][:, :], ones, ta[:, n * 512:(n + 1) * 512], start=True, stop=True).then_inc(s_cumb_ready, 1)
                    if s == 8:
                        for k in range(2):
                            last = nc.tensor.matmul(bank[2][:, k * T:(k + 1) * T], par[MIX_GLOW:MIX_GLOW + 16, C_WGK + k * P:C_WGK + (k + 1) * P],
                                                    mix[MIX_GLOW:MIX_GLOW + 16, :], start=True, stop=True)
                        last.then_inc(s_gl_pre, 1)
                    if s == 11:
                        pe.wait_ge(s_silu_ready, 3 * L + 1)
                        pe.wait_ge(s_ea_exp, 2 * (L + 1))
                        for c in range(TP):
                            for k in range(4):
                                last = nc.tensor.transpose(bank[5 + c][:, k * P:(k + 1) * P], xc[:, k, c * P:(c + 1) * P], ident)
                            last.then_inc(s_xs_t, 1)
                        for g in range(2):
                            last = nc.tensor.transpose(bank[7][:, g * P:(g + 1) * P], xc[:, 4 + g, 0:P], ident)
                        last.then_inc(s_xs_t, 1)
                        for c in range(TP):
                            for g in range(2):
                                last = nc.tensor.matmul(bank[4][:, (2 * c + g) * P:(2 * c + g + 1) * P], xc[:, 4 + g, c * P:(c + 1) * P],
                                                        xc[:, 6 + g, c * P:(c + 1) * P], start=True, stop=True)
                        last.then_inc(s_cb_ready, 1)
                    if s == 14:
                        pe.wait_ge(s_dsx_ready, L + 1)
                        pe.wait_ge(s_btok_ready, L + 1)
                        for g in range(2):
                            last = nc.tensor.matmul(bank[5][:, g * 256:(g + 1) * 256], btok[:, g * P:(g + 1) * P],
                                                    dsx[:, g * 256:(g + 1) * 256], start=True, stop=True)
                        last.then_inc(s_state_ready, 1)
                        pe.wait_ge(s_in_taken, IN_TILES * L + 13)
                        for c in range(TP):
                            for k in range(4):
                                last = nc.tensor.transpose(bank[2 + c][:, k * P:(k + 1) * P], proj[:, T_GV + k, c * P:(c + 1) * P], ident)
                        last.then_inc(s_gl_v, 1)
                    if s == 16:
                        pe.wait_ge(s_state_copied, L + 1)
                        pe.wait_ge(s_m_ready, 4 * (L + 1))
                        pe.wait_ge(s_cea_ready, 2 * (L + 1))
                        for h in range(SSD_H):
                            rows = slice(64 * (h % 2), 64 * (h % 2) + 64)
                            for c in range(TP):
                                col = ((h // 2) % 2) * T + c * P
                                out = bank[6 + h // 4][rows, col:col + P]
                                last = nc.tensor.matmul(out, xdt[:, c, h * 64:(h + 1) * 64], dec[:, c, h, :], start=True, stop=c == 0)
                                if c == 1:
                                    last = nc.tensor.matmul(out, sst[:, h * 64:(h + 1) * 64], cea[:, h, :], start=False, stop=True)
                        last.then_inc(s_y_ready, 1)
                    if s == 19:
                        pe.wait_ge(s_gl_kd, L + 1)
                        pe.wait_ge(s_gl_vcopied, 2 * (L + 1))
                        for n in range(4):
                            last = nc.tensor.transpose(bank[2][:, n * P:(n + 1) * P],
                                                       kq[:, 0, (n % 2) * T + (n // 2) * P:(n % 2) * T + (n // 2 + 1) * P], ident)
                        last.then_inc(s_gl_kt, 1)
                        pe.wait_ge(s_y_skip, L + 1)
                        gla_level(0)
                    if s == 20:
                        pe.wait_ge(s_gl_k, 2 * L + 1)
                        gla_level(1)
                    if s == 21:
                        gla_level(2)
                        gla_level(3)
                    if s == 22:
                        pe.wait_ge(s_gl_ktc, L + 1)
                        gla_update(0)
                        gla_update(1)
                    if s == 25:
                        pe.wait_ge(s_mla_sq, L + 1)
                        pe.wait_ge(s_gl_s, 3 * L + 2)
                        gla_update(2)
                        for k in range(4):
                            nc.tensor.matmul(bank[3][:, 0:T], ones, lat_sq[:, k, :], start=k == 0, stop=k == 3)
                        for k in range(2):
                            last = nc.tensor.matmul(bank[3][:, T:2 * T], ones, lat_sq[:, 4 + k, :], start=k == 0, stop=k == 1)
                        last.then_inc(s_mla_sums, 1)
                    if s == 27:
                        pe.wait_ge(s_gl_k, 2 * L + 2)
                        gla_level(4)
                        gla_level(5)
                    if s == 29:
                        gla_level(6)
                        pe.wait_ge(s_mla_rstd, L + 1)
                        nc.tensor.matmul(bank[3][:, 0:T], swap[0:64, :], mix[0:64, :], start=True, stop=True).then_inc(s_rope_swapped, 1)
                    if s == 30:
                        pe.wait_ge(s_y_sq, L + 1)
                        pe.wait_ge(s_gl_s, 3 * L + 3)
                        for k in range(4):
                            last = nc.tensor.matmul(bank[2][:, 0:T], ones, z[:, k, :], start=k == 0, stop=k == 3)
                        last.then_inc(s_y_sums, 1)
                        pe.wait_ge(s_gl_put, 14 * (L + 1))
                        pe.wait_ge(s_gl_qe, L + 1)
                        for q in range(2):
                            rows = slice(64 * q, 64 * q + 64)
                            for hp in range(2):
                                head = 2 * hp + q
                                for c in range(TP):
                                    nc.tensor.matmul(bank[4 + q][:, hp * T + c * P:hp * T + (c + 1) * P],
                                                     v_gla[:, c, head * P:(head + 1) * P],
                                                     attn[:, q, (2 * hp + c) * P:(2 * hp + c + 1) * P], start=True, stop=False)
                                    for n in (2 * c, 2 * c + 1):
                                        if n == 0:
                                            continue
                                        at = slice(hp * T + n * 64, hp * T + (n + 1) * 64)
                                        last = nc.tensor.matmul(bank[4 + q][:, at], st_gla[rows, n - 1, hp, :], kq[rows, 1, at],
                                                                start=False, stop=n == 2 * c + 1)
                        last.then_inc(s_gl_o, 1)
                    if s == 32:
                        pe.wait_ge(s_gl_osq, 2 * (L + 1))
                        for q in range(2):
                            last = nc.tensor.matmul(bank[6 + q][:, :], ones, o_sq[:, q, :], start=True, stop=True)
                        last.then_inc(s_gl_osum, 1)
                    if s == 33:
                        for b in range(2):
                            pe.wait_ge(bank_free[b], L * TURNS[b] + (TURN["mla", 0, 0, b] + 2))
                        pe.wait_ge(s_y_rstd, L + 1)
                        pe.wait_ge(s_k_rope, L + 1)
                        for b in range(2):
                            for k in range(2):
                                last = nc.tensor.matmul(bank[2 + b][:, k * T:(k + 1) * T], swap, qp[:, 2 * b + k, :], start=True, stop=True)
                            last.then_inc(s_rope_swapped, 1)
                    if s < N_MLA:
                        wide_tile(c0 + s, s, s % 2, h_hi, h_lo, L * TURNS[s % 2] + (TURN["in", s] + 1))
                    else:
                        if s == N_MLA:
                            pe.wait_ge(s_mla_split, 6 * (L + 1))
                        mla_chunk(s - N_MLA)

                for b in range(2):
                    pe.wait_ge(bank_free[b], L * TURNS[b] + (TURN["mla", 4, 1, b] + 2))
                pe.wait_ge(s_q_rope, L + 1)
                pe.wait_ge(s_k_dup, L + 1)
                pe.wait_ge(s_gl_y, L + 1)
                for k in range(2 * KT):
                    if k < HEADS_MLA:
                        head_scores(k)
                    if 2 <= k < HEADS_MLA + 2:
                        head_transpose(k - 2)
                    if 3 <= k < HEADS_MLA + 3:
                        head_values(k - 3)
                    if k == 0:
                        pe.wait_ge(s_gl_cat, L + 1)
                        pe.wait_ge(s_ssd_cat, 4 * (L + 1))
                    if k == KT:
                        pe.wait_ge(s_o_lo, 8 * (L + 1))
                    chunk, piece = N_OUT + k // 2, k % 2
                    rhs_hi, rhs_lo = (catb_hi, catb_lo) if k < KT else (cata_hi, cata_lo)
                    piece_ready(c0 + chunk, piece)
                    pe.wait_ge(bank_free[k % 2], L * TURNS[k % 2] + (TURN["out", k] + 1))
                    for u in range(8):
                        last = three(bank[k % 2][:, 0:T], unit(chunk, piece, u), rhs_hi[:, u, :], rhs_lo[:, u, :], u == 0, u == 7)
                    last.then_inc(s_pieces_used, 1)
                norm_sums(L * 2 * KT + KT)
                pe.wait_ge(s_h_ready, L * 2 * KT + KT + 1)

                for half in range(2):
                    pe.sem_inc(s_passed_pe, 1)
                    with pe.Fori(0, 11) as i:
                        for j in range(4):
                            wide_tile(c0 + Q_GATE[half] * 4 + i * 4 + j, j, j, h_hi, h_lo,
                                      L * TURNS[j] + i + (TURN["gate", half, j] + 1))
                    pe.wait_ge(s_hid_split, L * FT + (half + 1) * HALF)
                    pe.sem_inc(s_passed_pe, 1)
                    with pe.Fori(0, 4) as i:
                        for jj in range(8):
                            b, part, j = jj // 2, jj % 2, jj % 4
                            for piece in range(PIECES):
                                piece_ready(c0 + Q_DOWN[half] * 4 + i * 8 + jj, piece)
                                if part == 0 and piece == 0:
                                    pe.wait_ge(bank_free[b], L * TURNS[b] + i + (TURN["down", half, b] + 1))
                                for u in range(DOWN_KTS[piece]):
                                    kt = part * DOWN_KT + DOWN_KTS[0] * piece + u
                                    last = three(bank[b][:, 0:T], unit(j, piece, u), hid_hi[:, kt, :], hid_lo[:, kt, :],
                                                 kt == 0, kt == HALF - 1)
                                last.then_inc(s_pieces_used, 1)
            norm_sums(DEPTH * 2 * KT)


VEC_STEPS = 104


def _tiles(w, kt):
    k, m = w.shape
    return w.reshape(kt, P, m // P, P).transpose(2, 1, 0, 3).reshape(m // P, P, kt * P)


def _cols(v):
    return v.reshape(-1, P).T


def kernel(**inputs):
    import concourse.bacc as _bacc
    from concourse.bass_utils import run_bass_kernel_spmd as _run

    a = {k: np.asarray(v) for k, v in inputs.items()}
    f = np.float32
    order = []
    at = lambda start, n: order.extend(range(start, start + n))
    at(1344, 1024); at(2888, 512); at(2376, 256); at(2632, 256); at(0, 512); at(512, 256); at(832, 512); at(3416, 512)
    front, outw, gate, down, params = [], [], [], [], []
    for l in range(DEPTH):
        w = a["w_in"][l]
        mix = np.zeros((D, P), f)
        mix[:, 0:64] = w[:, 768:832]
        mix[:, MIX_GLOW:MIX_GLOW + 16] = w[:, 3400:3416]
        mix[:, MIX_DT:MIX_DT + 8] = w[:, 2368:2376]
        front.append(_tiles(np.concatenate([mix, w[:, order]], 1), KT))
        uq = a["mla_w_uq"][l].reshape(512, 8, 192)
        uq = np.concatenate([uq[:, :, 128:].reshape(512, 512), uq[:, :, :128].reshape(512, 1024)], 1)
        front.append(_tiles(uq, 4).reshape(3, 4, P, 512).transpose(0, 2, 1, 3).reshape(3, P, CHUNK))
        ukv = a["mla_w_ukv"][l].reshape(256, 8, 256)
        front.append(_tiles(np.ascontiguousarray(ukv[:, :, :128]).reshape(256, 1024), 2).transpose(1, 0, 2).reshape(1, P, CHUNK))
        front.append(np.ascontiguousarray(ukv[:, :, 128:]).reshape(2, P, 2, 512).transpose(1, 2, 0, 3).reshape(1, P, CHUNK))
        for rows in (slice(1024, 2048), slice(0, 1024)):
            w = _tiles(a["w_out"][l][rows], 8)
            outw.append(w.reshape(8, 2, P, 1024).transpose(0, 2, 1, 3).reshape(8, P, CHUNK))
        g, u = _tiles(a["ffn_w_gate"][l], KT), _tiles(a["ffn_w_up"][l], KT)
        gate.append(np.stack([g, u], 1).reshape(2 * FT, P, CHUNK))
        dn = a["ffn_w_down"][l].reshape(2, 2, DOWN_KT, P, KT, P)
        down.append(dn.transpose(0, 4, 1, 3, 2, 5).reshape(64, P, DOWN_CHUNK))
        p = np.zeros((P, NPAR), f)
        p[:, C_FFN:C_FFN + 16] = _cols(a["ffn_norm"][l])
        p[:, C_QG:C_QG + 4] = _cols(a["mla_q_norm"][l])
        p[:, C_KVG:C_KVG + 2] = _cols(a["mla_kv_norm"][l])
        p[:, C_SSDG:C_SSDG + 4] = _cols(a["ssd_norm"][l])
        p[:, C_DSK:C_DSK + 4] = _cols(np.repeat(a["ssd_d"][l], SSD_P))
        p[:, C_GLAG] = a["gla_norm"][l]
        p[:, C_BGK:C_BGK + 2] = _cols(a["gla_b_gk"][l])
        p[:, C_DTB:C_DTB + 8] = a["ssd_dt_bias"][l][None]
        p[:, C_ALOG:C_ALOG + 8] = a["ssd_a_log"][l][None]
        p[:, C_CONV:C_CONV + 32] = a["ssd_conv_w"][l].reshape(4, 8, P).transpose(2, 1, 0).reshape(P, 32)
        p[:, C_CONVB:C_CONVB + 8] = _cols(a["ssd_conv_b"][l])
        p[:, C_FW:C_FW + 132] = a["ffn_dw_w"][l].reshape(3, FT, P).transpose(2, 1, 0).reshape(P, 132)
        p[:, C_FB:C_FB + 44] = _cols(a["ffn_dw_b"][l])
        p[MIX_GLOW:MIX_GLOW + 16, C_WGK:C_WGK + 256] = a["gla_w_gk"][l]
        params.append(p)

    consts = np.zeros((P, NCONST), f)
    i = np.arange(P)
    consts[:, K_ID:K_ID + P] = np.eye(P)
    consts[:, K_ONES:K_ONES + P] = 1
    consts[i, K_SWAP + (i ^ 32)] = 1
    consts[:, K_TRI:K_TRI + P] = i[:, None] <= i[None]
    freq = f(10000.0) ** (-np.arange(0, ROPE, 2, dtype=f) / f(ROPE))
    ang = np.arange(T, dtype=f)[:, None] * freq[None]
    consts[:, K_COS:K_COS + T] = np.cos(ang).T[i % 32]
    consts[:, K_SIN:K_SIN + T] = np.sin(ang).T[i % 32] * np.where(i % 64 < 32, -1, 1)[:, None]
    hide = np.where(i[None] <= i[:, None], 0, -1e30)
    consts[:, K_MASK:K_MASK + P] = hide
    consts[:, K_MASK + 2 * P:K_MASK + 3 * P] = hide
    masks = np.zeros((P, LEVELS * P + 2 * T), f)
    for e in range(LEVELS):
        b = GLA_CH >> (e + 1)
        masks[:, e * P:(e + 1) * P] = ((i[:, None] // (2 * b) == i[None] // (2 * b))
                                       & (i[:, None] % (2 * b) < b) & (i[None] % (2 * b) >= b))
    masks[:, LEVELS * P:] = np.arange(2 * T) % GLA_CH != 0

    gains = np.concatenate([_cols(a["attn_norm"][l]) for l in range(DEPTH)] + [_cols(a["final_norm"])], 1)
    arrays = {
        "x_in": a["x"][0].T.reshape(KT, P, T).transpose(1, 0, 2),
        "gains_in": gains,
        "params_in": np.stack(params),
        "consts_in": consts,
        "masks_in": masks,
        "front_in": np.concatenate(front),
        "out_in": np.concatenate(outw),
        "gate_in": np.concatenate(gate),
        "down_in": np.concatenate(down),
    }
    arrays = {k: np.ascontiguousarray(v) for k, v in arrays.items()}
    nc = _bacc.Bacc("TRN2", target_bir_lowering=False, num_devices=1)
    args = [nc.dram_tensor(k, v.shape, mybir.dt.from_np(v.dtype), kind="ExternalInput").ap() for k, v in arrays.items()]
    args.append(nc.dram_tensor("y_out", (P, KT, T), F32, kind="ExternalOutput").ap())
    build(nc, *args)
    r = _run(nc, [arrays], core_ids=[0])
    y = r.results[0]["y_out"]
    return y.transpose(1, 0, 2).reshape(D, T).T.reshape(1, T, D)
```

```python
import numpy as np
import concourse.bass as bass
from concourse import mybir
from contextlib import ExitStack

F32 = mybir.dt.float32
F32R = mybir.dt.float32r
U8 = mybir.dt.uint8
ALU = mybir.AluOpType
ACT = mybir.ActivationFunctionType
AX = mybir.AxisListType

P = 128
D = 2048
T = 256
DEPTH = 2
EPS = 1e-6
KT = D // P
TP = T // P
HEADS_MLA, ROPE = 8, 64
SCALE = float((128 + 64) ** -0.5)
SSD_H, SSD_P, SSD_TAPS, XBC = 8, 64, 4, 8
GLA_CH = 64
GLA_TAU = 16.0
LEVELS = 6
CONV_POOL, CONV_DVE = (0, 2, 4, 6), (1, 3, 5, 7)
FT = 44
HALF = FT // 2
FTAPS = 3

T_XBC, T_Z, T_CQ, T_CKV, T_GQ, T_GK, T_GV, T_GR, T_MIX = 0, 8, 12, 16, 18, 20, 22, 26, 30
IN_ORDER = [T_MIX, *range(T_XBC, T_XBC + 8), *range(T_GV, T_GV + 4), *range(T_GQ, T_GQ + 2), *range(T_GK, T_GK + 2),
            *range(T_CQ, T_CQ + 4), *range(T_CKV, T_CKV + 2), *range(T_Z, T_Z + 4), *range(T_GR, T_GR + 4)]
IN_TILES = 31
MIX_GLOW, MIX_DT = 64, 96

CHUNK = 16 * P
DOWN_KT = 11
DOWN_CHUNK = DOWN_KT * P
RAW, SPLIT = 2, 2

PIECES = 2
OFFSET = CHUNK // PIECES
WIDE = (CHUNK // 2, CHUNK // 2)
DOWN_KTS = (6, 5)
NARROW = (DOWN_KTS[0] * P, DOWN_KTS[1] * P)

N_MLA, N_OUT, CHUNKS = 31, 36, 204
QUADS = CHUNKS // 4
Q_GATE = (13, 32)
Q_DOWN = (24, 43)


def mla_banks(c, piece):
    if c < 3:
        return [2 * (c % 2) + piece]
    return [2, 3] if piece == 0 else [0, 1]


def out_bank(k):
    return (k + 2) % 4


def _turns():
    n, use = [0, 0, 0, 0], {}

    def turn(b, *key):
        use[key] = n[b]
        n[b] += 1

    for c in range(N_MLA):
        turn(c % 2, "in", c)
    for c in range(5):
        for piece in range(PIECES):
            for b in mla_banks(c, piece):
                turn(b, "mla", c, piece, b)
    for k in range(2 * KT):
        turn(out_bank(k), "out", k)
    for half in range(2):
        for b in range(4):
            use["gate", half, b] = n[b]
            n[b] += HALF // 2
            use["down", half, b] = n[b]
            n[b] += KT // 4
    return use, n


TURN, TURNS = _turns()
HEAD_AT = {3 * h // 2 + 1: h for h in range(HEADS_MLA)}
NORMALISE_AFTER, TRANSPOSE_AFTER, VALUES_AFTER = 1, 2, 3

C_FFN, C_QG, C_KVG, C_SSDG, C_DSK, C_GLAG, C_BGK = 0, 16, 20, 22, 26, 30, 31
C_DTB, C_ALOG, C_CONV, C_CONVB, C_FW, C_FB, C_WGK = 33, 41, 49, 81, 89, 221, 265
NPAR = C_WGK + 256

K_ID, K_ONES, K_SWAP, K_TRI, K_COS, K_SIN, K_MASK = 0, 128, 256, 384, 512, 768, 1024
NCONST = K_MASK + 384


def build(nc, x_in, gains_in, params_in, consts_in, masks_in, front_in, out_in, gate_in, down_in, y_out):
    ctx = ExitStack()
    with ctx:
        def sb(name, shape, dt=F32, where=ctx):
            return where.enter_context(nc.sbuf_tensor(name, shape, dt))

        x = sb("x", [P, KT, T])
        raw = sb("raw", [P, RAW, CHUNK])
        w_hi = sb("w_hi", [P, SPLIT, CHUNK], F32R)
        w_lo = sb("w_lo", [P, SPLIT, CHUNK], F32R)
        par = sb("par", [P, NPAR])
        const = sb("const", [P, NCONST])
        gains = sb("gains", [P, (DEPTH + 1) * KT])
        masks = sb("masks", [P, LEVELS * P + 2 * T], U8)
        ssq = sb("ssq", [P, T])
        sqt = sb("sqt", [P, T])
        rstd = sb("rstd", [P, T])
        eps = sb("eps", [P, 1])
        small = sb("small", [P, 256])

        with ExitStack() as first:
            catb_hi = sb("catb_hi", [P, 8, T], F32R, first)
            catb_lo = sb("catb_lo", [P, 8, T], F32R, first)
        with ExitStack() as second:
            e_fine = sb("e_fine", [P, 3, 2 * T], F32, second)
            q_fine = sb("q_fine", [P, 3, 2 * T], F32, second)
        sb("catb_region", [P, 16 * T])

        with ExitStack() as first:
            cata_hi = sb("cata_hi", [P, 8, T], F32R, first)
            cata_lo = sb("cata_lo", [P, 8, T], F32R, first)
        with ExitStack() as second:
            dec = sb("dec", [P, TP, SSD_H, P], F32, second)
            xdt = sb("xdt", [P, TP, SSD_H * SSD_P], F32, second)
            cea = sb("cea", [P, SSD_H, P], F32, second)
        sb("cata_region", [P, 16 * T])

        with ExitStack() as first:
            h_hi = sb("h_hi", [P, KT, T], F32R, first)
            h_lo = sb("h_lo", [P, KT, T], F32R, first)
        with ExitStack() as second:
            qn = sb("qn", [P, HEADS_MLA, T], F32, second)
            kn = sb("kn", [P, HEADS_MLA, T], F32, second)
            vv = sb("vv", [P, TP, HEADS_MLA * P], F32, second)
            qp = sb("qp", [P, HEADS_MLA // 2, T], F32, second)
            probt = sb("probt", [P, 2, 3 * P], F32, second)
        sb("h_region", [P, 2 * KT * T])

        with ExitStack() as first:
            proj = sb("proj", [P, IN_TILES, T], F32, first)
            with ExitStack() as mixers:
                xc = sb("xc", [P, XBC, T], F32, mixers)
                e_coarse = sb("e_coarse", [P, 3, 2 * T], F32, mixers)
                q_coarse = sb("q_coarse", [P, 3, 2 * T], F32, mixers)
                kq = sb("kq", [P, 2, 2 * T], F32, mixers)
                attn = sb("attn", [P, 2, 4 * P], F32, mixers)
                gm = sb("gm", [P, 4, P], F32, mixers)
                dsx = sb("dsx", [P, SSD_H * SSD_P], F32, mixers)
            with ExitStack() as start:
                x_sq = sb("x_sq", [P, KT, T], F32, start)
                masks_raw = sb("masks_raw", [P, LEVELS * P + 2 * T], F32, start)
        with ExitStack() as second:
            hid_hi = sb("hid_hi", [P, HALF, T], F32R, second)
            hid_lo = sb("hid_lo", [P, HALF, T], F32R, second)
            gs = sb("gs", [P, 2, T], F32, second)
            cv = sb("cv", [P, 2, T], F32, second)
            sl = sb("sl", [P, 2, T], F32, second)
            us = sb("us", [P, 2, T], F32, second)
            hv = sb("hv", [P, 2, T], F32, second)

        ident = const[:, K_ID:K_ID + P]
        ones = const[:, K_ONES:K_ONES + P]
        swap = const[:, K_SWAP:K_SWAP + P]
        tri = const[:, K_TRI:K_TRI + P]
        cos = const[:, K_COS:K_COS + T]
        sin = const[:, K_SIN:K_SIN + T]
        causal = const[:, K_MASK:K_MASK + 3 * P]
        keep = masks[:, LEVELS * P:LEVELS * P + 2 * T]
        bank = [ctx.enter_context(nc.psum_tensor(f"bank{i}", [P, 512], F32)) for i in range(8)]

        def scol(i, n=1):
            return small[:, i:i + n]

        def flat(ap):
            return ap.rearrange("p a t -> p (a t)")

        y_ssd = proj[:, T_XBC:T_XBC + 4, :]
        st_gla = flat(proj[:, T_XBC + 4:T_XBC + 7, :]).rearrange("p (c h n) -> p c h n", c=3, h=2)
        prob = flat(proj[:, T_XBC:T_XBC + 6, :]).rearrange("p (a n) -> p a n", n=3 * P)
        sst = flat(proj[:, T_Z:T_Z + 2, :])
        btok = proj[:, T_Z + 2, :]
        z = proj[:, T_Z:T_Z + 4, :]
        g_cum = flat(proj[:, T_GR:T_GR + 2, :])
        v_gla = flat(proj[:, T_GV:T_GV + 4, :]).rearrange("p (b n) -> p b n", b=TP)
        qs = flat(proj[:, T_GQ:T_GQ + 2, :])
        ks = flat(proj[:, T_GK:T_GK + 2, :])
        kp = proj[:, T_CQ, :]
        ropet = proj[:, T_CQ + 1:T_CQ + 5, :]
        lat_sq = xc[:, 0:6, :]
        lat_rstd = xc[:, 6:8, :]
        kd_t = gm[:].rearrange("p (b h) n -> p b h n", b=TP)
        g_raw, g_neg = e_coarse[:, 0, :], e_coarse[:, 1, :]
        tap_terms = kq[:].rearrange("p a (b t) -> p (a b) t", b=2)
        sum_rstd = dsx[:, 0:T]
        o_sq = e_coarse[:].rearrange("p a t -> p (a t)")[:, 0:1024].rearrange("p (a t) -> p a t", a=2)
        o_rstd = q_coarse[:].rearrange("p a t -> p (a t)")[:, 0:1024].rearrange("p (a t) -> p a t", a=2)
        o_y = attn

        def late(ap, e):
            half = GLA_CH >> e
            return ap.rearrange("p (g b) -> p g b", b=2 * half)[:, :, half:]

        e_levels, q_levels = (e_coarse, e_fine), (q_coarse, q_fine)

        def sem(name):
            return ctx.enter_context(nc.semaphore(name))

        s_x_loaded = [sem(f"x_loaded{i}") for i in range(4)]
        s_consts_loaded = sem("consts_loaded")
        s_masks_set = sem("masks_set")
        s_params_loaded = sem("params_loaded")
        s_params_free = sem("params_free")
        s_y_stored = sem("y_stored")
        s_eps_set = sem("eps_set")
        s_hi_ready = sem("hi_ready")
        s_lo_ready = sem("lo_ready")
        s_pieces_used = sem("pieces_used")
        s_x_ready = sem("x_ready")
        s_h_hi_ready = sem("h_hi_ready")
        s_h_ready = sem("h_ready")
        s_sq_ready = sem("sq_ready")
        s_ssq_added = sem("ssq_added")
        s_sums_ready = sem("sums_ready")
        s_rstd_log = sem("rstd_log")
        s_rstd_ready = sem("rstd_ready")
        s_conv_step = sem("conv_step")
        s_conv_ready = sem("conv_ready")
        s_silu_ready = sem("silu_ready")
        s_gate_step = sem("gate_step")
        s_gate_ready = sem("gate_ready")
        s_gate_silu = sem("gate_silu")
        s_hid_ready = sem("hid_ready")
        s_hid_hi_ready = sem("hid_hi_ready")
        s_hid_split = sem("hid_split")
        s_mla_sq = sem("mla_sq")
        s_mla_sums = sem("mla_sums")
        s_mla_log = sem("mla_log")
        s_mla_rstd = sem("mla_rstd")
        s_mla_normed = sem("mla_normed")
        s_mla_hi = sem("mla_hi")
        s_mla_split = sem("mla_split")
        s_rope_swapped = sem("rope_swapped")
        s_k_rope = sem("k_rope")
        s_k_dup = sem("k_dup")
        s_q_rope = sem("q_rope")
        s_scores_ready = sem("scores_ready")
        s_masked = sem("masked")
        s_prob_ready = sem("prob_ready")
        s_prob_norm = sem("prob_norm")
        s_probt_ready = sem("probt_ready")
        s_probt_copied = sem("probt_copied")
        s_o_ready = sem("o_ready")
        s_o_hi = sem("o_hi")
        s_o_lo = sem("o_lo")
        s_dt_t = sem("dt_t")
        s_xs_t = sem("xs_t")
        s_dt_abs = sem("dt_abs")
        s_dt_exp = sem("dt_exp")
        s_dt_log = sem("dt_log")
        s_neg_a = sem("neg_a")
        s_a_ready = sem("a_ready")
        s_xdt_ready = sem("xdt_ready")
        s_btok_ready = sem("btok_ready")
        s_ta_ready = sem("ta_ready")
        s_acum_ready = sem("acum_ready")
        s_acum_copied = sem("acum_copied")
        s_cumb_ready = sem("cumb_ready")
        s_seg_ready = sem("seg_ready")
        s_seg_exp = sem("seg_exp")
        s_ea_exp = sem("ea_exp")
        s_ds_exp = sem("ds_exp")
        s_cb_ready = sem("cb_ready")
        s_m_ready = sem("m_ready")
        s_cea_ready = sem("cea_ready")
        s_dsx_ready = sem("dsx_ready")
        s_state_ready = sem("state_ready")
        s_state_copied = sem("state_copied")
        s_y_ready = sem("y_ready")
        s_y_gated = sem("y_gated")
        s_y_sq = sem("y_sq")
        s_y_sums = sem("y_sums")
        s_y_log = sem("y_log")
        s_y_rstd = sem("y_rstd")
        s_y_normed = sem("y_normed")
        s_y_hi = sem("y_hi")
        s_ssd_cat = sem("ssd_cat")
        s_vec_step = sem("vec_step")
        s_gl_pre = sem("gl_pre")
        s_gl_v = sem("gl_v")
        s_gl_neg = sem("gl_neg")
        s_gl_exp = sem("gl_exp")
        s_gl_log = sem("gl_log")
        s_gl_diff = sem("gl_diff")
        s_gl_e = sem("gl_e")
        s_gl_qs = sem("gl_qs")
        s_gl_vcopied = sem("gl_vcopied")
        s_gl_q = sem("gl_q")
        s_gl_k = sem("gl_k")
        s_gl_kt = sem("gl_kt")
        s_gl_ktc = sem("gl_ktc")
        s_gl_zero = sem("gl_zero")
        s_gl_lvl = sem("gl_lvl")
        s_gl_put = sem("gl_put")
        s_gl_u = sem("gl_u")
        s_gl_s = sem("gl_s")
        s_gl_o = sem("gl_o")
        s_gl_osq = sem("gl_osq")
        s_gl_osum = sem("gl_osum")
        s_gl_olog = sem("gl_olog")
        s_gl_orstd = sem("gl_orstd")
        s_gl_y = sem("gl_y")
        s_gl_hi = sem("gl_hi")
        s_gl_cat = sem("gl_cat")
        s_gl_scan = sem("gl_scan")
        s_final_ready = sem("final_ready")
        s_passed_act = sem("passed_act")
        s_passed_dve = sem("passed_dve")
        s_passed_pe = sem("passed_pe")
        s_gains_loaded = sem("gains_loaded")
        s_start_sq = sem("start_sq")
        s_start_sum = sem("start_sum")
        s_passed_pool = sem("passed_pool")
        s_conv_sum = sem("conv_sum")
        s_masks_loaded = sem("masks_loaded")
        s_start_hi = sem("start_hi")
        s_in_taken = sem("in_taken")
        s_y_skip = sem("y_skip")
        s_gl_kq = sem("gl_kq")
        s_gl_kqd = sem("gl_kqd")
        s_gl_kd = sem("gl_kd")
        s_gl_qe = sem("gl_qe")
        s_ssq_zeroed = sem("ssq_zeroed")
        raw_landed = [sem(f"raw_landed{i}") for i in range(RAW * PIECES)]
        bank_free = [sem(f"bank_free{i}") for i in range(4)]

        def mla_evac(engine, on_act, L, c0, c, piece):
            if on_act != (c > 0):
                return
            copy = nc.scalar.copy if on_act else nc.vector.tensor_copy
            engine.wait_ge(s_pieces_used, (c0 + N_MLA + c) * PIECES + (piece + 1 + SPLIT * PIECES))
            for n, b in enumerate(mla_banks(c, piece)):
                source, two = bank[b][:, :], bank[b][:, :].rearrange("p (a t) -> p a t", a=2)
                if c == 0:
                    copy(qp[:, 2 * piece:2 * piece + 2, :], two).then_inc(bank_free[b], 1)
                elif c < 3:
                    at = 4 * (c - 1) + 2 * piece
                    copy(qn[:, at:at + 2, :], two).then_inc(bank_free[b], 1)
                elif c == 3:
                    at = 4 * piece + 2 * n
                    copy(kn[:, at:at + 2, :], two).then_inc(bank_free[b], 1)
                else:
                    copy(vv[:, n, piece * 512:piece * 512 + 512], source).then_inc(bank_free[b], 1)

        block = ctx.enter_context(nc.Block())

        @block.sync
        def _(sp):
            def load(source, row, chunk, j, widths=WIDE, pieces=range(PIECES)):
                for piece in pieces:
                    sp.wait_ge(s_lo_ready, chunk * PIECES + (piece + 1))
                    first, n = widths[0] * piece, widths[piece]
                    sp.dma_start(raw[:, j % RAW, OFFSET * piece:OFFSET * piece + n],
                                 source[bass.ds(row, 1), :, first:first + n].rearrange("a p n -> p (a n)")
                                 ).then_inc(raw_landed[PIECES * (j % RAW) + piece], 16)

            sp.dma_start(gains[:], gains_in).then_inc(s_gains_loaded, 16)
            for k in range(4):
                at = slice(4 * k, 4 * k + 4)
                sp.dma_start(x[:, at, :], x_in[:, at, :]).then_inc(s_x_loaded[k], 16)
                if k == 1:
                    load(front_in, 0, 0, 0, pieces=(0,))
            load(front_in, 0, 0, 0, pieces=(1,))
            load(front_in, 1, 1, 1)

            with sp.Fori(0, DEPTH) as L:
                c0 = L * CHUNKS
                sp.wait_ge(s_params_free, L + 1)
                sp.dma_start(par[:], params_in[bass.ds(L, 1), :, :].rearrange("a p n -> p (a n)")).then_inc(s_params_loaded, 16)
                for j in (2, 3):
                    load(front_in, L * N_OUT + j, c0 + j, j)
                with sp.Fori(1, N_OUT // 4) as i:
                    for j in range(4):
                        load(front_in, L * N_OUT + i * 4 + j, c0 + i * 4 + j, j)
                with sp.Fori(0, 4) as i:
                    for j in range(4):
                        load(out_in, L * 16 + i * 4 + j, c0 + N_OUT + i * 4 + j, j)
                for half in range(2):
                    with sp.Fori(0, 11) as i:
                        for j in range(4):
                            load(gate_in, L * 88 + half * 44 + i * 4 + j, c0 + Q_GATE[half] * 4 + i * 4 + j, j)
                    with sp.Fori(0, 8) as i:
                        for j in range(4):
                            load(down_in, L * 64 + half * 32 + i * 4 + j, c0 + Q_DOWN[half] * 4 + i * 4 + j, j, NARROW)
                for j in (0, 1):
                    load(front_in, L * N_OUT + (N_OUT + j), c0 + (CHUNKS + j), j)
            for k in range(4):
                sp.wait_ge(s_final_ready, 4 * k + 4)
                sp.dma_start(y_out[:, 4 * k:4 * k + 4, :], x[:, 4 * k:4 * k + 4, :]).then_inc(s_y_stored, 16)
            sp.wait_ge(s_y_stored, 64)

        @block.gpsimd
        def _(pool):
            for k in range(4):
                at = slice(4 * k, 4 * k + 4)
                pool.wait_ge(s_x_loaded[k], 16)
                nc.gpsimd.tensor_tensor(x_sq[:, at, :], x[:, at, :], x[:, at, :], ALU.mult).then_inc(s_start_sq, 1)
                if k == 1:
                    pool.dma_start(const[:], consts_in).then_inc(s_consts_loaded, 16)
            pool.dma_start(masks_raw[:], masks_in).then_inc(s_masks_loaded, 16)
            pool.wait_ge(s_start_sq, 4)
            nc.gpsimd.tensor_tensor(x_sq[:, 8:12, :], x_sq[:, 8:12, :], x_sq[:, 12:16, :], ALU.add).then_inc(s_start_sum, 1)
            pool.wait_ge(s_start_sum, 2)
            nc.gpsimd.tensor_tensor(x_sq[:, 0:4, :], x_sq[:, 0:4, :], x_sq[:, 8:12, :], ALU.add).then_inc(s_start_sum, 1)
            pool.wait_ge(s_start_sum, 3)
            nc.gpsimd.tensor_tensor(x_sq[:, 0:2, :], x_sq[:, 0:2, :], x_sq[:, 2:4, :], ALU.add).then_inc(s_start_sum, 1)
            pool.wait_ge(s_start_sum, 4)
            nc.gpsimd.tensor_tensor(ssq[:], x_sq[:, 0, :], x_sq[:, 1, :], ALU.add).then_inc(s_ssq_added, 1)
            pool.wait_ge(s_masks_loaded, 16)
            nc.gpsimd.tensor_copy(masks[:], masks_raw[:]).then_inc(s_masks_set, 1)

            with pool.Fori(0, DEPTH) as L:
                for n, t in enumerate(CONV_POOL):
                    before = (L * len(CONV_POOL) + n) * (2 * SSD_TAPS - 1)
                    pool.wait_ge(s_in_taken, IN_TILES * L + (t + 2))
                    pool.sem_inc(s_passed_pool, 1)
                    for k in range(SSD_TAPS):
                        at = C_CONV + SSD_TAPS * t + SSD_TAPS - 1 - k
                        tap = par[:, at:at + 1]
                        if k == 0:
                            ins = nc.gpsimd.tensor_scalar(xc[:, t, :], proj[:, t, :], tap, par[:, C_CONVB + t:C_CONVB + t + 1],
                                                          ALU.mult, ALU.add)
                        else:
                            ins = nc.gpsimd.tensor_scalar(tap_terms[:, k, :], proj[:, t, :], tap, None, ALU.mult)
                        ins.then_inc(s_conv_sum, 1)
                    for k in range(1, SSD_TAPS):
                        pool.wait_ge(s_conv_sum, before + (SSD_TAPS + k - 1))
                        nc.gpsimd.tensor_tensor(xc[:, t, k:T], xc[:, t, k:T], tap_terms[:, k, 0:T - k],
                                                ALU.add).then_inc(s_conv_sum, 1)
                    pool.wait_ge(s_conv_sum, before + (2 * SSD_TAPS - 1))
                    pool.sem_inc(s_conv_ready, 1)
                pool.wait_ge(s_y_gated, L + 1)
                nc.gpsimd.tensor_tensor(z, y_ssd, y_ssd, ALU.mult).then_inc(s_y_sq, 1)

        @block.scalar
        def _(act):
            def hi(chunk, quad, j, piece, widths=WIDE):
                act.wait_ge(raw_landed[PIECES * (j % RAW) + piece], quad * 32 + 16 * (j // RAW + 1))
                act.wait_ge(s_pieces_used, chunk * PIECES + (piece + 1))
                slot = slice(OFFSET * piece, OFFSET * piece + widths[piece])
                nc.scalar.copy(w_hi[:, j % SPLIT, slot], raw[:, j % RAW, slot]).then_inc(s_hi_ready, 1)

            def refresh(tile, nth, gain):
                act.wait_ge(s_x_ready, nth + 1)
                act.sem_inc(s_passed_act, 1)
                nc.scalar.activation(h_hi[:, bass.ds(tile, 1), :], x[:, bass.ds(tile, 1), :], ACT.Copy,
                                     scale=gain).then_inc(s_h_hi_ready, 1)
                act.wait_ge(s_ssq_added, nth + 1)
                act.sem_inc(s_passed_act, 1)
                nc.scalar.activation(sqt[:], x[:, bass.ds(tile, 1), :].rearrange("p a t -> p (a t)"),
                                     ACT.Square).then_inc(s_sq_ready, 1)

            def token_rstd(nth):
                act.wait_ge(s_sums_ready, nth + 1)
                nc.scalar.activation(rstd[:], bank[4][:, 0:T], ACT.Ln, bias=eps[:], scale=1.0 / D).then_inc(s_rstd_log, 1)
                act.wait_ge(s_rstd_log, nth + 1)
                nc.scalar.activation(rstd[:], rstd[:], ACT.Exp, scale=-0.5).then_inc(s_rstd_ready, 1)

            act.wait_ge(s_gains_loaded, 16)
            for k in range(KT):
                if k % 4 == 0:
                    act.wait_ge(s_x_loaded[k // 4], 16)
                nc.scalar.activation(h_hi[:, k, :], x[:, k, :], ACT.Copy, scale=gains[:, k:k + 1]).then_inc(s_start_hi, 1)
                if k % 8 == 7:
                    hi(0, 0, 0, k // 8)
            hi(1, 0, 1, 0)
            hi(1, 0, 1, 1)
            act.wait_ge(s_eps_set, 1)
            act.sem_inc(s_passed_act, 1)

            with act.Fori(0, DEPTH) as L:
                c0, q0 = L * CHUNKS, L * QUADS

                def ahead(s, piece):
                    s += 2
                    hi(c0 + s, q0 + s // 4, s % 4, piece)

                def head_weights(h):
                    act.wait_ge(s_masked, 8 * L + h + 1)
                    for qb, first, end in ((0, 0, P), (1, P, 3 * P)):
                        nc.scalar.activation(prob[:, h % 4, first:end], prob[:, h % 4, first:end], ACT.Exp, scale=SCALE,
                                             bias=scol(192 + 2 * h + qb), accum_out=scol(224 + 2 * h + qb)).then_inc(s_prob_ready, 1)

                def head_transposed(h):
                    act.wait_ge(s_probt_ready, 8 * L + h + 1)
                    if h >= 2:
                        act.wait_ge(s_o_ready, 8 * L + h - 1)
                    nc.scalar.copy(probt[:, h % 2, :], bank[6][:, 0:3 * P]).then_inc(s_probt_copied, 1)

                def head_out(h):
                    act.wait_ge(s_o_ready, 8 * L + h + 1)
                    nc.scalar.copy(cata_hi[:, h, :], bank[7][:, 0:T]).then_inc(s_o_hi, 1)

                for s in range(N_OUT):
                    ahead(s, 0)
                    if s == 0:
                        token_rstd(L * 2)
                    if s >= N_MLA:
                        mla_evac(act, True, L, c0, s - N_MLA, 0)
                    ahead(s, 1)
                    if s >= N_MLA:
                        mla_evac(act, True, L, c0, s - N_MLA, 1)
                    if s == 2:
                        act.wait_ge(s_params_loaded, 16 * (L + 1))
                        nc.scalar.activation(scol(64, 8), par[:, C_ALOG:C_ALOG + 8], ACT.Exp).then_inc(s_neg_a, 1)
                    if s == 3:
                        act.wait_ge(s_dt_abs, L + 1)
                        nc.scalar.activation(scol(32, 16), scol(16, 16), ACT.Exp).then_inc(s_dt_exp, 1)
                        act.wait_ge(s_dt_exp, L + 1)
                        nc.scalar.activation(scol(48, 16), scol(32, 16), ACT.Ln, bias=1.0).then_inc(s_dt_log, 1)
                    if s == 7:
                        act.wait_ge(s_seg_ready, 4 * L + 2)
                        nc.scalar.activation(scol(128, 8), scol(120, 8), ACT.Exp).then_inc(s_ds_exp, 1)
                        nc.scalar.activation(dec[:, 0], dec[:, 0], ACT.Exp).then_inc(s_seg_exp, 1)
                    if s == 8:
                        act.wait_ge(s_seg_ready, 4 * L + 4)
                        nc.scalar.activation(dec[:, 1], dec[:, 1], ACT.Exp).then_inc(s_seg_exp, 1)
                        for g, b in ((0, 7), (1, 4)):
                            nc.scalar.activation(cea[:, 4 * g:4 * g + 4, :], bank[b][:, :].rearrange("p (h t) -> p h t", h=4),
                                                 ACT.Exp).then_inc(s_ea_exp, 1)
                    if s == 9:
                        act.wait_ge(s_conv_ready, 8 * (L + 1))
                        nc.scalar.activation(xc[:], xc[:], ACT.Silu).then_inc(s_silu_ready, 1)
                    if s == 10:
                        act.wait_ge(s_gl_neg, L + 1)
                        nc.scalar.activation(g_neg, g_neg, ACT.Exp).then_inc(s_gl_exp, 1)
                        act.wait_ge(s_gl_exp, L + 1)
                        nc.scalar.activation(g_neg, g_neg, ACT.Ln, bias=1.0).then_inc(s_gl_log, 1)
                    if s == 11:
                        act.wait_ge(s_xs_t, 3 * (L + 1))
                        nc.scalar.copy(btok, bank[7][:, 0:256]).then_inc(s_btok_ready, 1)
                    if s == 14:
                        act.wait_ge(s_state_ready, L + 1)
                        nc.scalar.copy(sst, bank[5][:, :]).then_inc(s_state_copied, 1)
                        act.wait_ge(s_gl_v, L + 1)
                        for c in range(TP):
                            nc.scalar.copy(v_gla[:, c, :], bank[2 + c][:, :]).then_inc(s_gl_vcopied, 1)
                        act.wait_ge(s_gl_diff, 2 * L + 1)
                        nc.scalar.activation(e_coarse[:], e_coarse[:], ACT.Exp, scale=1.0 / GLA_TAU).then_inc(s_gl_e, 1)
                    if s == 15:
                        act.wait_ge(s_gl_kqd, L + 1)
                        nc.scalar.activation(kq[:], kq[:], ACT.Exp, scale=1.0 / GLA_TAU).then_inc(s_gl_kq, 1)
                        act.wait_ge(s_in_taken, IN_TILES * L + 15)
                        nc.scalar.activation(qs, qs, ACT.Copy, scale=GLA_CH ** -0.5).then_inc(s_gl_qs, 1)
                    if s == 16:
                        act.wait_ge(s_gl_diff, 2 * L + 2)
                        nc.scalar.activation(e_fine[:], e_fine[:], ACT.Exp, scale=1.0 / GLA_TAU).then_inc(s_gl_e, 1)
                    if s == 19:
                        act.wait_ge(s_gl_kt, L + 1)
                        nc.scalar.copy(kd_t, bank[2][:, :].rearrange("p (b h n) -> p b h n", b=TP, h=2)).then_inc(s_gl_ktc, 1)
                    if s == 23:
                        act.wait_ge(s_in_taken, IN_TILES * L + 23)
                        act.wait_ge(s_y_skip, L + 1)
                        nc.scalar.activation(lat_sq, proj[:, T_CQ:T_CQ + 6, :], ACT.Square).then_inc(s_mla_sq, 1)
                    if s == 25:
                        act.wait_ge(s_mla_sums, L + 1)
                        nc.scalar.activation(lat_rstd[:, 0, :], bank[3][:, 0:T], ACT.Ln, bias=eps[:], scale=1.0 / 512).then_inc(s_mla_log, 1)
                        nc.scalar.activation(lat_rstd[:, 1, :], bank[3][:, T:2 * T], ACT.Ln, bias=eps[:], scale=1.0 / 256).then_inc(s_mla_log, 1)
                        act.wait_ge(s_mla_log, 2 * (L + 1))
                        nc.scalar.activation(lat_rstd, lat_rstd, ACT.Exp, scale=-0.5).then_inc(s_mla_rstd, 1)
                    if s == 27:
                        for k in range(6):
                            act.wait_ge(s_mla_normed, 2 * L + (1 if k < 4 else 2))
                            nc.scalar.activation(cata_hi[:, k, :], proj[:, T_CQ + k, :], ACT.Copy,
                                                 scale=par[:, C_QG + k:C_QG + k + 1]).then_inc(s_mla_hi, 1)
                        act.wait_ge(s_gl_o, L + 1)
                        for q in range(2):
                            nc.scalar.activation(o_sq[:, q, :], bank[4 + q][:, :], ACT.Square).then_inc(s_gl_osq, 1)
                    if s == 28:
                        act.wait_ge(s_in_taken, IN_TILES * L + 27)
                        nc.scalar.activation(z, z, ACT.Silu).then_inc(s_silu_ready, 1)
                    if s == 29:
                        act.wait_ge(s_gl_osum, L + 1)
                        for q in range(2):
                            nc.scalar.activation(o_rstd[:, q, :], bank[6 + q][:, :], ACT.Ln, bias=eps[:],
                                                 scale=1.0 / P).then_inc(s_gl_olog, 1)
                        act.wait_ge(s_gl_olog, 2 * (L + 1))
                        nc.scalar.activation(o_rstd, o_rstd, ACT.Exp, scale=-0.5).then_inc(s_gl_orstd, 1)
                    if s == 30:
                        act.wait_ge(s_in_taken, IN_TILES * (L + 1))
                        nc.scalar.activation(proj[:, T_GR:T_GR + 4, :], proj[:, T_GR:T_GR + 4, :], ACT.Silu).then_inc(s_silu_ready, 1)
                    if s == 31:
                        act.wait_ge(s_k_rope, L + 1)
                        nc.scalar.copy(kp[64:128, :], kp[0:64, :]).then_inc(s_k_dup, 1)
                        act.wait_ge(s_y_sums, L + 1)
                        nc.scalar.activation(sum_rstd, bank[6][:, 0:T], ACT.Ln, bias=eps[:], scale=1.0 / 512).then_inc(s_y_log, 1)
                        act.wait_ge(s_y_log, L + 1)
                        nc.scalar.activation(sum_rstd, sum_rstd, ACT.Exp, scale=-0.5).then_inc(s_y_rstd, 1)
                    if s == 32:
                        act.wait_ge(s_gl_y, L + 1)
                        nc.scalar.copy(catb_hi[:, 4:8, :].rearrange("p (h q) t -> p q h t", q=2),
                                       o_y.rearrange("p q (h t) -> p q h t", h=2)).then_inc(s_gl_hi, 1)
                    if s == 33:
                        act.wait_ge(s_y_normed, L + 1)
                        for k in range(4):
                            nc.scalar.activation(catb_hi[:, k, :], y_ssd[:, k, :], ACT.Copy,
                                                 scale=par[:, C_SSDG + k:C_SSDG + k + 1]).then_inc(s_y_hi, 1)

                for k in range(2 * KT):
                    if k in HEAD_AT:
                        head_weights(HEAD_AT[k])
                    if k - TRANSPOSE_AFTER in HEAD_AT:
                        head_transposed(HEAD_AT[k - TRANSPOSE_AFTER])
                    if k - VALUES_AFTER in HEAD_AT:
                        head_out(HEAD_AT[k - VALUES_AFTER])
                    ahead(N_OUT + k // 2, k % 2)
                    if k >= KT:
                        refresh(k - KT, L * 2 * KT + k - KT, par[:, C_FFN + k - KT:C_FFN + k - KT + 1])

                for half in range(2):
                    def gate_hi(i, j, piece, widths=WIDE):
                        quad = q0 + Q_GATE[half] + i
                        hi(quad * 4 + j + 2, quad + (j + 2) // 4, (j + 2) % 4, piece, widths)

                    def gate_silu(i, f):
                        act.wait_ge(s_gate_ready, L * FT + (half * HALF + f + 1) + i * 2)
                        nc.scalar.activation(sl[:, f % 2, :], cv[:, f % 2, :], ACT.Silu).then_inc(s_gate_silu, 1)

                    def hidden_hi(i, f):
                        act.wait_ge(s_hid_ready, L * FT + (half * HALF + f + 1) + i * 2)
                        nc.scalar.copy(hid_hi[:, bass.ds(i * 2 + f, 1), :], hv[:, f % 2:f % 2 + 1, :]).then_inc(s_hid_hi_ready, 1)

                    gate_hi(0, 0, 0)
                    if half == 0:
                        token_rstd(L * 2 + 1)
                    gate_hi(0, 0, 1)
                    gate_hi(0, 1, 0)
                    act.sem_inc(s_passed_act, 1)
                    with act.Fori(0, 10) as i:
                        for f in range(2):
                            gate_silu(i, f)
                            gate_hi(i, 2 * f + 1, 1)
                            gate_hi(i, 2 * f + 2, 0)
                            gate_hi(i, 2 * f + 2, 1)
                            hidden_hi(i, f)
                            gate_hi(i, 2 * f + 3, 0)
                    gate_silu(10, 0)
                    gate_hi(10, 1, 1)
                    gate_hi(10, 2, 0, NARROW)
                    gate_hi(10, 2, 1, NARROW)
                    hidden_hi(10, 0)
                    gate_hi(10, 3, 0, NARROW)
                    gate_silu(10, 1)
                    gate_hi(10, 3, 1, NARROW)
                    hidden_hi(10, 1)

                    def down_chunk(i, jj, widths):
                        quad = q0 + Q_DOWN[half] + i * 2
                        at = (quad * 4 + jj + 2, quad + (jj + 2) // 4, (jj + 2) % 4)
                        hi(*at, 0, widths)
                        if half == 1 and jj % 2 == 1:
                            m = i * 4 + jj // 2
                            refresh(m, L * 2 * KT + KT + m, gains[:, bass.ds((L + 1) * KT + m, 1)])
                        hi(*at, 1, widths)

                    act.sem_inc(s_passed_act, 1)
                    with act.Fori(0, 3) as i:
                        for jj in range(8):
                            down_chunk(i, jj, NARROW)
                    for jj in range(8):
                        down_chunk(3, jj, NARROW if jj < 6 else WIDE)

            token_rstd(2 * DEPTH)

        @block.vector
        def _(dve):
            def lo(chunk, j, piece, widths=WIDE):
                dve.wait_ge(s_hi_ready, chunk * PIECES + (piece + 1))
                slot = slice(OFFSET * piece, OFFSET * piece + widths[piece])
                nc.vector.tensor_tensor(w_lo[:, j % SPLIT, slot], raw[:, j % RAW, slot],
                                        w_hi[:, j % SPLIT, slot].bitcast(F32), ALU.subtract).then_inc(s_lo_ready, 1)

            def refresh(tile, nth, gain):
                at = bass.ds(tile, 1)
                dve.wait_ge(s_h_hi_ready, nth + 1)
                nc.vector.scalar_tensor_tensor(out=h_lo[:, at, :], in0=x[:, at, :], scalar=gain,
                                               in1=h_hi[:, at, :].bitcast(F32), op0=ALU.mult,
                                               op1=ALU.subtract).then_inc(s_h_ready, 1)
                dve.wait_ge(s_sq_ready, nth + 1)
                dve.wait_ge(s_ssq_added, nth + 1)
                nc.vector.tensor_tensor(ssq[:], ssq[:], sqt[:], ALU.add).then_inc(s_ssq_added, 1)

            nc.vector.memset(eps[:], EPS).then_inc(s_eps_set, 1)
            dve.sem_inc(s_lo_ready, RAW * PIECES)
            dve.sem_inc(s_params_free, 1)
            for b in range(4):
                dve.sem_inc(bank_free[b], 1)
            dve.wait_ge(s_gains_loaded, 16)
            for k in range(KT):
                dve.wait_ge(s_start_hi, k + 1)
                nc.vector.scalar_tensor_tensor(out=h_lo[:, k, :], in0=x[:, k, :], scalar=gains[:, k:k + 1],
                                               in1=h_hi[:, k, :].bitcast(F32), op0=ALU.mult,
                                               op1=ALU.subtract).then_inc(s_h_ready, 1)
                if k % 8 == 7:
                    lo(0, 0, k // 8)
            dve.wait_ge(s_start_sq, 2)
            nc.vector.tensor_tensor(x_sq[:, 0:4, :], x_sq[:, 0:4, :], x_sq[:, 4:8, :], ALU.add).then_inc(s_start_sum, 1)
            lo(1, 1, 0)
            lo(1, 1, 1)

            class Steps:
                def __init__(self, counted, before):
                    self.counted, self.before, self.n = counted, before, 0

                def step(self, ins):
                    ins.then_inc(self.counted, 1)
                    self.n += 1

                def settle(self):
                    dve.wait_ge(self.counted, self.before + self.n)

            with dve.Fori(0, DEPTH) as L:
                c0 = L * CHUNKS
                vec = Steps(s_vec_step, L * VEC_STEPS)
                step, settle = vec.step, vec.settle

                def ahead(s, piece):
                    lo(c0 + s + 2, s + 2, piece)

                def after_piece(chunk, piece):
                    dve.wait_ge(s_pieces_used, (c0 + chunk) * PIECES + (piece + 1 + SPLIT * PIECES))

                def take(s):
                    after_piece(s, 1)
                    nc.vector.tensor_tensor(proj[:, IN_ORDER[s], :], bank[s % 2][:, 0:T], rstd[:],
                                            ALU.mult).then_inc(bank_free[s % 2], 1)
                    dve.wait_ge(bank_free[s % 2], L * TURNS[s % 2] + (TURN["in", s] + 2))
                    dve.sem_inc(s_in_taken, 1)

                def convolve(n):
                    t = CONV_DVE[n]
                    for k in range(SSD_TAPS):
                        at = C_CONV + SSD_TAPS * t + SSD_TAPS - 1 - k
                        tap = par[:, at:at + 1]
                        if k == 0:
                            nc.vector.tensor_scalar(xc[:, t, :], proj[:, t, :], tap, par[:, C_CONVB + t:C_CONVB + t + 1],
                                                    ALU.mult, ALU.add).then_inc(s_conv_step, 1)
                        else:
                            dve.wait_ge(s_conv_step, (L * len(CONV_DVE) + n) * 3 + k)
                            nc.vector.scalar_tensor_tensor(
                                out=xc[:, t, k:T], in0=proj[:, t, 0:T - k], scalar=tap, in1=xc[:, t, k:T],
                                op0=ALU.mult, op1=ALU.add).then_inc(s_conv_step if k < 3 else s_conv_ready, 1)

                two8 = lambda ap: ap.rearrange("p (c h) -> p c h", c=TP)
                heads = lambda ap: ap.rearrange("p (h q) -> p h q", h=8)

                def segments(c):
                    for g in range(2):
                        b = bank[(5, 6, 7, 4)[2 * c + g]]
                        dve.wait_ge(s_cumb_ready, 4 * L + 2 * c + g + 1)
                        for h in range(4):
                            step(nc.vector.tensor_scalar(dec[:, c, 4 * g + h, :], b[:, h * P:(h + 1) * P],
                                                         scol(144 + 8 * c + 4 * g + h), 0.0, ALU.subtract, ALU.min))
                        if c == 0:
                            step(nc.vector.tensor_tensor(scol(120 + 4 * g, 4),
                                                         b[:, :].rearrange("p (h t) -> p h t", h=4)[:, :, P - 1],
                                                         scol(144 + 4 * g, 4), ALU.subtract))
                        settle()
                        dve.sem_inc(s_seg_ready, 1)

                def level_distances(batch):
                    for e in range(3):
                        size = GLA_CH >> (3 * batch + e + 1)
                        g_v = g_cum.rearrange("p (n b) -> p n b", b=2 * size)
                        e_v = e_levels[batch][:, e, :].rearrange("p (n b) -> p n b", b=2 * size)
                        ref = g_v[:, :, size - 1:size].to_broadcast([P, 2 * T // (2 * size), size])
                        step(nc.vector.tensor_tensor(e_v[:, :, size:], g_v[:, :, size:], ref, ALU.subtract))
                        step(nc.vector.tensor_tensor(e_v[:, :, :size], ref, g_v[:, :, :size], ALU.subtract))
                    settle()
                    dve.sem_inc(s_gl_diff, 1)

                def level_queries(batch):
                    dve.wait_ge(s_gl_e, 2 * L + batch + 1)
                    dve.wait_ge(s_gl_qs, L + 1)
                    nc.vector.tensor_tensor(q_levels[batch][:], e_levels[batch][:], qs.unsqueeze(1).to_broadcast([P, 3, 2 * T]),
                                            ALU.mult).then_inc(s_gl_q, 1)

                def level_keys(batch):
                    dve.wait_ge(s_gl_q, 2 * L + batch + 1)
                    nc.vector.tensor_tensor(e_levels[batch][:], e_levels[batch][:], ks.unsqueeze(1).to_broadcast([P, 3, 2 * T]),
                                            ALU.mult).then_inc(s_gl_k, 1)

                def place_level(e):
                    n = P if e == 0 else P // 2
                    which = ident.bitcast(mybir.dt.int32) if e == 0 else late(masks[:, (e - 1) * P:e * P], e)
                    for q in range(2):
                        dve.wait_ge(s_gl_lvl, 14 * L + 2 * e + q + 1)
                        if e:
                            dve.wait_ge(s_gl_put, 14 * L + 2 * e - 1 + q)
                        else:
                            dve.wait_ge(s_gl_zero, L + 1)
                        dve.sem_inc(s_passed_dve, 1)
                        to, scores = attn[:, q, :], bank[4 + 2 * (e % 2) + q][:, 0:4 * n]
                        if e == 0:
                            nc.vector.copy_predicated(to.rearrange("p (n t) -> p n t", n=4),
                                                      which.unsqueeze(1).to_broadcast([P, 4, P]),
                                                      scores.rearrange("p (n t) -> p n t", n=4)).then_inc(s_gl_put, 1)
                        else:
                            half = GLA_CH >> e
                            blocks = P // (2 * half)
                            nc.vector.copy_predicated(
                                to.rearrange("p (n g b) -> p n g b", n=4, b=2 * half)[:, :, :, half:],
                                which.unsqueeze(1).to_broadcast([P, 4, blocks, half]),
                                scores.rearrange("p (n g b) -> p n g b", n=4, b=half)).then_inc(s_gl_put, 1)

                def gla_state(c):
                    b = bank[2 + c % 2]
                    dve.wait_ge(s_gl_u, 3 * L + c + 1)
                    for hp in range(2):
                        for q in range(2):
                            rows = slice(64 * q, 64 * q + 64)
                            new = b[rows, hp * 256 + q * P:hp * 256 + q * P + P]
                            if c == 0:
                                step(nc.vector.tensor_copy(st_gla[rows, 0, hp, :], new))
                            else:
                                step(nc.vector.scalar_tensor_tensor(
                                    out=st_gla[rows, c, hp, :], in0=st_gla[rows, c - 1, hp, :],
                                    scalar=small[rows, 176 + 4 * hp + c:177 + 4 * hp + c], in1=new,
                                    op0=ALU.mult, op1=ALU.add))
                    settle()
                    dve.sem_inc(s_gl_s, 1)

                def head_scores(h):
                    dve.wait_ge(s_scores_ready, 8 * L + h + 1)
                    if h >= 4:
                        dve.wait_ge(s_probt_ready, 8 * L + h - 3)
                    row = prob[:, h % 4, :]
                    step(nc.vector.tensor_tensor(row, bank[4 + h % 2][:, 0:3 * P], causal, ALU.add))
                    settle()
                    step(nc.vector.reduce_max(scol(208 + 2 * h), row[:, 0:P], AX.X))
                    step(nc.vector.reduce_max(scol(209 + 2 * h), row[:, P:3 * P], AX.X))
                    settle()
                    nc.vector.tensor_scalar(scol(192 + 2 * h, 2), scol(208 + 2 * h, 2), -SCALE, None, ALU.mult).then_inc(s_masked, 1)

                def head_normalise(h):
                    dve.wait_ge(s_prob_ready, 16 * L + 2 * h + 2)
                    row = prob[:, h % 4, :]
                    step(nc.vector.reciprocal(scol(240 + 2 * (h % 4), 2), scol(224 + 2 * h, 2)))
                    settle()
                    step(nc.vector.tensor_scalar(row[:, 0:P], row[:, 0:P], scol(240 + 2 * (h % 4)), None, ALU.mult))
                    settle()
                    nc.vector.tensor_scalar(row[:, P:3 * P], row[:, P:3 * P], scol(241 + 2 * (h % 4)), None, ALU.mult).then_inc(s_prob_norm, 1)

                def head_out(h):
                    dve.wait_ge(s_o_hi, 8 * L + h + 1)
                    nc.vector.tensor_tensor(cata_lo[:, h, :], bank[7][:, 0:T], cata_hi[:, h, :].bitcast(F32),
                                            ALU.subtract).then_inc(s_o_lo, 1)

                dve.wait_ge(s_params_loaded, 16 * (L + 1))

                for s in range(N_OUT):
                    ahead(s, 0)
                    if s == 0:
                        dve.wait_ge(s_rstd_ready, 2 * L + 1)
                    if s < N_MLA:
                        take(s)
                    else:
                        mla_evac(dve, False, L, c0, s - N_MLA, 0)
                    ahead(s, 1)
                    if s >= N_MLA:
                        mla_evac(dve, False, L, c0, s - N_MLA, 1)
                    if s == 2:
                        dve.wait_ge(s_dt_t, L + 1)
                        step(nc.vector.tensor_tensor(two8(scol(0, 16)), two8(bank[4][:, 0:16]),
                                                     par[:, C_DTB:C_DTB + 8].unsqueeze(1).to_broadcast([P, TP, 8]), ALU.add))
                        settle()
                        nc.vector.scalar_tensor_tensor(out=scol(16, 16), in0=scol(0, 16), scalar=-1.0, in1=scol(0, 16),
                                                       op0=ALU.mult, op1=ALU.min).then_inc(s_dt_abs, 1)
                    if s == 3:
                        convolve(0)
                    if s == 4:
                        dve.wait_ge(s_dt_log, L + 1)
                        step(nc.vector.scalar_tensor_tensor(out=scol(80, 16), in0=scol(0, 16), scalar=0.0, in1=scol(48, 16),
                                                            op0=ALU.max, op1=ALU.add))
                        settle()
                        dve.wait_ge(s_neg_a, L + 1)
                        nc.vector.scalar_tensor_tensor(out=two8(scol(96, 16)), in0=two8(scol(80, 16)), scalar=-1.0,
                                                       in1=scol(64, 8).unsqueeze(1).to_broadcast([P, TP, 8]),
                                                       op0=ALU.mult, op1=ALU.mult).then_inc(s_a_ready, 1)
                        dve.wait_ge(s_a_ready, L + 1)
                        nc.vector.tensor_tensor(dec[:].rearrange("p c h t -> p (c h) t"),
                                                scol(96, 16).unsqueeze(2).to_broadcast([P, 16, P]),
                                                tri.unsqueeze(1).to_broadcast([P, 16, P]), ALU.mult).then_inc(s_ta_ready, 1)
                    if s == 5:
                        convolve(1)
                    if s == 6:
                        dve.wait_ge(s_acum_ready, L + 1)
                        nc.vector.tensor_copy(scol(144, 16), bank[3][:, 0:16]).then_inc(s_acum_copied, 1)
                        dve.wait_ge(s_acum_copied, L + 1)
                        dve.wait_ge(s_cumb_ready, 4 * L + 4)
                        segments(0)
                    if s == 7:
                        segments(1)
                    if s == 8:
                        convolve(2)
                        convolve(3)
                    if s == 9:
                        dve.wait_ge(s_gl_pre, L + 1)
                        for k in range(2):
                            step(nc.vector.tensor_scalar(g_raw[:, k * T:(k + 1) * T], bank[2][:, k * T:(k + 1) * T],
                                                         par[:, C_BGK + k:C_BGK + k + 1], None, ALU.add))
                        settle()
                        nc.vector.scalar_tensor_tensor(out=g_neg, in0=g_raw, scalar=-1.0, in1=g_raw,
                                                       op0=ALU.mult, op1=ALU.min).then_inc(s_gl_neg, 1)
                    if s == 11:
                        dve.wait_ge(s_masks_set, 1)
                        dve.wait_ge(s_gl_log, L + 1)
                        step(nc.vector.scalar_tensor_tensor(out=g_raw, in0=g_raw, scalar=0.0, in1=g_neg,
                                                            op0=ALU.min, op1=ALU.subtract))
                        settle()
                        nc.vector.tensor_tensor_scan(g_cum, keep, g_raw, 0.0, ALU.mult, ALU.add).then_inc(s_gl_scan, 1)
                        dve.wait_ge(s_gl_scan, L + 1)
                        dve.wait_ge(s_xs_t, 3 * (L + 1))
                        for c in range(TP):
                            nc.vector.tensor_tensor(heads(xdt[:, c, :]), heads(bank[5 + c][:, :]),
                                                    scol(80 + 8 * c, 8).unsqueeze(2).to_broadcast([P, 8, SSD_P]),
                                                    ALU.mult).then_inc(s_xdt_ready, 1)
                        dve.wait_ge(s_cb_ready, L + 1)
                        step(nc.vector.tensor_tensor(gm[:], bank[4][:, :].rearrange("p (a t) -> p a t", a=4),
                                                     tri.unsqueeze(1).to_broadcast([P, 4, P]), ALU.mult))
                        settle()
                    if s == 12:
                        dve.wait_ge(s_ds_exp, L + 1)
                        dve.wait_ge(s_xdt_ready, 2 * (L + 1))
                        nc.vector.tensor_tensor(heads(dsx[:]), heads(xdt[:, 0, :]),
                                                scol(128, 8).unsqueeze(2).to_broadcast([P, 8, SSD_P]), ALU.mult).then_inc(s_dsx_ready, 1)
                        dve.wait_ge(s_seg_exp, 2 * (L + 1))
                        for c in range(TP):
                            for g in range(2):
                                nc.vector.tensor_tensor(dec[:, c, 4 * g:4 * g + 4, :], dec[:, c, 4 * g:4 * g + 4, :],
                                                        gm[:, 2 * c + g:2 * c + g + 1, :].to_broadcast([P, 4, P]),
                                                        ALU.mult).then_inc(s_m_ready, 1)
                    if s == 13:
                        dve.wait_ge(s_ea_exp, 2 * (L + 1))
                        for g in range(2):
                            nc.vector.tensor_tensor(cea[:, 4 * g:4 * g + 4, :], cea[:, 4 * g:4 * g + 4, :],
                                                    xc[:, 6 + g:7 + g, P:T].to_broadcast([P, 4, P]), ALU.mult).then_inc(s_cea_ready, 1)
                        level_distances(0)
                    if s == 14:
                        g_v = g_cum.rearrange("p (n b) -> p n b", b=GLA_CH)
                        step(nc.vector.tensor_tensor(kq[:, 0, :].rearrange("p (n b) -> p n b", b=GLA_CH),
                                                     g_v[:, :, GLA_CH - 1:GLA_CH].to_broadcast([P, 8, GLA_CH]), g_v, ALU.subtract))
                        step(nc.vector.tensor_copy(kq[:, 1, :], g_cum))
                        settle()
                        dve.sem_inc(s_gl_kqd, 1)
                        nc.vector.memset(attn[:], 0.0).then_inc(s_gl_zero, 1)
                    if s == 15:
                        level_distances(1)
                    if s == 16:
                        dve.wait_ge(s_y_ready, L + 1)
                        for k in range(4):
                            step(nc.vector.scalar_tensor_tensor(out=y_ssd[:, k, :], in0=xc[:, k, :],
                                                                scalar=par[:, C_DSK + k:C_DSK + k + 1],
                                                                in1=bank[6 + k // 2][:, (k % 2) * T:(k % 2) * T + T],
                                                                op0=ALU.mult, op1=ALU.add))
                        settle()
                        dve.sem_inc(s_y_skip, 1)
                    if s == 17:
                        dve.wait_ge(s_gl_kq, L + 1)
                        step(nc.vector.tensor_copy(scol(176, 8).unsqueeze(2),
                                                   kq[:, 1, :].rearrange("p (n b) -> p n b", b=GLA_CH)[:, :, GLA_CH - 1:GLA_CH]))
                        nc.vector.tensor_tensor(kq[:, 0, :], kq[:, 0, :], ks, ALU.mult).then_inc(s_gl_kd, 1)
                        settle()
                        dve.wait_ge(s_gl_qs, L + 1)
                        nc.vector.tensor_tensor(kq[:, 1, :], kq[:, 1, :], qs, ALU.mult).then_inc(s_gl_qe, 1)
                        level_queries(0)
                    if s == 18:
                        level_keys(0)
                    if s == 19:
                        place_level(0)
                        level_queries(1)
                    if s == 20:
                        place_level(1)
                        level_keys(1)
                    if 21 <= s <= 25:
                        place_level(s - 19)
                    if s == 23:
                        gla_state(0)
                        gla_state(1)
                    if s == 25:
                        gla_state(2)
                    if s == 26:
                        dve.wait_ge(s_mla_rstd, L + 1)
                        for first, n, which in ((T_CQ, 4, 0), (T_CKV, 2, 1)):
                            nc.vector.tensor_tensor(proj[:, first:first + n, :], proj[:, first:first + n, :],
                                                    lat_rstd[:, which:which + 1, :].to_broadcast([P, n, T]),
                                                    ALU.mult).then_inc(s_mla_normed, 1)
                        dve.wait_ge(s_mla_normed, 2 * (L + 1))
                    if s == 28:
                        for k in range(6):
                            dve.wait_ge(s_mla_hi, 6 * L + k + 1)
                            nc.vector.scalar_tensor_tensor(out=cata_lo[:, k, :], in0=proj[:, T_CQ + k, :],
                                                           scalar=par[:, C_QG + k:C_QG + k + 1],
                                                           in1=cata_hi[:, k, :].bitcast(F32), op0=ALU.mult,
                                                           op1=ALU.subtract).then_inc(s_mla_split, 1)
                    if s == 29:
                        dve.wait_ge(s_silu_ready, 3 * L + 2)
                        nc.vector.tensor_tensor(y_ssd, y_ssd, z, ALU.mult).then_inc(s_y_gated, 1)
                    if s == 30:
                        dve.wait_ge(s_mla_split, 6 * (L + 1))
                        dve.wait_ge(s_rope_swapped, 3 * L + 1)
                        step(nc.vector.tensor_tensor(ropet[0:64, 0, :], bank[3][0:64, 0:T], sin[0:64, :], ALU.mult))
                        step(nc.vector.tensor_tensor(kp[0:64, :], proj[0:64, T_MIX, :], cos[0:64, :], ALU.mult))
                        settle()
                        nc.vector.tensor_tensor(kp[0:64, :], kp[0:64, :], ropet[0:64, 0, :], ALU.add).then_inc(s_k_rope, 1)
                        dve.wait_ge(s_k_rope, L + 1)
                        dve.wait_ge(s_gl_orstd, L + 1)
                        for q in range(2):
                            step(nc.vector.scalar_tensor_tensor(out=o_y[:, q, :], in0=bank[4 + q][:, :],
                                                                scalar=par[:, C_GLAG:C_GLAG + 1], in1=o_rstd[:, q, :],
                                                                op0=ALU.mult, op1=ALU.mult))
                        settle()
                    if s == 31:
                        dve.wait_ge(s_silu_ready, 3 * (L + 1))
                        for q in range(2):
                            pair = o_y[:, q, :].rearrange("p (h t) -> p h t", h=2)
                            step(nc.vector.tensor_tensor(
                                pair, pair, proj[:, T_GR:T_GR + 4, :].rearrange("p (h q) t -> p q h t", q=2)[:, q], ALU.mult))
                        settle()
                        dve.sem_inc(s_gl_y, 1)
                    if s == 32:
                        dve.wait_ge(s_y_rstd, L + 1)
                        nc.vector.tensor_tensor(y_ssd, y_ssd, sum_rstd.unsqueeze(1).to_broadcast([P, 4, T]),
                                                ALU.mult).then_inc(s_y_normed, 1)
                        dve.wait_ge(s_gl_hi, L + 1)
                        nc.vector.tensor_tensor(catb_lo[:, 4:8, :].rearrange("p (h q) t -> p q h t", q=2),
                                                o_y.rearrange("p q (h t) -> p q h t", h=2),
                                                catb_hi[:, 4:8, :].rearrange("p (h q) t -> p q h t", q=2).bitcast(F32),
                                                ALU.subtract).then_inc(s_gl_cat, 1)
                    if s == 33:
                        dve.wait_ge(s_rope_swapped, 3 * L + 3)
                        for b in range(2):
                            step(nc.vector.tensor_tensor(ropet[:, 2 * b:2 * b + 2, :], bank[6 + b][:, :].rearrange("p (a t) -> p a t", a=2),
                                                         sin.unsqueeze(1).to_broadcast([P, 2, T]), ALU.mult))
                        step(nc.vector.tensor_tensor(qp[:], qp[:], cos.unsqueeze(1).to_broadcast([P, 4, T]), ALU.mult))
                        settle()
                        nc.vector.tensor_tensor(qp[:], qp[:], ropet, ALU.add).then_inc(s_q_rope, 1)
                    if s == 34:
                        dve.wait_ge(s_y_normed, L + 1)
                        for k in range(4):
                            dve.wait_ge(s_y_hi, 4 * L + k + 1)
                            nc.vector.scalar_tensor_tensor(out=catb_lo[:, k, :], in0=y_ssd[:, k, :],
                                                           scalar=par[:, C_SSDG + k:C_SSDG + k + 1],
                                                           in1=catb_hi[:, k, :].bitcast(F32), op0=ALU.mult,
                                                           op1=ALU.subtract).then_inc(s_ssd_cat, 1)
                for k in range(2 * KT):
                    if k == 0:
                        nc.vector.memset(ssq[:], 0.0).then_inc(s_ssq_zeroed, 1)
                        dve.wait_ge(s_ssd_cat, 4 * (L + 1))
                    if k in HEAD_AT:
                        head_scores(HEAD_AT[k])
                    if k - NORMALISE_AFTER in HEAD_AT:
                        head_normalise(HEAD_AT[k - NORMALISE_AFTER])
                    if k - VALUES_AFTER in HEAD_AT:
                        head_out(HEAD_AT[k - VALUES_AFTER])
                    after_piece(N_OUT + k // 2, k % 2)
                    b, m = out_bank(k), k % KT
                    nc.vector.tensor_tensor(x[:, m, :], x[:, m, :], bank[b][:, 0:T], ALU.add).then_inc(bank_free[b], 1)
                    if k >= KT - 4:
                        dve.wait_ge(bank_free[b], L * TURNS[b] + (TURN["out", k] + 2))
                    if k == KT:
                        dve.wait_ge(s_ssq_zeroed, 2 * L + 1)
                    if k >= KT:
                        dve.sem_inc(s_x_ready, 1)
                    ahead(N_OUT + k // 2, k % 2)
                    if k >= KT:
                        refresh(m, L * 2 * KT + m, par[:, C_FFN + m:C_FFN + m + 1])
                assert vec.n == VEC_STEPS, vec.n

                for half in range(2):
                    def gate_lo(i, j, piece, widths=WIDE):
                        lo(c0 + (Q_GATE[half] * 4 + j + 2) + i * 4, j + 2, piece, widths)

                    def gate_take(i, j):
                        b, f = j % 4, j // 2 % 2
                        dve.wait_ge(s_pieces_used, (c0 + (Q_GATE[half] * 4 + j + 1 + SPLIT) + i * 4) * PIECES)
                        to = gs if j % 2 == 0 else us
                        nc.vector.tensor_tensor(to[:, f, :], bank[b][:, 0:T], rstd[:], ALU.mult).then_inc(bank_free[b], 1)

                    def gate_taken(i, j):
                        dve.wait_ge(bank_free[j % 4], L * TURNS[j % 4] + (TURN["gate", half, j % 4] + j // 4 + 2) + i)

                    def convolve_gate(i, f):
                        gate_taken(i, 2 * f)
                        ft, nth, f = i * 2 + (half * HALF + f), L * FT + (half * HALF + f) + i * 2, f % 2
                        for k in range(FTAPS):
                            tap = par[:, bass.ds(ft * FTAPS + (C_FW + FTAPS - 1 - k), 1)]
                            if k == 0:
                                nc.vector.tensor_scalar(cv[:, f, :], gs[:, f, :], tap, par[:, bass.ds(ft + C_FB, 1)],
                                                        ALU.mult, ALU.add).then_inc(s_gate_step, 1)
                            else:
                                dve.wait_ge(s_gate_step, nth * 2 + k)
                                nc.vector.scalar_tensor_tensor(
                                    out=cv[:, f, k:T], in0=gs[:, f, 0:T - k], scalar=tap, in1=cv[:, f, k:T],
                                    op0=ALU.mult, op1=ALU.add).then_inc(s_gate_step if k < 2 else s_gate_ready, 1)

                    def hidden(i, f):
                        gate_taken(i, 2 * f + 1)
                        dve.wait_ge(s_gate_silu, L * FT + (half * HALF + f + 1) + i * 2)
                        nc.vector.tensor_tensor(hv[:, f % 2, :], us[:, f % 2, :], sl[:, f % 2, :], ALU.mult).then_inc(s_hid_ready, 1)

                    def hidden_lo(i, f):
                        dve.wait_ge(s_hid_hi_ready, L * FT + (half * HALF + f + 1) + i * 2)
                        at = bass.ds(i * 2 + f, 1)
                        nc.vector.tensor_tensor(hid_lo[:, at, :], hv[:, f % 2:f % 2 + 1, :], hid_hi[:, at, :].bitcast(F32),
                                                ALU.subtract).then_inc(s_hid_split, 1)

                    def gate_turn(i, f, widths):
                        gate_lo(i, 2 * f + 2, 0, widths)
                        gate_take(i, 2 * f + 2)
                        hidden(i, f)
                        gate_lo(i, 2 * f + 2, 1, widths)
                        convolve_gate(i, f + 1)
                        hidden_lo(i, f)
                        gate_lo(i, 2 * f + 3, 0, widths)
                        gate_take(i, 2 * f + 3)
                        gate_lo(i, 2 * f + 3, 1, widths)

                    gate_lo(0, 0, 0)
                    if half == 0:
                        dve.wait_ge(s_rstd_ready, 2 * L + 2)
                    gate_take(0, 0)
                    gate_lo(0, 0, 1)
                    convolve_gate(0, 0)
                    gate_lo(0, 1, 0)
                    gate_take(0, 1)
                    gate_lo(0, 1, 1)
                    if half == 0:
                        nc.vector.memset(ssq[:], 0.0).then_inc(s_ssq_zeroed, 1)
                    dve.sem_inc(s_passed_dve, 1)
                    with dve.Fori(0, 10) as i:
                        for f in range(2):
                            gate_turn(i, f, WIDE)
                    gate_turn(10, 0, NARROW)
                    hidden(10, 1)
                    hidden_lo(10, 1)
                    if half == 1:
                        dve.wait_ge(s_gate_ready, (L + 1) * FT)
                        dve.sem_inc(s_params_free, 1)
                        dve.wait_ge(s_ssq_zeroed, 2 * L + 2)

                    def down_chunk(i, jj, widths, last=False):
                        chunk = c0 + Q_DOWN[half] * 4 + i * 8 + jj
                        if not last:
                            lo(chunk + 2, jj + 2, 0, widths)
                        if jj % 2 == 1:
                            b, m = jj // 2, i * 4 + jj // 2
                            dve.wait_ge(s_pieces_used, chunk * PIECES + (PIECES + SPLIT * PIECES))
                            xt = x[:, bass.ds(m, 1), :].rearrange("p a t -> p (a t)")
                            nc.vector.tensor_tensor(xt, xt, bank[b][:, 0:T], ALU.add).then_inc(bank_free[b], 1)
                        if jj % 2 == 1 and half == 1:
                            dve.wait_ge(bank_free[b], L * TURNS[b] + i + (TURN["down", half, b] + 2))
                            dve.sem_inc(s_x_ready, 1)
                        if last:
                            lo(chunk + 2, jj + 2, 0, widths)
                        if jj % 2 == 1 and half == 1:
                            refresh(m, L * 2 * KT + KT + m, gains[:, bass.ds((L + 1) * KT + m, 1)])
                        lo(chunk + 2, jj + 2, 1, widths)

                    dve.sem_inc(s_passed_dve, 1)
                    with dve.Fori(0, 3) as i:
                        for jj in range(8):
                            down_chunk(i, jj, NARROW)
                    for jj in range(8):
                        down_chunk(3, jj, NARROW if jj < 6 else WIDE, jj == 7)
                    if half == 0:
                        for b in range(4):
                            dve.wait_ge(bank_free[b], L * TURNS[b] + (TURN["down", 0, b] + 5))

            dve.wait_ge(s_rstd_ready, 2 * DEPTH + 1)
            for m in range(KT):
                nc.vector.scalar_tensor_tensor(out=x[:, m, :], in0=x[:, m, :], scalar=gains[:, DEPTH * KT + m:DEPTH * KT + m + 1],
                                               in1=rstd[:], op0=ALU.mult, op1=ALU.mult).then_inc(s_final_ready, 1)

        @block.tensor
        def _(pe):
            pe.sem_inc(s_pieces_used, SPLIT * PIECES)
            def three(out, w, rhs_hi, rhs_lo, first, last):
                w_high, w_low = w
                nc.tensor.matmul(out, w_high, rhs_hi, start=first, stop=False)
                nc.tensor.matmul(out, w_high, rhs_lo, start=False, stop=False)
                return nc.tensor.matmul(out, w_low, rhs_hi, start=False, stop=last)

            def piece_ready(chunk, piece):
                pe.wait_ge(s_lo_ready, chunk * PIECES + (piece + 1 + RAW * PIECES))

            def unit(j, piece, u, n=P):
                at = slice(OFFSET * piece + u * n, OFFSET * piece + (u + 1) * n)
                return w_hi[:, j % SPLIT, at], w_lo[:, j % SPLIT, at]

            def norm_sums(nth):
                pe.wait_ge(s_ssq_added, nth + 1)
                nc.tensor.matmul(bank[4][:, 0:T], ones, ssq[:], start=True, stop=True).then_inc(s_sums_ready, 1)

            def wide_tile(chunk, j, b, uses, normed=None):
                for piece in range(PIECES):
                    piece_ready(chunk, piece)
                    if normed is not None:
                        pe.wait_ge(s_h_ready, normed + 8 * (piece + 1))
                    if piece == 0:
                        pe.wait_ge(bank_free[b], uses)
                    for u in range(8):
                        k = 8 * piece + u
                        last = three(bank[b][:, 0:T], unit(j, piece, u), h_hi[:, k, :], h_lo[:, k, :], k == 0, k == KT - 1)
                    last.then_inc(s_pieces_used, 1)

            with pe.Fori(0, DEPTH) as L:
                c0 = L * CHUNKS
                mix = proj[:, T_MIX, :]

                def mla_chunk(c):
                    j = (N_MLA + c) % 4
                    for piece in range(PIECES):
                        piece_ready(c0 + N_MLA + c, piece)
                        for n, b in enumerate(mla_banks(c, piece)):
                            pe.wait_ge(bank_free[b], L * TURNS[b] + (TURN["mla", c, piece, b] + 1))
                            if c < 3:
                                for a in range(2):
                                    for k in range(4):
                                        last = three(bank[b][:, a * T:(a + 1) * T], unit(j, piece, 4 * a + k),
                                                     cata_hi[:, k, :], cata_lo[:, k, :], k == 0, k == 3)
                            elif c == 3:
                                for a in range(2):
                                    for k in range(2):
                                        last = three(bank[b][:, a * T:(a + 1) * T], unit(j, piece, 2 * (2 * n + a) + k),
                                                     cata_hi[:, 4 + k, :], cata_lo[:, 4 + k, :], k == 0, k == 1)
                            else:
                                at = slice(n * P, n * P + P)
                                for k in range(2):
                                    w_high, w_low = unit(j, piece, k, 512)
                                    nc.tensor.matmul(bank[b][:, :], cata_hi[:, 4 + k, at], w_high, start=k == 0, stop=False)
                                    nc.tensor.matmul(bank[b][:, :], cata_lo[:, 4 + k, at], w_high, start=False, stop=False)
                                    last = nc.tensor.matmul(bank[b][:, :], cata_hi[:, 4 + k, at], w_low, start=False, stop=k == 1)
                        last.then_inc(s_pieces_used, 1)

                def gla_level(e):
                    for q in range(2):
                        if e >= 2:
                            pe.wait_ge(s_gl_put, 14 * L + 2 * (e - 2) + q + 1)
                        rows = slice(64 * q, 64 * q + 64)
                        k_, q_ = (ks, qs) if e == 0 else (e_levels[(e - 1) // 3][:, (e - 1) % 3, :], q_levels[(e - 1) // 3][:, (e - 1) % 3, :])
                        for n in range(4):
                            at = slice(n * P, (n + 1) * P)
                            out = bank[4 + 2 * (e % 2) + q]
                            if e == 0:
                                last = nc.tensor.matmul(out[:, at], k_[rows, at], q_[rows, at], start=True, stop=True)
                            else:
                                last = nc.tensor.matmul(out[:, n * P // 2:(n + 1) * P // 2], k_[rows, at],
                                                        late(q_[rows, at], e), start=True, stop=True)
                        last.then_inc(s_gl_lvl, 1)

                def gla_update(c):
                    rows = slice((c % 2) * 64, (c % 2) * 64 + 64)
                    for hp in range(2):
                        last = nc.tensor.matmul(bank[2 + c % 2][:, hp * 256:(hp + 1) * 256], kd_t[rows, c // 2, hp, :],
                                                v_gla[rows, c // 2, hp * 256:(hp + 1) * 256], start=True, stop=True)
                    last.then_inc(s_gl_u, 1)

                def head_scores(h):
                    b = bank[4 + h % 2]
                    if h >= 2:
                        pe.wait_ge(s_masked, 8 * L + h - 1)
                    rows = slice(64 * (h % 2), 64 * (h % 2) + 64)
                    nc.tensor.matmul(b[:, 0:P], qn[:, h, 0:P], kn[:, h, 0:P], start=True, stop=False)
                    nc.tensor.matmul(b[:, 0:P], qp[rows, h // 2, 0:P], kp[rows, 0:P], start=False, stop=True)
                    nc.tensor.matmul(b[:, P:3 * P], qn[:, h, P:T], kn[:, h, :], start=True, stop=False)
                    nc.tensor.matmul(b[:, P:3 * P], qp[rows, h // 2, P:T], kp[rows, :], start=False, stop=True).then_inc(s_scores_ready, 1)

                def head_transpose(h):
                    pe.wait_ge(s_prob_norm, 8 * L + h + 1)
                    if h >= 1:
                        pe.wait_ge(s_probt_copied, 8 * L + h)
                    for k in range(3):
                        last = nc.tensor.transpose(bank[6][:, k * P:(k + 1) * P], prob[:, h % 4, k * P:(k + 1) * P], ident)
                    last.then_inc(s_probt_ready, 1)

                def head_values(h):
                    pe.wait_ge(s_probt_copied, 8 * L + h + 1)
                    if h >= 1:
                        pe.wait_ge(s_o_lo, 8 * L + h)
                    pt, v = probt[:, h % 2, :], vv[:, :, h * P:(h + 1) * P]
                    nc.tensor.matmul(bank[7][:, 0:P], v[:, 0, :], pt[:, 0:P], start=True, stop=True)
                    nc.tensor.matmul(bank[7][:, P:T], v[:, 0, :], pt[:, P:2 * P], start=True, stop=False)
                    nc.tensor.matmul(bank[7][:, P:T], v[:, 1, :], pt[:, 2 * P:3 * P], start=False, stop=True).then_inc(s_o_ready, 1)

                for s in range(N_OUT):
                    if s == 1:
                        pe.wait_ge(s_consts_loaded, 16)
                        norm_sums(L * 2 * KT)
                    if s == 2:
                        pe.wait_ge(s_in_taken, IN_TILES * L + 1)
                        pe.wait_ge(s_rstd_ready, 2 * L + 1)
                        pe.sem_inc(s_passed_pe, 1)
                        for c in range(TP):
                            last = nc.tensor.transpose(bank[4][:, 8 * c:8 * c + 8], mix[MIX_DT:MIX_DT + 8, c * P:(c + 1) * P],
                                                       ident[MIX_DT:MIX_DT + 8, MIX_DT:MIX_DT + 8])
                        last.then_inc(s_dt_t, 1)
                    if s == 6:
                        pe.wait_ge(s_a_ready, L + 1)
                        nc.tensor.matmul(bank[3][:, 0:16], tri, scol(96, 16), start=True, stop=True).then_inc(s_acum_ready, 1)
                        pe.wait_ge(s_ta_ready, L + 1)
                        ta = dec[:].rearrange("p c h t -> p (c h t)")
                        for n, b in enumerate((5, 6, 7, 4)):
                            nc.tensor.matmul(bank[b][:, :], ones, ta[:, n * 512:(n + 1) * 512], start=True, stop=True).then_inc(s_cumb_ready, 1)
                    if s == 8:
                        for k in range(2):
                            last = nc.tensor.matmul(bank[2][:, k * T:(k + 1) * T], par[MIX_GLOW:MIX_GLOW + 16, C_WGK + k * P:C_WGK + (k + 1) * P],
                                                    mix[MIX_GLOW:MIX_GLOW + 16, :], start=True, stop=True)
                        last.then_inc(s_gl_pre, 1)
                    if s == 11:
                        pe.wait_ge(s_silu_ready, 3 * L + 1)
                        pe.wait_ge(s_ea_exp, 2 * (L + 1))
                        for c in range(TP):
                            for k in range(4):
                                last = nc.tensor.transpose(bank[5 + c][:, k * P:(k + 1) * P], xc[:, k, c * P:(c + 1) * P], ident)
                            last.then_inc(s_xs_t, 1)
                        for g in range(2):
                            last = nc.tensor.transpose(bank[7][:, g * P:(g + 1) * P], xc[:, 4 + g, 0:P], ident)
                        last.then_inc(s_xs_t, 1)
                        for c in range(TP):
                            for g in range(2):
                                last = nc.tensor.matmul(bank[4][:, (2 * c + g) * P:(2 * c + g + 1) * P], xc[:, 4 + g, c * P:(c + 1) * P],
                                                        xc[:, 6 + g, c * P:(c + 1) * P], start=True, stop=True)
                        last.then_inc(s_cb_ready, 1)
                    if s == 14:
                        pe.wait_ge(s_dsx_ready, L + 1)
                        pe.wait_ge(s_btok_ready, L + 1)
                        for g in range(2):
                            last = nc.tensor.matmul(bank[5][:, g * 256:(g + 1) * 256], btok[:, g * P:(g + 1) * P],
                                                    dsx[:, g * 256:(g + 1) * 256], start=True, stop=True)
                        last.then_inc(s_state_ready, 1)
                        pe.wait_ge(s_in_taken, IN_TILES * L + 13)
                        for c in range(TP):
                            for k in range(4):
                                last = nc.tensor.transpose(bank[2 + c][:, k * P:(k + 1) * P], proj[:, T_GV + k, c * P:(c + 1) * P], ident)
                        last.then_inc(s_gl_v, 1)
                    if s == 16:
                        pe.wait_ge(s_state_copied, L + 1)
                        pe.wait_ge(s_m_ready, 4 * (L + 1))
                        pe.wait_ge(s_cea_ready, 2 * (L + 1))
                        for h in range(SSD_H):
                            rows = slice(64 * (h % 2), 64 * (h % 2) + 64)
                            for c in range(TP):
                                col = ((h // 2) % 2) * T + c * P
                                out = bank[6 + h // 4][rows, col:col + P]
                                last = nc.tensor.matmul(out, xdt[:, c, h * 64:(h + 1) * 64], dec[:, c, h, :], start=True, stop=c == 0)
                                if c == 1:
                                    last = nc.tensor.matmul(out, sst[:, h * 64:(h + 1) * 64], cea[:, h, :], start=False, stop=True)
                        last.then_inc(s_y_ready, 1)
                    if s == 19:
                        pe.wait_ge(s_gl_kd, L + 1)
                        pe.wait_ge(s_gl_vcopied, 2 * (L + 1))
                        for n in range(4):
                            last = nc.tensor.transpose(bank[2][:, n * P:(n + 1) * P],
                                                       kq[:, 0, (n % 2) * T + (n // 2) * P:(n % 2) * T + (n // 2 + 1) * P], ident)
                        last.then_inc(s_gl_kt, 1)
                        pe.wait_ge(s_y_skip, L + 1)
                        gla_level(0)
                    if s == 20:
                        pe.wait_ge(s_gl_k, 2 * L + 1)
                        gla_level(1)
                    if s == 21:
                        gla_level(2)
                    if s == 22:
                        gla_level(3)
                        pe.wait_ge(s_gl_ktc, L + 1)
                        gla_update(0)
                        gla_update(1)
                    if 23 <= s <= 25:
                        if s == 23:
                            pe.wait_ge(s_gl_k, 2 * L + 2)
                        gla_level(s - 19)
                    if s == 25:
                        pe.wait_ge(s_mla_sq, L + 1)
                        pe.wait_ge(s_gl_s, 3 * L + 2)
                        gla_update(2)
                        for k in range(4):
                            nc.tensor.matmul(bank[3][:, 0:T], ones, lat_sq[:, k, :], start=k == 0, stop=k == 3)
                        for k in range(2):
                            last = nc.tensor.matmul(bank[3][:, T:2 * T], ones, lat_sq[:, 4 + k, :], start=k == 0, stop=k == 1)
                        last.then_inc(s_mla_sums, 1)
                    if s == 27:
                        pe.wait_ge(s_gl_put, 14 * (L + 1))
                        pe.wait_ge(s_gl_qe, L + 1)
                        pe.wait_ge(s_gl_s, 3 * (L + 1))
                        for q in range(2):
                            rows = slice(64 * q, 64 * q + 64)
                            for hp in range(2):
                                head = 2 * hp + q
                                for c in range(TP):
                                    nc.tensor.matmul(bank[4 + q][:, hp * T + c * P:hp * T + (c + 1) * P],
                                                     v_gla[:, c, head * P:(head + 1) * P],
                                                     attn[:, q, (2 * hp + c) * P:(2 * hp + c + 1) * P], start=True, stop=False)
                                    for n in (2 * c, 2 * c + 1):
                                        if n == 0:
                                            continue
                                        at = slice(hp * T + n * 64, hp * T + (n + 1) * 64)
                                        last = nc.tensor.matmul(bank[4 + q][:, at], st_gla[rows, n - 1, hp, :], kq[rows, 1, at],
                                                                start=False, stop=n == 2 * c + 1)
                        last.then_inc(s_gl_o, 1)
                    if s == 29:
                        pe.wait_ge(s_gl_osq, 2 * (L + 1))
                        for q in range(2):
                            last = nc.tensor.matmul(bank[6 + q][:, :], ones, o_sq[:, q, :], start=True, stop=True)
                        last.then_inc(s_gl_osum, 1)
                        pe.wait_ge(s_mla_rstd, L + 1)
                        nc.tensor.matmul(bank[3][:, 0:T], swap[0:64, :], mix[0:64, :], start=True, stop=True).then_inc(s_rope_swapped, 1)
                    if s == 31:
                        pe.wait_ge(s_y_sq, L + 1)
                        pe.wait_ge(s_gl_olog, 2 * (L + 1))
                        for k in range(4):
                            last = nc.tensor.matmul(bank[6][:, 0:T], ones, z[:, k, :], start=k == 0, stop=k == 3)
                        last.then_inc(s_y_sums, 1)
                    if s == 32:
                        pe.wait_ge(s_gl_s, 3 * L + 3)
                        pe.wait_ge(s_k_rope, L + 1)
                    if s == 33:
                        for b in range(2):
                            pe.wait_ge(bank_free[b], L * TURNS[b] + (TURN["mla", 0, b, b] + 2))
                        pe.wait_ge(s_y_rstd, L + 1)
                        for b in range(2):
                            for k in range(2):
                                last = nc.tensor.matmul(bank[6 + b][:, k * T:(k + 1) * T], swap, qp[:, 2 * b + k, :], start=True, stop=True)
                            last.then_inc(s_rope_swapped, 1)
                    if s < N_MLA:
                        wide_tile(c0 + s, s, s % 2, L * TURNS[s % 2] + (TURN["in", s] + 1), L * 2 * KT if s == 0 else None)
                    else:
                        if s == N_MLA:
                            pe.wait_ge(s_mla_split, 6 * (L + 1))
                        mla_chunk(s - N_MLA)

                pe.wait_ge(s_q_rope, L + 1)
                pe.wait_ge(s_k_dup, L + 1)
                pe.wait_ge(s_gl_y, L + 1)
                for k in range(2 * KT):
                    if k in HEAD_AT:
                        head_scores(HEAD_AT[k])
                    if k - TRANSPOSE_AFTER in HEAD_AT:
                        head_transpose(HEAD_AT[k - TRANSPOSE_AFTER])
                    if k == 3:
                        for b in range(4):
                            pe.wait_ge(bank_free[b], L * TURNS[b] + (TURN["out", (b + 2) % 4] + 1))
                    if k - VALUES_AFTER in HEAD_AT:
                        head_values(HEAD_AT[k - VALUES_AFTER])
                    if k == 0:
                        pe.wait_ge(s_gl_cat, L + 1)
                        pe.wait_ge(s_ssd_cat, 4 * (L + 1))
                    if k == KT:
                        pe.wait_ge(s_o_lo, 8 * (L + 1))
                    chunk, piece = N_OUT + k // 2, k % 2
                    rhs_hi, rhs_lo = (catb_hi, catb_lo) if k < KT else (cata_hi, cata_lo)
                    piece_ready(c0 + chunk, piece)
                    b = out_bank(k)
                    pe.wait_ge(bank_free[b], L * TURNS[b] + (TURN["out", k] + 1))
                    for u in range(8):
                        last = three(bank[b][:, 0:T], unit(chunk, piece, u), rhs_hi[:, u, :], rhs_lo[:, u, :], u == 0, u == 7)
                    last.then_inc(s_pieces_used, 1)
                for half in range(2):
                    def gate_tile(i, j, normed=None):
                        wide_tile(c0 + (Q_GATE[half] * 4 + j) + i * 4, j, j % 4,
                                  L * TURNS[j % 4] + (TURN["gate", half, j % 4] + j // 4 + 1) + i, normed)

                    gate_tile(0, 0, L * 2 * KT + KT if half == 0 else None)
                    if half == 0:
                        norm_sums(L * 2 * KT + KT)
                    gate_tile(0, 1)
                    pe.sem_inc(s_passed_pe, 1)
                    with pe.Fori(0, 10) as i:
                        for j in range(2, 6):
                            gate_tile(i, j)
                    gate_tile(10, 2)
                    gate_tile(10, 3)

                    def down_turn(i, first=False):
                        for jj in range(8):
                            b, part, j = jj // 2, jj % 2, jj % 4
                            for piece in range(PIECES):
                                done = part * DOWN_KT + DOWN_KTS[0] * piece
                                if first and jj < 2:
                                    pe.wait_ge(s_hid_split, L * FT + (half * HALF + done + DOWN_KTS[piece]))
                                piece_ready(c0 + Q_DOWN[half] * 4 + i * 8 + jj, piece)
                                if part == 0 and piece == 0:
                                    pe.wait_ge(bank_free[b], L * TURNS[b] + i + (TURN["down", half, b] + 1))
                                for u in range(DOWN_KTS[piece]):
                                    last = three(bank[b][:, 0:T], unit(j, piece, u), hid_hi[:, done + u, :], hid_lo[:, done + u, :],
                                                 done + u == 0, done + u == HALF - 1)
                                last.then_inc(s_pieces_used, 1)

                    down_turn(0, True)
                    pe.sem_inc(s_passed_pe, 1)
                    with pe.Fori(1, 4) as i:
                        down_turn(i)
            norm_sums(DEPTH * 2 * KT)


VEC_STEPS = 104


def _tiles(w, kt):
    k, m = w.shape
    return w.reshape(kt, P, m // P, P).transpose(2, 1, 0, 3).reshape(m // P, P, kt * P)


def _cols(v):
    return v.reshape(-1, P).T


def kernel(**inputs):
    import concourse.bacc as _bacc
    from concourse.bass_utils import run_bass_kernel_spmd as _run

    a = {k: np.asarray(v) for k, v in inputs.items()}
    f = np.float32
    order = []
    at = lambda start, n: order.extend(range(start, start + n))
    at(1344, 1024); at(2888, 512); at(2376, 256); at(2632, 256); at(0, 512); at(512, 256); at(832, 512); at(3416, 512)
    front, outw, gate, down, params = [], [], [], [], []
    for l in range(DEPTH):
        w = a["w_in"][l]
        mix = np.zeros((D, P), f)
        mix[:, 0:64] = w[:, 768:832]
        mix[:, MIX_GLOW:MIX_GLOW + 16] = w[:, 3400:3416]
        mix[:, MIX_DT:MIX_DT + 8] = w[:, 2368:2376]
        front.append(_tiles(np.concatenate([mix, w[:, order]], 1), KT))
        uq = a["mla_w_uq"][l].reshape(512, 8, 192)
        uq = np.concatenate([uq[:, :, 128:].reshape(512, 512), uq[:, :, :128].reshape(512, 1024)], 1)
        front.append(_tiles(uq, 4).reshape(3, 4, P, 512).transpose(0, 2, 1, 3).reshape(3, P, CHUNK))
        ukv = a["mla_w_ukv"][l].reshape(256, 8, 256)
        front.append(_tiles(np.ascontiguousarray(ukv[:, :, :128]).reshape(256, 1024), 2).transpose(1, 0, 2).reshape(1, P, CHUNK))
        front.append(np.ascontiguousarray(ukv[:, :, 128:]).reshape(2, P, 2, 512).transpose(1, 2, 0, 3).reshape(1, P, CHUNK))
        for rows in (slice(1024, 2048), slice(0, 1024)):
            w = _tiles(a["w_out"][l][rows], 8)
            outw.append(w.reshape(8, 2, P, 1024).transpose(0, 2, 1, 3).reshape(8, P, CHUNK))
        g, u = _tiles(a["ffn_w_gate"][l], KT), _tiles(a["ffn_w_up"][l], KT)
        gate.append(np.stack([g, u], 1).reshape(2 * FT, P, CHUNK))
        dn = a["ffn_w_down"][l].reshape(2, 2, DOWN_KT, P, KT, P)
        down.append(dn.transpose(0, 4, 1, 3, 2, 5).reshape(64, P, DOWN_CHUNK))
        p = np.zeros((P, NPAR), f)
        p[:, C_FFN:C_FFN + 16] = _cols(a["ffn_norm"][l])
        p[:, C_QG:C_QG + 4] = _cols(a["mla_q_norm"][l])
        p[:, C_KVG:C_KVG + 2] = _cols(a["mla_kv_norm"][l])
        p[:, C_SSDG:C_SSDG + 4] = _cols(a["ssd_norm"][l])
        p[:, C_DSK:C_DSK + 4] = _cols(np.repeat(a["ssd_d"][l], SSD_P))
        p[:, C_GLAG] = a["gla_norm"][l]
        p[:, C_BGK:C_BGK + 2] = _cols(a["gla_b_gk"][l])
        p[:, C_DTB:C_DTB + 8] = a["ssd_dt_bias"][l][None]
        p[:, C_ALOG:C_ALOG + 8] = a["ssd_a_log"][l][None]
        p[:, C_CONV:C_CONV + 32] = a["ssd_conv_w"][l].reshape(4, 8, P).transpose(2, 1, 0).reshape(P, 32)
        p[:, C_CONVB:C_CONVB + 8] = _cols(a["ssd_conv_b"][l])
        p[:, C_FW:C_FW + 132] = a["ffn_dw_w"][l].reshape(3, FT, P).transpose(2, 1, 0).reshape(P, 132)
        p[:, C_FB:C_FB + 44] = _cols(a["ffn_dw_b"][l])
        p[MIX_GLOW:MIX_GLOW + 16, C_WGK:C_WGK + 256] = a["gla_w_gk"][l]
        params.append(p)

    consts = np.zeros((P, NCONST), f)
    i = np.arange(P)
    consts[:, K_ID:K_ID + P] = np.eye(P)
    consts[:, K_ONES:K_ONES + P] = 1
    consts[i, K_SWAP + (i ^ 32)] = 1
    consts[:, K_TRI:K_TRI + P] = i[:, None] <= i[None]
    freq = f(10000.0) ** (-np.arange(0, ROPE, 2, dtype=f) / f(ROPE))
    ang = np.arange(T, dtype=f)[:, None] * freq[None]
    consts[:, K_COS:K_COS + T] = np.cos(ang).T[i % 32]
    consts[:, K_SIN:K_SIN + T] = np.sin(ang).T[i % 32] * np.where(i % 64 < 32, -1, 1)[:, None]
    hide = np.where(i[None] <= i[:, None], 0, -1e30)
    consts[:, K_MASK:K_MASK + P] = hide
    consts[:, K_MASK + 2 * P:K_MASK + 3 * P] = hide
    masks = np.zeros((P, LEVELS * P + 2 * T), f)
    for e in range(LEVELS):
        b = GLA_CH >> (e + 1)
        masks[:, e * P:(e + 1) * P] = ((i[:, None] // (2 * b) == i[None] // (2 * b))
                                       & (i[:, None] % (2 * b) < b) & (i[None] % (2 * b) >= b))
    masks[:, LEVELS * P:] = np.arange(2 * T) % GLA_CH != 0

    gains = np.concatenate([_cols(a["attn_norm"][l]) for l in range(DEPTH)] + [_cols(a["final_norm"])], 1)
    arrays = {
        "x_in": a["x"][0].T.reshape(KT, P, T).transpose(1, 0, 2),
        "gains_in": gains,
        "params_in": np.stack(params),
        "consts_in": consts,
        "masks_in": masks,
        "front_in": np.concatenate(front + [np.zeros((2, P, CHUNK), f)]),
        "out_in": np.concatenate(outw),
        "gate_in": np.concatenate(gate),
        "down_in": np.concatenate(down),
    }
    arrays = {k: np.ascontiguousarray(v) for k, v in arrays.items()}
    nc = _bacc.Bacc("TRN2", target_bir_lowering=False, num_devices=1)
    args = [nc.dram_tensor(k, v.shape, mybir.dt.from_np(v.dtype), kind="ExternalInput").ap() for k, v in arrays.items()]
    args.append(nc.dram_tensor("y_out", (P, KT, T), F32, kind="ExternalOutput").ap())
    build(nc, *args)
    r = _run(nc, [arrays], core_ids=[0])
    y = r.results[0]["y_out"]
    return y.transpose(1, 0, 2).reshape(D, T).T.reshape(1, T, D)
```
